# Optimizing a Trainium2 kernel written in Bass

```python
import math
import jax, jax.numpy as jnp
from jax import lax
import numpy as np

D_MODEL = 2048
BATCH = 1
SEQ = 256
DEPTH = 2
DEC_BATCH = 8
DEC_SEQ = 8
PAST_LEN = 2048
PAGE_SIZE = 128

N_MIXERS = 2
N_POOL_LAYERS = (DEPTH + 1) // 2
N_MLSTM_LAYERS = DEPTH // 2
POOL_WINDOWS = (2, 4, 8, 16)
N_POOL_GROUPS = len(POOL_WINDOWS)
POOL_GROUP_DIM = D_MODEL // N_POOL_GROUPS
POOL_BUF = max(POOL_WINDOWS) - 1
MLSTM_HEADS = 4
QK_DIM = D_MODEL // 2
V_DIM = D_MODEL
QK_HEAD_DIM = QK_DIM // MLSTM_HEADS
V_HEAD_DIM = V_DIM // MLSTM_HEADS
MLSTM_IN_DIM = 2 * QK_DIM + 2 * V_DIM + 2 * MLSTM_HEADS
CHUNK = 64
GATE_CAP = 15.0
D_FF = 4 * D_MODEL
EPS = 1e-6

kernel_name = "hybrid_pool_mlstm_decoder_step"

def rmsnorm(x, g):
    xf = x.astype(jnp.float32)
    y = xf * lax.rsqrt(jnp.mean(xf * xf, axis=-1, keepdims=True) + EPS)
    return (y * g.astype(jnp.float32)).astype(x.dtype)

def sq_relu_mlp(u, w_up, w_down):
    a = jax.nn.relu(u @ w_up)
    return (a * a) @ w_down

def pool_mixer(u, buf, pos0, w_group, scale):
    B, T, D = u.shape
    P = POOL_BUF
    u_ext = jnp.concatenate([buf.astype(u.dtype), u], axis=1).astype(jnp.float32)
    cs = jnp.cumsum(jnp.pad(u_ext, ((0, 0), (1, 0), (0, 0))), axis=1)
    pos = pos0 + jnp.arange(T, dtype=jnp.int32)
    outs = []
    for g, w in enumerate(POOL_WINDOWS):
        sl = slice(g * POOL_GROUP_DIM, (g + 1) * POOL_GROUP_DIM)
        s = cs[:, P + 1:P + 1 + T, sl] - cs[:, P + 1 - w:P + 1 - w + T, sl]
        cnt = jnp.minimum(pos + 1, w).astype(jnp.float32)
        outs.append(s / cnt[None, :, None])
    pooled = jnp.concatenate(outs, axis=-1)
    d = (pooled - u_ext[:, P:]).reshape(B, T, N_POOL_GROUPS, POOL_GROUP_DIM)
    y = jnp.einsum('btgc,gcd->btgd', d, w_group.astype(jnp.float32)).reshape(B, T, D)
    y = y * scale.astype(jnp.float32)
    new_buf = u_ext[:, T:]
    return y.astype(u.dtype), new_buf

def mlstm_chunkwise(q, k, v, i_pre, logf, C0, n0, m0):
    B, H, T, DK = q.shape
    DV = v.shape[-1]
    L = math.gcd(T, CHUNK)
    NC = T // L

    def to_chunks(a):
        return jnp.moveaxis(a.reshape(B, H, NC, L, *a.shape[3:]), 2, 0)

    xs = (to_chunks(q), to_chunks(k), to_chunks(v), to_chunks(i_pre), to_chunks(logf))
    causal = jnp.tril(jnp.ones((L, L), dtype=bool))

    def step(carry, inp):
        C, n, m = carry
        qc, kc, vc, ic, fc = inp
        b = jnp.cumsum(fc, axis=-1)
        a = b + m[..., None]
        Dm = b[..., :, None] - b[..., None, :] + ic[..., None, :]
        Dm = jnp.where(causal, Dm, -jnp.inf)
        m_row = jnp.maximum(a, jnp.max(Dm, axis=-1))
        w_intra = jnp.exp(Dm - m_row[..., None])
        w_inter = jnp.exp(a - m_row)
        s = jnp.einsum('bhik,bhjk->bhij', qc, kc) * w_intra
        num = w_inter[..., None] * jnp.einsum('bhik,bhkv->bhiv', qc, C) + jnp.einsum('bhij,bhjv->bhiv', s, vc)
        den = w_inter * jnp.einsum('bhik,bhk->bhi', qc, n) + jnp.sum(s, axis=-1)
        h = num / jnp.maximum(jnp.abs(den), jnp.exp(-m_row))[..., None]
        bL = b[..., -1]
        m_new = m_row[..., -1]
        decay = jnp.exp(bL + m - m_new)
        w_k = jnp.exp(bL[..., None] - b + ic - m_new[..., None])
        kw = kc * w_k[..., None]
        C_new = decay[..., None, None] * C + jnp.einsum('bhjk,bhjv->bhkv', kw, vc)
        n_new = decay[..., None] * n + jnp.sum(kw, axis=2)
        return (C_new, n_new, m_new), h

    carry0 = (C0.astype(jnp.float32), n0.astype(jnp.float32), m0.astype(jnp.float32))
    (C, n, m), hs = lax.scan(step, carry0, xs)
    h = jnp.moveaxis(hs, 0, 2).reshape(B, H, T, DV)
    return h, C, n, m

def mlstm_mixer(u, C0, n0, m0, w_in, b_gate, head_norm, w_out):
    B, T, _ = u.shape
    proj = u @ w_in
    splits = np.cumsum([QK_DIM, QK_DIM, V_DIM, V_DIM, MLSTM_HEADS]).tolist()
    q, k, v, o, i_g, f_g = jnp.split(proj, splits, axis=-1)
    f32 = jnp.float32
    q = q.astype(f32).reshape(B, T, MLSTM_HEADS, QK_HEAD_DIM).transpose(0, 2, 1, 3) * (QK_HEAD_DIM ** -0.5)
    k = k.astype(f32).reshape(B, T, MLSTM_HEADS, QK_HEAD_DIM).transpose(0, 2, 1, 3)
    v = v.astype(f32).reshape(B, T, MLSTM_HEADS, V_HEAD_DIM).transpose(0, 2, 1, 3)
    bg = b_gate.astype(f32)
    i_pre = GATE_CAP * jnp.tanh((i_g.astype(f32) + bg[:MLSTM_HEADS]) / GATE_CAP)
    f_pre = GATE_CAP * jnp.tanh((f_g.astype(f32) + bg[MLSTM_HEADS:]) / GATE_CAP)
    logf = jax.nn.log_sigmoid(f_pre)
    h, C, n, m = mlstm_chunkwise(q, k, v, i_pre.transpose(0, 2, 1), logf.transpose(0, 2, 1), C0, n0, m0)
    h = h.transpose(0, 2, 1, 3)
    h = h * lax.rsqrt(jnp.mean(h * h, axis=-1, keepdims=True) + EPS)
    h = h.reshape(B, T, V_DIM) * head_norm.astype(f32)
    out = (jax.nn.sigmoid(o.astype(f32)) * h).astype(u.dtype) @ w_out
    return out, C, n, m

def trunk(x, pos0, pool_state, C_state, n_state, m_state, norm_mix, norm_ffn, norm_final,
          pool_w, pool_scale, mlstm_w_in, mlstm_b_gate, mlstm_head_norm, mlstm_w_out, ffn_w_up, ffn_w_down):
    h = x
    new_pool, new_C, new_n, new_m = [], [], [], []
    for layer in range(DEPTH):
        j = layer // N_MIXERS
        u = rmsnorm(h, norm_mix[layer])
        if layer % N_MIXERS == 0:
            y, buf = pool_mixer(u, pool_state[j], pos0, pool_w[j], pool_scale[j])
            new_pool.append(buf)
        else:
            y, C, n, m = mlstm_mixer(u, C_state[j], n_state[j], m_state[j], mlstm_w_in[j],
                                     mlstm_b_gate[j], mlstm_head_norm[j], mlstm_w_out[j])
            new_C.append(C)
            new_n.append(n)
            new_m.append(m)
        h = h + y.astype(h.dtype)
        h = h + sq_relu_mlp(rmsnorm(h, norm_ffn[layer]), ffn_w_up[layer], ffn_w_down[layer]).astype(h.dtype)
    dt = x.dtype
    return (rmsnorm(h, norm_final), jnp.stack(new_pool).astype(dt), jnp.stack(new_C).astype(dt),
            jnp.stack(new_n).astype(dt), jnp.stack(new_m).astype(dt))

def setup_inputs(seed: int = 0) -> dict:
    key = jax.random.key(seed)
    ks = jax.random.split(key, 20)
    nrm = jax.random.normal
    f32 = jnp.float32
    b_i = 0.1 * nrm(ks[10], (N_MLSTM_LAYERS, MLSTM_HEADS), f32)
    b_f = jnp.linspace(3.0, 6.0, MLSTM_HEADS, dtype=f32)[None, :] + 0.1 * nrm(ks[11], (N_MLSTM_LAYERS, MLSTM_HEADS), f32)
    return {
        "x_prompt": nrm(ks[0], (BATCH, SEQ, D_MODEL), f32),
        "x_sample": nrm(ks[1], (DEC_BATCH, DEC_SEQ, D_MODEL), f32),
        "state_pool": nrm(ks[2], (N_POOL_LAYERS, DEC_BATCH, POOL_BUF, D_MODEL), f32),
        "state_mlstm_C": 0.05 * nrm(ks[3], (N_MLSTM_LAYERS, DEC_BATCH, MLSTM_HEADS, QK_HEAD_DIM, V_HEAD_DIM), f32),
        "state_mlstm_n": 0.1 * nrm(ks[4], (N_MLSTM_LAYERS, DEC_BATCH, MLSTM_HEADS, QK_HEAD_DIM), f32),
        "state_mlstm_m": nrm(ks[5], (N_MLSTM_LAYERS, DEC_BATCH, MLSTM_HEADS), f32),
        "norm_mix": 1.0 + 0.02 * nrm(ks[6], (DEPTH, D_MODEL), f32),
        "norm_ffn": 1.0 + 0.02 * nrm(ks[7], (DEPTH, D_MODEL), f32),
        "norm_final": 1.0 + 0.02 * nrm(ks[8], (D_MODEL,), f32),
        "pool_w": nrm(ks[9], (N_POOL_LAYERS, N_POOL_GROUPS, POOL_GROUP_DIM, POOL_GROUP_DIM), f32) * POOL_GROUP_DIM ** -0.5,
        "pool_scale": 1.0 + 0.02 * nrm(ks[12], (N_POOL_LAYERS, D_MODEL), f32),
        "mlstm_w_in": nrm(ks[13], (N_MLSTM_LAYERS, D_MODEL, MLSTM_IN_DIM), f32) * D_MODEL ** -0.5,
        "mlstm_b_gate": jnp.concatenate([b_i, b_f], axis=-1),
        "mlstm_head_norm": 1.0 + 0.02 * nrm(ks[14], (N_MLSTM_LAYERS, V_DIM), f32),
        "mlstm_w_out": nrm(ks[15], (N_MLSTM_LAYERS, V_DIM, D_MODEL), f32) * V_DIM ** -0.5,
        "ffn_w_up": nrm(ks[16], (DEPTH, D_MODEL, D_FF), f32) * D_MODEL ** -0.5,
        "ffn_w_down": nrm(ks[17], (DEPTH, D_FF, D_MODEL), f32) * D_FF ** -0.5,
    }

def reference(x_prompt, x_sample, state_pool, state_mlstm_C, state_mlstm_n, state_mlstm_m,
              norm_mix, norm_ffn, norm_final, pool_w, pool_scale, mlstm_w_in, mlstm_b_gate,
              mlstm_head_norm, mlstm_w_out, ffn_w_up, ffn_w_down):
    B = x_prompt.shape[0]
    dt = x_prompt.dtype
    pool0 = jnp.zeros((N_POOL_LAYERS, B, POOL_BUF, D_MODEL), dt)
    C0 = jnp.zeros((N_MLSTM_LAYERS, B, MLSTM_HEADS, QK_HEAD_DIM, V_HEAD_DIM), jnp.float32)
    n0 = jnp.zeros((N_MLSTM_LAYERS, B, MLSTM_HEADS, QK_HEAD_DIM), jnp.float32)
    m0 = jnp.zeros((N_MLSTM_LAYERS, B, MLSTM_HEADS), jnp.float32)
    y_prompt, pool_p, C_p, n_p, m_p = trunk(
        x_prompt, 0, pool0, C0, n0, m0, norm_mix, norm_ffn, norm_final, pool_w, pool_scale,
        mlstm_w_in, mlstm_b_gate, mlstm_head_norm, mlstm_w_out, ffn_w_up, ffn_w_down)
    y_sample, pool_s, C_s, n_s, m_s = trunk(
        x_sample, PAST_LEN, state_pool, state_mlstm_C, state_mlstm_n, state_mlstm_m,
        norm_mix, norm_ffn, norm_final, pool_w, pool_scale,
        mlstm_w_in, mlstm_b_gate, mlstm_head_norm, mlstm_w_out, ffn_w_up, ffn_w_down)
    return (y_prompt, y_sample, pool_p, pool_s, C_p, n_p, m_p, C_s, n_s, m_s)


_drawn_inputs = setup_inputs


def setup_inputs(seed=0):
    import zlib

    import numpy as np

    out = dict(_drawn_inputs(seed))
    spreads = {}
    factors = {}
    for name, (base, spread) in spreads.items():
        noise = np.random.default_rng([zlib.crc32(name.encode()), seed]).standard_normal(out[name].shape)
        drawn = base * np.exp(spread * noise) if base else spread * noise
        out[name] = __import__('jax').numpy.asarray(drawn.astype(out[name].dtype))
    for name, factor in factors.items():
        out[name] = (out[name] * factor).astype(out[name].dtype)
    return out
```

```python
from contextlib import ExitStack

import numpy as np

import concourse.bass as bass
from concourse import mybir

F32 = mybir.dt.float32
F32R = mybir.dt.float32r
ACT = mybir.ActivationFunctionType
ALU = mybir.AluOpType

P = 128
D = 2048
KT = D // P
TP, NSEQ, TS = 256, 8, 8
NS = NSEQ * TS
T = TP + NS
TT = 3
ROWS = (P, P, NS)
EPS = 1e-6

RING = 4
CK = 2
NC = 512
MT = NC // P
CH = KT // CK
LEAD = 3

GROUPS = 4
PAD = 15
SEG = PAD + TS
UX = PAD + TP + NSEQ * SEG

HEADS, DK, DV = 4, 256, 512
QSCALE = DK ** -0.5
CAP = 15.0
NEG = -1e30
GP = 32
D_FF = 4 * D
SLICES = D_FF // D

V_MIX, V_FFN, V_FIN, V_SCALE, V_HEAD, V_ALL = 0, 32, 64, 80, 96, 112

S_FFN0, S_QKV, S_O, S_OUT, S_FFN1, S_END = 0, 32, 40, 44, 48, 80

R_NEGM, R_E, R_WI, R_DEC, R_WK, R_ALL = 0, T, 2 * T, 2 * T + NS, 2 * T + NS + 16, 3 * T + NS + 16
BC = T + NS + 16


def chunk_no(s, c):
    return s * CH + (2 * GROUPS + c)


def used(s, c):
    return s * (CH + MT - 1) + (5 * GROUPS + (c + 1 if c < CH - 1 else CH + MT - 1))


def tile_done(s, m):
    return s * (CH + MT - 1) + (5 * GROUPS + CH + m)


def pool_used(g, c):
    return 5 * g + (1 if c == 0 else 5)


def pool_tile(g, m):
    return 5 * g + 2 + m


def used_before(s, c):
    if c >= RING:
        return used(s, c - RING)
    if isinstance(s, int) and s == 0:
        return pool_used((RING + c) // 2, c % 2)
    return used(s - 1, c + CH - RING)


def tiles_out(s, m):
    return s * MT + (MT * GROUPS + m + 1)


def fill_list():
    prep = lambda h: [("turn", h, t) for t in range(TT)] + [("rows", h, 0), ("score", h, 0)]
    out = [("cols", 0, 0)] + prep(0)
    for h in range(HEADS):
        out.append(("num", h, 0))
        pieces = prep(h + 1) if h + 1 < HEADS else []
        for b in range(NSEQ):
            if b < len(pieces):
                out.append(pieces[b])
            if b == 5:
                out.append(("n", h, 0))
            out.append(("upd", h, b))
        out.append(("updp", h, 0))
    return out


FILL = {f: n + 1 for n, f in enumerate(fill_list())}
ACT_FILL = {f: n + 1 for n, f in enumerate([f for f in fill_list() if f[0] in ("turn", "rows", "updp")])}
X3_USES = {u: n + 1 for n, u in enumerate(["den0", "den1", "ms0", "den2", "ms1", "den3", "ms2", "ms3"])}


def c_slot(b):
    return b % 3


def c_loads(h, b):
    return (3 if c_slot(b) < 2 else 2) * h + b // 3 + 1


def c_stores(h, b):
    return 3 * h + b // 3 + 1


def bc(ap, shape):
    return ap.unsqueeze(1).broadcast_to(shape)


def build(nc, A, O):
    with ExitStack() as ctx:
        def sb(name, shape, dt=F32, where=ctx):
            return where.enter_context(nc.sbuf_tensor(name, shape, dt))

        def head_rows(name, shape, where=ctx):
            full = sb(name, [GP + HEADS] + shape, F32, where)
            return full[GP:GP + HEADS, :] if len(shape) == 1 else full[GP:GP + HEADS, :, :]

        def sem(name):
            return ctx.enter_context(nc.semaphore(name))

        hT = sb("hT", [P, KT, T])
        w_raw = sb("w_raw", [P, RING, CK, NC])
        w_hi = sb("w_hi", [P, RING, CK, NC], F32R)
        w_lo = sb("w_lo", [P, RING, CK, NC], F32R)
        ident = sb("ident", [P, P])
        ones = sb("ones", [P, P])
        causal = sb("causal", [P, P])
        causal_s = sb("causal_s", [P, NS])
        seqmask = sb("seqmask", [P, TT, 1 + NSEQ])
        sel = head_rows("sel", [HEADS, P])
        icnt = sb("icnt", [P, PAD])
        vrow = sb("vrow", [P, P])
        vecs = sb("vecs", [P, V_ALL])
        Rb = sb("Rb", [P, T])
        rv = sb("rv", [P, T])
        acc = sb("acc", [P, T])
        sqt = sb("sqt", [P, T])
        xcol = sb("xcol", [P, 4])
        rcol = sb("rcol", [P, 4])
        bgate = head_rows("bgate", [2])
        m0 = head_rows("m0", [NSEQ])
        mnew = head_rows("mnew", [1 + NSEQ])

        with ExitStack() as r:
            srow = sb("srow", [P, D], F32, r)
            with ExitStack() as r2:
                xrow = sb("xrow", [P, TT, D], F32, r2)
            win = [sb(f"win{i}", [P, GROUPS, UX], F32, r) for i in range(3)]
            ur_s = sb("ur_s", [P, D], F32, r)
            diag = sb("diag", [P, TT, P], F32, r)
        with ExitStack() as r:
            yT = sb("yT", [P, KT, T], F32, r)
        op_hi = sb("op_hi", [P, KT, T], F32R)
        op_lo = sb("op_lo", [P, KT, T], F32R)

        with ExitStack() as r:
            qkv = sb("qkv", [P, 2 * KT, T], F32, r)
        a_hi = sb("a_hi", [P, KT, T], F32R)
        a_lo = sb("a_lo", [P, KT, T], F32R)

        with ExitStack() as r:
            uext = sb("uext", [P, KT, UX], F32, r)
            win.append(sb("win3", [P, GROUPS, UX], F32, r))
            ur_p = sb("ur_p", [P, 2, NC], F32, r)
            dtmp = sb("dtmp", [P, MT, T], F32, r)
            us = sb("us", [P, KT, NS], F32, r)
        with ExitStack() as r:
            with ExitStack() as r2:
                gw_raw = sb("gw_raw", [P, KT, 2 * HEADS], F32, r2)
                gw_hi = sb("gw_hi", [P, KT, 68], F32R, r2)
                gw_lo = sb("gw_lo", [P, KT, 68], F32R, r2)
            with ExitStack() as r2:
                scan_p = [head_rows(f"scan_p{i}", [P + TP], r2) for i in range(2)]
                scan_s = [head_rows(f"scan_s{i}", [NSEQ, 4 + TS], r2) for i in range(2)]
                pad_ = sb("pad_", [P, 1500], F32, r2)
                grow = head_rows("grow", [T], r2)
                nbrow = head_rows("nbrow", [T], r2)
                mrow = head_rows("mrow", [T], r2)
                gz = head_rows("gz", [2, T], r2)
            pad2 = sb("pad2", [P, 4608], F32, r)
            relu = sb("relu", [P, MT, T], F32, r)
            sq = sb("sq", [P, 2, T], F32, r)
            yrow = sb("yrow", [P, TT, D], F32, r)
        with ExitStack() as r:
            kv = sb("kv", [P, 2, TT, DV + DK], F32, r)
            cst = sb("cst", [P, 3, 2, DV], F32, r)
            ST = sb("ST", [P, 2, 448], F32, r)
            EW = sb("EW", [P, 2, BC], F32, r)
            eb = sb("eb", [P, 448], F32, r)
            qw = sb("qw", [P, 2, 2, NS], F32, r)
            qn = sb("qn", [P, 2, 2, NS], F32, r)
            nts = sb("nts", [P, 2 * (1 + NSEQ)], F32, r)
            kwb = sb("kwb", [P, 2, DK], F32, r)
            kwp = sb("kwp", [P, 2, DK], F32, r)
            wkm = sb("wkm", [P, TT, 1 + NSEQ], F32, r)
            gates_n = sb("gates_n", [GP + HEADS, R_ALL], F32, r)
            nrow = gates_n[0:1 + NSEQ, 0:HEADS * DK]
            gates = gates_n[GP:GP + HEADS, :]
            cols = sb("cols", [P, 6, HEADS], F32, r)
            dect = sb("dect", [1 + NSEQ, HEADS], F32, r)
        rden, r2b, hss = rv, sqt, acc

        G = ctx.enter_context(nc.psum_tensor("G", [P, MT, 512], F32))
        X = [ctx.enter_context(nc.psum_tensor(f"X{i}", [P, 512], F32)) for i in range(4)]

        x_in = [sem(f"x_in{t}") for t in range(TT)]
        state_in = sem("state_in")
        vecs_in = sem("vecs_in")
        small_in = sem("small_in")
        w_in = [sem(f"w_in{i}") for i in range(RING)]
        c_in = [sem(f"c_in{i}") for i in range(3)]
        c_out = [sem(f"c_out{i}") for i in range(3)]
        rows_out = [sem(f"rows_out{i}") for i in range(2)]
        outs = sem("outs")
        y_out = sem("y_out")
        consts = sem("consts")
        w_hi_ok = sem("w_hi_ok")
        w_lo_ok = sem("w_lo_ok")
        gemm = sem("gemm")
        evicted = sem("evicted")
        x_sq = sem("x_sq")
        x_turned = sem("x_turned")
        x_kept = sem("x_kept")
        s_turned = sem("s_turned")
        s_kept = sem("s_kept")
        r_sum = sem("r_sum")
        r_inv = sem("r_inv")
        r_ok = sem("r_ok")
        dve = sem("dve_chain")
        pool_c = sem("pool_chain")
        act_c = sem("act_chain")
        vec_turned = sem("vec_turned")
        u_ok = sem("u_ok")
        us_ok = sem("us_ok")
        win_ok = sem("win_ok")
        d_ok = sem("d_ok")
        d_hi_ok = sem("d_hi_ok")
        d_lo_ok = sem("d_lo_ok")
        np_turned = sem("np_turned")
        np_kept = sem("np_kept")
        op_hi_ok = sem("op_hi_ok")
        op_lo_ok = sem("op_lo_ok")
        sq_ok = sem("sq_ok")
        ssq_ok = sem("ssq_ok")
        a_hi_ok = sem("a_hi_ok")
        a_sq_ok = sem("a_sq_ok")
        a_lo_ok = sem("a_lo_ok")
        gw_hi_ok = sem("gw_hi_ok")
        gw_lo_ok = sem("gw_lo_ok")
        gates_sum = sem("gates_sum")
        gz_ok = sem("gz_ok")
        tanh_ok = sem("tanh_ok")
        g_ok = sem("g_ok")
        m_ok = sem("m_ok")
        rows_ok = sem("rows_ok")
        gates_exp = sem("gates_exp")
        filled = sem("filled")
        drained = sem("drained")
        drained_a = sem("drained_a")
        eb_exp = sem("eb_exp")
        prep_ok = sem("prep_ok")
        x3_filled = sem("x3_filled")
        x3_read = sem("x3_read")
        x2_filled = sem("x2_filled")
        att_s = sem("att_s")
        kw_ok = sem("kw_ok")
        hss_ok = sem("hss_ok")
        ez_ok = sem("ez_ok")
        ez1_ok = sem("ez1_ok")
        r2_inv = sem("r2_inv")
        r2_ok = sem("r2_ok")
        att_ok = sem("att_ok")
        att_hi_ok = sem("att_hi_ok")
        att_lo_ok = sem("att_lo_ok")
        y_ok = sem("y_ok")
        y_turned = sem("y_turned")
        y_kept_a = sem("y_kept_a")
        y_kept_d = sem("y_kept_d")
        y_done = [sem(f"y_done{t}") for t in range(TT)]

        w_up = [A["ffn_w_up"][i].rearrange("(c t p) n -> c p t n", t=CK, p=P) for i in range(2)]
        w_down = [A["ffn_w_down"][i].rearrange("(s c t p) n -> s c p t n", c=CH, t=CK, p=P) for i in range(2)]
        w_qkvo = A["mlstm_w_in"][0].rearrange("(c t p) n -> c p t n", t=CK, p=P)
        w_out = A["mlstm_w_out"][0].rearrange("(c t p) n -> c p t n", t=CK, p=P)
        w_pool = A["pool_w"][0].rearrange("g (c t p) n -> g c p t n", t=CK, p=P)
        w_gate = A["mlstm_w_in"][0].rearrange("(k p) n -> p k n", p=P)[:, :, 2 * HEADS * DK + 2 * D:]
        c_dram = A["state_mlstm_C"][0].rearrange("b h (t p) n -> b h p t n", p=P)
        c_new = O["C_sample"][0].rearrange("b h (t p) n -> b h p t n", p=P)
        c_new_p = O["C_prompt"][0, 0].rearrange("h (t p) n -> h p t n", p=P)

        def vec(n):
            return vecs[:, n:n + 1]

        def tok(t):
            return slice(t * P, t * P + ROWS[t])

        def head_block(h):
            return 4 * h

        def z_block(h):
            return 0 if h < 3 else 12

        def sq_block(h):
            return 4 if h < 3 else 8

        def att(h):
            return qkv[:, KT + 4 * h:KT + 4 * h + 4, :]

        def seqs(row, a=0):
            return row[:, a + TP:a + T].rearrange("h (b t) -> h b t", t=TS)

        def scan(eng, link, op):
            for n in range(8):
                w, a, b = 1 << n, scan_p[n % 2], scan_p[1 - n % 2]
                link(eng.tensor_tensor(b[:, P:], a[:, P:], a[:, P - w:P + TP - w], op))
            for n in range(3):
                w, a, b = 1 << n, scan_s[n % 2], scan_s[1 - n % 2]
                link(eng.tensor_tensor(b[:, :, 4:], a[:, :, 4:], a[:, :, 4 - w:4 + TS - w], op))

        block = ctx.enter_context(nc.Block())

        @block.sync
        def _(sp):
            for t in range(TT):
                src = A["x_prompt"][0, t * P:(t + 1) * P, :] if t < 2 else A["x_sample"].rearrange("b t d -> (b t) d")
                sp.dma_start(xrow[0:ROWS[t], t, :], src).then_inc(x_in[t], 16)
            sp.dma_start(srow[0:NSEQ * PAD, :], A["state_pool"][0].rearrange("b r d -> (b r) d")).then_inc(state_in, 16)

            def load(s, c, src):
                sp.wait_ge(w_lo_ok, chunk_no(s, c) - RING + 1)
                sp.dma_start(w_raw[:, c % RING], src).then_inc(w_in[c % RING], 16)

            def state_load(h, b):
                if h or b > 2:
                    prev = (h, b - 3) if b > 2 else (h - 1, b + 6)
                    sp.wait_ge(c_out[c_slot(b)], 16 * c_stores(*prev))
                sp.dma_start(cst[:, c_slot(b)], c_dram[b, h]).then_inc(c_in[c_slot(b)], 16)

            def state_store(h, b):
                if b < NSEQ:
                    sp.wait_ge(drained, FILL["upd", h, b])
                    sp.dma_start(c_new[b, h], cst[:, c_slot(b)]).then_inc(c_out[c_slot(b)], 16)
                else:
                    sp.wait_ge(drained, FILL["updp", h, 0])
                    sp.wait_ge(drained_a, ACT_FILL["updp", h, 0])
                    sp.dma_start(c_new_p[h], cst[:, c_slot(b)]).then_inc(c_out[c_slot(b)], 16)

            for g in range(GROUPS):
                for c in range(2):
                    n = 2 * g + c
                    if n >= RING:
                        sp.wait_ge(w_lo_ok, n - RING + 1)
                    sp.dma_start(w_raw[:, n % RING], w_pool[g, c]).then_inc(w_in[n % RING], 16)

            def ffn(layer, s0):
                with sp.Fori(0, SLICES) as sl:
                    with sp.Fori(0, MT) as j:
                        for c in range(CH):
                            load(s0 + sl * 8 + j, c, w_up[layer][c][:, :, bass.ds(sl * D + j * NC, NC)])
                    with sp.Fori(0, MT) as j:
                        for c in range(CH):
                            load(s0 + 4 + sl * 8 + j, c, w_down[layer][sl, c][:, :, bass.ds(j * NC, NC)])

            ffn(0, S_FFN0)
            with sp.Fori(0, 8) as j:
                for c in range(CH):
                    load(S_QKV + j, c, w_qkvo[c][:, :, bass.ds(j * NC, NC)])
            sp.wait_ge(op_lo_ok, 2 * KT)
            sp.wait_ge(a_lo_ok, SLICES * KT)
            for b in range(3):
                state_load(0, b)
            for q in range(HEADS + 1):
                for c in range(CH):
                    if q < HEADS:
                        load(S_O + q, c, w_qkvo[c][:, :, (8 + q) * NC:(9 + q) * NC])
                    else:
                        load(S_OUT, c, w_out[c][:, :, 0:NC])
                    if q == 0:
                        continue
                    for b in (c, NSEQ) if c == CH - 1 else (c,):
                        state_store(q - 1, b)
                        if b + 3 < NSEQ:
                            state_load(q - 1, b + 3)
                        elif b + 3 > NSEQ and q < HEADS:
                            state_load(q, b - 6)
            with sp.Fori(1, MT) as j:
                for c in range(CH):
                    load(S_OUT + j, c, w_out[c][:, :, bass.ds(j * NC, NC)])
            ffn(1, S_FFN1)
            for t in range(TT):
                sp.wait_ge(y_done[t], 1)
                dst = O["y_prompt"][0, t * P:(t + 1) * P, :] if t < 2 else O["y_sample"].rearrange("b t d -> (b t) d")
                sp.dma_start(dst, yrow[0:ROWS[t], t, :]).then_inc(y_out, 16)
            for i in range(3):
                sp.wait_ge(c_out[i], 16 * 3 * HEADS)
            for i in range(2):
                sp.wait_ge(rows_out[i], 16 * 2)
            sp.wait_ge(outs, 16 * (1 + NSEQ + 2 + 2))
            sp.wait_ge(y_out, 16 * TT)

        @block.gpsimd
        def _(pool):
            n_chain = [0]

            def link(ins):
                n_chain[0] += 1
                ins.then_inc(pool_c, 1)
                pool.wait_ge(pool_c, n_chain[0])

            for n, (name, at) in enumerate((("norm_mix", V_MIX), ("norm_ffn", V_FFN), ("norm_final", V_FIN),
                                            ("pool_scale", V_SCALE), ("mlstm_head_norm", V_HEAD))):
                src = A[name]
                src = src.rearrange("(k p) -> k p", p=P) if len(src.shape) == 1 else src.rearrange("l (k p) -> (l k) p", p=P)
                pool.dma_start(vrow[at:at + src.shape[0], :], src).then_inc(vecs_in, 16)
            def select(ap, pattern, cm, base=0, op=ALU.is_ge, fill=0.0):
                link(pool.affine_select(out=ap, in_=ap, compare_op=op, fill=fill, base=base, pattern=pattern,
                                        channel_multiplier=cm))

            link(pool.memset(ident[:, :], 0.0))
            select(ident[:, :], [[-1, P]], 1, op=ALU.not_equal, fill=1.0)
            link(pool.memset(ones[:, :], 1.0))
            link(pool.memset(uext[:, :, 0:PAD], 0.0))
            for n in range(PAD):
                link(pool.memset(icnt[:, n:n + 1], 1.0 / (n + 1)))
            link(pool.memset(causal[:, :], 0.0))
            select(causal[:, :], [[1, P]], -1, fill=NEG)
            link(pool.memset(causal_s[:, :], 0.0))
            select(causal_s[:, :], [[1, NS]], -1, fill=NEG)
            select(causal_s[:, :].rearrange("p (b t) -> p b t", t=TS), [[-TS, NSEQ], [0, TS]], 1, fill=NEG)
            link(pool.memset(seqmask[:, :, :], 0.0))
            link(pool.memset(seqmask[:, 0:2, 0:1], 1.0))
            link(pool.memset(seqmask[:, 2, 1:], 1.0))
            select(seqmask[:, 2, 1:], [[-TS, NSEQ]], 1)
            select(seqmask[:, 2, 1:], [[TS, NSEQ]], -1, base=TS - 1)
            link(pool.memset(sel[:, :, :], 0.0))
            select(sel[:, :, :], [[-1, HEADS], [0, P]], 1, op=ALU.not_equal, fill=1.0)
            pool.memset(xcol[:, :], 1.0).then_inc(consts, 1)
            pool.wait_ge(consts, 1)
            pool.dma_start(O["pool_sample"][0, :, 0:PAD - TS, :], A["state_pool"][0, :, TS:PAD, :]).then_inc(outs, 16)
            with nc.allow_non_contiguous_dma("a few values"):
                pool.dma_start(bgate[:, :], A["mlstm_b_gate"][0].rearrange("(g h) -> h g", h=HEADS)).then_inc(small_in, 16)
                pool.dma_start(m0[:, :], A["state_mlstm_m"][0].rearrange("b h -> h b")).then_inc(small_in, 16)

            def pack(g):
                pool.wait_ge(u_ok, 2 * (4 * g + 4))
                src = uext[:, 4 * g:4 * g + 4, PAD + TP:].rearrange("p k (b r) -> p k b r", r=SEG)[:, :, :, PAD:]
                pool.tensor_copy(us[:, 4 * g:4 * g + 4, :].rearrange("p k (b t) -> p k b t", t=TS), src).then_inc(us_ok, 1)

            pack(0)
            pack(1)
            for g in (2, 3):
                pack(g)
                pool.wait_ge(u_ok, 2 * (4 * g + 4))
                pool.wait_ge(s_kept, g + 1)
                if g == 3:
                    pool.wait_ge(d_ok, 3)
                src = uext[:, 4 * g:4 * g + 4, :]
                for n in range(g + 1):
                    w = 1 << n
                    dst = win[1 + n % 2]
                    ins = pool.tensor_tensor(dst[:, :, 2 * w - 1:], src[:, :, 2 * w - 1:], src[:, :, w - 1:UX - w], ALU.add)
                    if n < g:
                        link(ins)
                    src = dst
                ins.then_inc(win_ok, 1)

            def new_pool_rows(g):
                pool.wait_ge(np_kept, 2 * g + 1)
                pool.dma_start(O["pool_prompt"][0, 0, :, g * NC:(g + 1) * NC],
                               ur_p[P - PAD:P, g % 2, :]).then_inc(rows_out[g % 2], 16)

            new_pool_rows(0)
            new_pool_rows(1)

            def squares(j, base):
                if j:
                    pool.wait_ge(r_inv, 2 * j)
                link(pool.memset(acc[:, :], 0.0))
                for k in range(KT):
                    pool.wait_ge(evicted, base + k + 1)
                    pool.tensor_tensor(sqt[:, :], hT[:, k, :], hT[:, k, :], ALU.mult).then_inc(sq_ok, 1)
                    pool.wait_ge(sq_ok, KT * j + k + 1)
                    pool.tensor_tensor(acc[:, :], acc[:, :], sqt[:, :], ALU.add).then_inc(ssq_ok, 1)
                    pool.wait_ge(ssq_ok, KT * j + k + 1)

            squares(0, 0)
            new_pool_rows(2)
            new_pool_rows(3)
            pool.wait_ge(np_kept, 8)
            for b in range(NSEQ):
                pool.dma_start(O["pool_sample"][0, b, PAD - TS:, :], ur_s[b * TS:(b + 1) * TS, :]).then_inc(outs, 16)

            def ffn(layer, s0):
                f0 = 16 * SLICES * layer
                with pool.Fori(0, SLICES) as sl:
                    with pool.Fori(0, MT) as j:
                        hidden_tiles(f0 + sl * KT + j * MT, s0 + sl * 8 + j, j * MT)

            def hidden_tiles(first, s, k0):
                for m in range(MT):
                    hi = a_hi[:, bass.ds(k0 + m, 1), :]
                    lo = a_lo[:, bass.ds(k0 + m, 1), :]
                    pool.wait_ge(evicted, tiles_out(s, m))
                    pool.tensor_tensor(sq[:, m % 2], relu[:, m], relu[:, m], ALU.mult).then_inc(a_sq_ok, 1)
                    pool.wait_ge(a_sq_ok, first + m + 1)
                    pool.wait_ge(a_hi_ok, first + m + 1)
                    pool.tensor_tensor(lo, sq[:, m % 2:m % 2 + 1], hi.bitcast(F32), ALU.subtract).then_inc(a_lo_ok, 1)

            pool.wait_ge(d_ok, 4)
            pool.wait_ge(outs, 16 * (1 + NSEQ))
            for i in range(2):
                pool.wait_ge(rows_out[i], 32)
            with nc.allow_non_contiguous_dma("8 columns"):
                pool.dma_start(gw_raw[:, :, :], w_gate).then_inc(small_in, 16)
            pool.memset(gw_hi[:, :, :].bitcast(F32), 0.0).then_inc(gw_lo_ok, 1)
            pool.memset(gw_lo[:, :, :].bitcast(F32), 0.0).then_inc(gw_lo_ok, 1)

            ffn(0, S_FFN0)
            squares(1, MT * GROUPS + MT * (S_QKV - MT))
            pool.wait_ge(gw_hi_ok, 2)
            pool.wait_ge(gw_lo_ok, 2)
            for n, at in enumerate((GP, 64)):
                pool.tensor_tensor(gw_lo[:, :, at:at + HEADS], gw_raw[:, :, n * HEADS:(n + 1) * HEADS],
                                   gw_hi[:, :, at:at + HEADS].bitcast(F32), ALU.subtract).then_inc(gw_lo_ok, 1)

            pool.wait_ge(gates_sum, 1)
            for i in range(2):
                link(pool.memset(scan_p[i][:, 0:P], 0.0))
                link(pool.memset(scan_s[i][:, :, 0:4], 0.0))
            pool.dma_start(nrow[1:, :], A["state_mlstm_n"][0].rearrange("b h d -> b (h d)")).then_inc(small_in, 16)
            pool.wait_ge(tanh_ok, 4)

            scan(pool, link, ALU.add)
            link(pool.tensor_copy(nbrow[:, 0:TP], scan_p[0][:, P:]))
            link(pool.tensor_copy(seqs(nbrow), scan_s[1][:, :, 4:]))
            link(pool.tensor_scalar(grow[:, :], grow[:, :], CAP, None, ALU.mult))
            link(pool.tensor_tensor(grow[:, :], grow[:, :], nbrow[:, :], ALU.add))
            for i in range(2):
                link(pool.memset(scan_p[i][:, 0:P], NEG))
                link(pool.memset(scan_s[i][:, :, 0:4], NEG))
            link(pool.tensor_copy(scan_p[0][:, P:], grow[:, 0:TP]))
            pool.tensor_copy(scan_s[0][:, :, 4:], seqs(grow)).then_inc(g_ok, 1)
            pool.wait_ge(m_ok, 2)
            m0b = m0[:, :].unsqueeze(2).broadcast_to([HEADS, NSEQ, TS])
            last_s = seqs(mrow)[:, :, TS - 1]
            last_p = mrow[:, TP - 1:TP]
            link(pool.memset(gates[:, R_DEC:R_WK], 0.0))
            link(pool.tensor_scalar(gates[:, R_NEGM:R_E], mrow[:, :], -1.0, None, ALU.mult))
            link(pool.tensor_tensor(gates[:, R_E:R_WI], nbrow[:, :], mrow[:, :], ALU.subtract))
            link(pool.tensor_tensor(gates[:, R_WI:R_DEC].rearrange("h (b t) -> h b t", t=TS), m0b, seqs(mrow), ALU.subtract))
            link(pool.tensor_scalar(gates[:, R_DEC:R_DEC + 1], last_p, -1.0, None, ALU.mult))
            link(pool.tensor_tensor(gates[:, R_DEC + 1:R_DEC + 1 + NSEQ], m0[:, :], last_s, ALU.subtract))
            link(pool.tensor_tensor(gates[:, R_WK:R_WK + TP], grow[:, 0:TP], last_p.broadcast_to([HEADS, TP]), ALU.subtract))
            link(pool.tensor_tensor(seqs(gates, R_WK), seqs(grow),
                                    last_s.unsqueeze(2).broadcast_to([HEADS, NSEQ, TS]), ALU.subtract))
            link(pool.tensor_tensor(mnew[:, 0:1], last_p, nbrow[:, TP - 1:TP], ALU.subtract))
            link(pool.tensor_tensor(mnew[:, 1:], last_s, seqs(nbrow)[:, :, TS - 1], ALU.subtract))
            link(pool.memset(cols[:, :, :], 0.0))
            pool.memset(nrow[0:1, :], 0.0).then_inc(rows_ok, 1)
            with nc.allow_non_contiguous_dma("36 values"):
                pool.dma_start(O["m_prompt"][0].rearrange("b h -> h b"), mnew[:, 0:1]).then_inc(outs, 16)
                pool.dma_start(O["m_sample"][0].rearrange("b h -> h b"), mnew[:, 1:]).then_inc(outs, 16)

            for h in range(HEADS):
                kt = kv[:, h % 2, :, DV:]
                wk = cols[:, 1::2, h]
                pool.wait_ge(drained, FILL["turn", h, 2])
                if h:
                    pool.wait_ge(filled, FILL["updp", h - 1, 0])
                pool.tensor_tensor(wkm[:, :, :], seqmask[:, :, :],
                                   wk.unsqueeze(2).broadcast_to([P, TT, 1 + NSEQ]), ALU.mult).then_inc(kw_ok, 1)
                pool.wait_ge(kw_ok, 10 * h + 1)
                pool.tensor_tensor(kwp[:, :, :], kt[:, 0:2, :],
                                   wk[:, 0:2].unsqueeze(2).broadcast_to([P, 2, DK]), ALU.mult).then_inc(kw_ok, 1)
                for b in range(NSEQ):
                    if b > 1:
                        pool.wait_ge(filled, FILL["upd", h, b - 2])
                    pool.tensor_scalar(kwb[0:NS, b % 2, :], kt[0:NS, 2, :], wkm[0:NS, 2, 1 + b:2 + b], None,
                                       ALU.mult).then_inc(kw_ok, 1)
                pool.wait_ge(att_s, h + 1)
                s4 = qkv[:, sq_block(h):sq_block(h) + 4, :]
                link(pool.tensor_tensor(s4, att(h), att(h), ALU.mult))
                link(pool.tensor_tensor(s4[:, 0:2], s4[:, 0:2], s4[:, 2:4], ALU.add))
                if h:
                    pool.wait_ge(x3_filled, X3_USES[f"ms{h - 1}"])
                pool.tensor_tensor(hss[:, :], s4[:, 0], s4[:, 1], ALU.add).then_inc(hss_ok, 1)
                pool.wait_ge(ez_ok, h + 1)
                z4 = qkv[:, z_block(h):z_block(h) + 4, :]
                pool.tensor_scalar(z4, z4, 1.0, None, ALU.add).then_inc(ez1_ok, 1)
            pool.wait_ge(drained, FILL["n", HEADS - 1, 0])
            pool.dma_start(O["n_prompt"][0].rearrange("b h d -> b (h d)"), nrow[0:1, :]).then_inc(outs, 16)
            pool.dma_start(O["n_sample"][0].rearrange("b h d -> b (h d)"), nrow[1:, :]).then_inc(outs, 16)
            pool.wait_ge(x3_filled, X3_USES["ms3"])
            pool.wait_ge(att_ok, HEADS)
            pool.wait_ge(hss_ok, HEADS)
            squares(2, MT * GROUPS + MT * S_OUT)
            ffn(1, S_FFN1)
            squares(3, MT * GROUPS + MT * (S_END - MT))
            pool.wait_ge(r_ok, 5)
            pool.wait_ge(y_kept_a, 2 * MT)
            pool.tensor_scalar(yrow[0:NS, 2, :], yrow[0:NS, 2, :], rcol[0:NS, 2:3], None, ALU.mult).then_inc(y_done[2], 1)

        @block.scalar
        def _(act):
            def split(s, c):
                act.wait_ge(w_in[c % RING], (s * (CH // RING) + 2 + c // RING + 1) * 16)
                act.wait_ge(gemm, used_before(s, c))
                act.activation(w_hi[:, c % RING], w_raw[:, c % RING], ACT.Copy).then_inc(w_hi_ok, 1)

            def split_pool(n):
                act.wait_ge(w_in[n % RING], 16 * (n // RING + 1))
                if n >= RING:
                    act.wait_ge(gemm, pool_used((n - RING) // 2, n % 2))
                act.activation(w_hi[:, n % RING], w_raw[:, n % RING], ACT.Copy).then_inc(w_hi_ok, 1)

            def slab(s, after=None, mid=None, last=False):
                for i in range(CH):
                    c = LEAD + i
                    if c < CH:
                        split(s, c)
                    elif not last:
                        split(s + 1, c - CH)
                    if mid and i in mid:
                        mid[i]()
                for m in range(MT):
                    if after:
                        after(m)

            def root(j, dst, src):
                act.wait_ge(r_inv, 2 * j + 2)
                act.activation(dst, src, ACT.Sqrt).then_inc(r_ok, 1)

            for t in range(TT):
                act.wait_ge(x_in[t], 16)
                act.wait_ge(consts, 1)
                if t:
                    act.wait_ge(x_sq, t)
                act.activation(G[0:ROWS[t], :, :], xrow[0:ROWS[t], t, :].rearrange("p (a n) -> p a n", n=512), ACT.Square,
                               accum_out=xcol[0:ROWS[t], t:t + 1]).then_inc(x_sq, 1)
            for k in range(3):
                act.wait_ge(x_turned, k + 1)
                act.activation(hT[:, k, :], X[k % 3][:, 0:T], ACT.Copy).then_inc(x_kept, 1)
            root(0, rcol[:, 0:TT], rcol[:, 0:TT])
            for k in range(3, KT):
                act.wait_ge(x_turned, k + 1)
                act.activation(hT[:, k, :], X[k % 3][:, 0:T], ACT.Copy).then_inc(x_kept, 1)
                if k >= 13:
                    split_pool(k - 13)
            for g in range(GROUPS):
                act.wait_ge(s_turned, g + 1)
                dst = uext[:, 4 * g:4 * g + 4, PAD + TP:].rearrange("p k (b r) -> p k b r", r=SEG)[:, :, :, 0:PAD]
                for i in range(4):
                    ins = act.activation(dst[:, i], X[g % 2][:, i * NSEQ * PAD:(i + 1) * NSEQ * PAD].rearrange("p (b r) -> p b r", r=PAD), ACT.Copy)
                ins.then_inc(s_kept, 1)

            def d_hi(g):
                act.wait_ge(d_ok, g + 1)
                act.activation(a_hi[:, 4 * g:4 * g + 4, :], dtmp[:, :, :], ACT.Copy).then_inc(d_hi_ok, 1)

            def keep_new_pool(g):
                act.wait_ge(np_turned, g + 1)
                if g > 1:
                    act.wait_ge(rows_out[g % 2], 16)
                act.activation(ur_p[:, g % 2, :], X[0][:, :], ACT.Copy).then_inc(np_kept, 1)
                act.activation(ur_s[0:NS, g * NC:(g + 1) * NC], X[1][0:NS, :], ACT.Copy).then_inc(np_kept, 1)

            def op_split(j, k, scale):
                act.activation(op_hi[:, k, :], hT[:, k, :], ACT.Copy, scale=scale).then_inc(op_hi_ok, 1)

            d_hi(0)
            d_hi(1)
            for g in range(GROUPS):
                for n in (2 * g + LEAD, 2 * g + LEAD + 1):
                    split_pool(n) if n < 8 else split(0, n - 8)
                keep_new_pool(g)
                if g + 2 < GROUPS:
                    d_hi(g + 2)
            act.wait_ge(np_kept, 8)
            act.wait_ge(outs, 16 * (1 + NSEQ))
            act.wait_ge(d_lo_ok, 4)
            for k in range(KT):
                act.wait_ge(evicted, k + 1)
                op_split(0, k, vec(V_FFN + k))

            def hidden(s, first, k0):
                def after(m):
                    act.wait_ge(evicted, tiles_out(s, m))
                    act.activation(a_hi[:, bass.ds(k0 + m, 1), :], relu[:, m:m + 1], ACT.Square).then_inc(a_hi_ok, 1)
                return after

            def norm_op(s, j, col):
                def after(m):
                    act.wait_ge(evicted, tiles_out(s, m))
                    op_split(j, (s % 4) * MT + m, vec(col + (s % 4) * MT + m))
                return after

            def ffn(layer, s0, rj):
                f0 = KT * SLICES * layer
                slab(s0, hidden(s0, f0, 0), {6: lambda: root(rj, Rb[:, :], rv[:, :])})
                with act.Fori(1, MT) as j:
                    slab(s0 + j, hidden(s0 + j, f0 + j * MT, j * MT))
                with act.Fori(0, MT) as j:
                    slab(s0 + 4 + j)
                with act.Fori(1, SLICES - 1) as sl:
                    with act.Fori(0, MT) as j:
                        slab(s0 + sl * 8 + j, hidden(s0 + sl * 8 + j, f0 + sl * KT + j * MT, j * MT))
                    with act.Fori(0, MT) as j:
                        slab(s0 + 4 + sl * 8 + j)
                sl = SLICES - 1
                with act.Fori(0, MT) as j:
                    slab(s0 + sl * 8 + j, hidden(s0 + sl * 8 + j, f0 + sl * KT + j * MT, j * MT))

            ffn(0, S_FFN0, 1)
            for j in range(MT):
                s = S_QKV - MT + j
                slab(s, norm_op(s, 1, V_MIX + KT))
                if j == 0:
                    act.wait_ge(small_in, 48)
                    act.wait_ge(gw_lo_ok, 2)
                    for n, at in enumerate((GP, 64)):
                        act.activation(gw_hi[:, :, at:at + HEADS], gw_raw[:, :, n * HEADS:(n + 1) * HEADS],
                                       ACT.Copy).then_inc(gw_hi_ok, 1)
            slab(S_QKV, None, {6: lambda: root(2, Rb[:, :], rv[:, :])})
            act.wait_ge(gz_ok, 3)
            act.activation(grow[:, :], gz[:, 0, :], ACT.Tanh, scale=1.0 / CAP, bias=bgate[:, 0:1]).then_inc(tanh_ok, 1)
            act.activation(gz[:, 1, :], gz[:, 1, :], ACT.Tanh, scale=1.0 / CAP, bias=bgate[:, 1:2]).then_inc(act_c, 1)
            act.wait_ge(act_c, 1)
            act.activation(gz[:, 1, :], gz[:, 1, :], ACT.Exp, scale=-CAP).then_inc(tanh_ok, 1)
            act.wait_ge(tanh_ok, 2)
            act.activation(scan_p[0][:, P:], gz[:, 1, 0:TP], ACT.Ln, bias=1.0).then_inc(tanh_ok, 1)
            act.activation(scan_s[0][:, :, 4:], gz[:, 1, TP:].rearrange("h (b t) -> h b t", t=TS), ACT.Ln,
                           bias=1.0).then_inc(tanh_ok, 1)
            with act.Fori(1, 8) as j:
                slab(S_QKV + j)
            act.wait_ge(rows_ok, 1)
            act.activation(gates[:, R_E:], gates[:, R_E:], ACT.Exp).then_inc(gates_exp, 1)

            def prep(h, i):
                p = h % 2
                if i < TT:
                    act.wait_ge(filled, FILL["turn", h, i])
                    act.activation(kv[0:ROWS[i], p, i, 0:DV], X[0][0:ROWS[i], :], ACT.Copy).then_inc(drained_a, 1)
                elif i == TT:
                    act.wait_ge(filled, FILL["rows", h, 0])
                    act.activation(EW[:, p, :], X[1][:, 0:BC], ACT.Copy).then_inc(drained_a, 1)
                    act.wait_ge(drained, FILL["rows", h, 0])
                    act.activation(eb[:, 0:384], eb[:, 0:384], ACT.Exp).then_inc(eb_exp, 1)
                    act.activation(eb[0:NS, 384:448], eb[0:NS, 384:448], ACT.Exp).then_inc(eb_exp, 1)

            for i in range(TT + 1):
                prep(0, i)

            def root2(h):
                act.wait_ge(r2_inv, h + 1)
                act.activation(r2b[:, :], r2b[:, :], ACT.Sqrt).then_inc(r2_ok, 1)

            for h in range(HEADS):
                for c in range(CH):
                    n = LEAD + c
                    split(S_O + h, n) if n < CH else split(S_O + h + 1, n - CH)
                    if h + 1 < HEADS and c <= TT:
                        prep(h + 1, c)
                    if h and c == 3:
                        root2(h - 1)
                act.wait_ge(evicted, tiles_out(S_O + h, MT - 1))
                z4 = qkv[:, z_block(h):z_block(h) + 4, :]
                act.activation(z4, z4, ACT.Exp, scale=-1.0).then_inc(ez_ok, 1)
                act.wait_ge(filled, FILL["updp", h, 0])
                act.wait_ge(c_out[2], 16 * c_stores(h, 5))
                act.activation(cst[:, 2, 1, :], X[1][:, :], ACT.Copy).then_inc(drained_a, 1)
            for k in range(KT):
                if k == 12:
                    root2(HEADS - 1)
                act.wait_ge(att_ok, k // 4 + 1)
                act.wait_ge(hss_ok, HEADS)
                act.activation(a_hi[:, k, :], qkv[:, KT + k, :], ACT.Copy).then_inc(att_hi_ok, 1)
            for j in range(MT):
                s = S_OUT + j
                slab(s, norm_op(s, 2, V_FFN + KT))
            ffn(1, S_FFN1, 3)
            for j in range(MT):
                s = S_END - MT + j

                def keep(m, j=j):
                    if m == MT - 1:
                        act.wait_ge(y_turned, j + 1)
                        act.activation(yrow[:, 0, j * NC:(j + 1) * NC], X[0][:, :], ACT.Copy).then_inc(y_kept_a, 1)
                        act.activation(yrow[0:NS, 2, j * NC:(j + 1) * NC], X[2][0:NS, :], ACT.Copy).then_inc(y_kept_a, 1)
                slab(s, keep, last=j == MT - 1)
            root(4, rcol[:, 0:TT], rcol[:, 0:TT])
            act.wait_ge(r_ok, 5)
            act.wait_ge(y_kept_a, 2 * MT)
            act.activation(yrow[:, 0, :], yrow[:, 0, :], ACT.Copy, scale=rcol[:, 0:1]).then_inc(y_done[0], 1)

        @block.vector
        def _(v):
            n_chain = [0]

            def link(ins):
                n_chain[0] += 1
                ins.then_inc(dve, 1)
                v.wait_ge(dve, n_chain[0])

            def lo_of(slot):
                v.tensor_tensor(w_lo[:, slot], w_raw[:, slot], w_hi[:, slot].bitcast(F32), ALU.subtract).then_inc(w_lo_ok, 1)

            def split(s, c):
                v.wait_ge(w_hi_ok, chunk_no(s, c) + 1)
                lo_of(c % RING)

            def split_pool(n):
                v.wait_ge(w_hi_ok, n + 1)
                lo_of(n % RING)

            def slab(s, evict, mid=None, last=False):
                for i in range(CH):
                    c = LEAD + i
                    if c < CH:
                        split(s, c)
                    elif not last:
                        split(s + 1, c - CH)
                    if mid and i in mid:
                        mid[i]()
                for m in range(MT):
                    v.wait_ge(gemm, tile_done(s, m))
                    evict(m)

            def inverse(j, dst, src, n):
                v.tensor_scalar(dst, src, 1.0 / n, EPS, ALU.mult, ALU.add).then_inc(r_inv, 1)
                v.wait_ge(r_inv, 2 * j + 1)
                v.reciprocal(dst, dst).then_inc(r_inv, 1)

            v.wait_ge(consts, 1)
            v.wait_ge(x_sq, TT)
            inverse(0, rcol[:, 0:TT], xcol[:, 0:TT], D)
            v.wait_ge(r_ok, 1)
            for t in range(TT):
                ins = v.tensor_scalar(diag[:, t, :], ident[:, :], rcol[:, t:t + 1], None, ALU.mult)
            link(ins)
            v.wait_ge(vec_turned, 1)
            link(v.tensor_copy(vecs[:, :], X[3][:, T:T + V_ALL]))
            v.wait_ge(r_sum, 1)
            link(v.tensor_copy(Rb[:, :], X[3][:, 0:T]))
            for k in range(KT):
                v.wait_ge(x_kept, k + 1)
                v.scalar_tensor_tensor(out=uext[:, k, PAD:PAD + TP], in0=hT[:, k, 0:TP], scalar=vec(V_MIX + k),
                                       in1=Rb[:, 0:TP], op0=ALU.mult, op1=ALU.mult).then_inc(u_ok, 1)
                dst = uext[:, k, PAD + TP:].rearrange("p (b r) -> p b r", r=SEG)[:, :, PAD:]
                v.scalar_tensor_tensor(out=dst, in0=hT[:, k, TP:].rearrange("p (b t) -> p b t", t=TS), scalar=vec(V_MIX + k),
                                       in1=Rb[:, TP:].rearrange("p (b t) -> p b t", t=TS), op0=ALU.mult,
                                       op1=ALU.mult).then_inc(u_ok, 1)
                if k >= 13:
                    split_pool(k - 13)

            def pooled(g):
                w = 2 << g
                u = uext[:, 4 * g:4 * g + 4, :]
                v.wait_ge(u_ok, 2 * (4 * g + 4))
                v.wait_ge(s_kept, g + 1)
                if g:
                    v.wait_ge(d_lo_ok, g)
                if g < 2:
                    src = u
                    for n in range(g + 1):
                        s = 1 << n
                        dst = (win[0], win[3])[n % 2]
                        link(v.tensor_tensor(dst[:, :, 2 * s - 1:], src[:, :, 2 * s - 1:], src[:, :, s - 1:UX - s], ALU.add))
                        src = dst
                else:
                    v.wait_ge(win_ok, g - 1)
                    src = win[1 + g % 2]
                for i in range(MT):
                    v.scalar_tensor_tensor(out=dtmp[:, i, 0:TP], in0=src[:, i, PAD:PAD + TP], scalar=1.0 / w,
                                           in1=u[:, i, PAD:PAD + TP], op0=ALU.mult, op1=ALU.subtract)
                    seg = lambda a: a[:, i, PAD + TP:].rearrange("p (b r) -> p b r", r=SEG)[:, :, PAD:]
                    ins = v.scalar_tensor_tensor(out=dtmp[:, i, TP:].rearrange("p (b t) -> p b t", t=TS), in0=seg(src),
                                                 scalar=1.0 / w, in1=seg(u), op0=ALU.mult, op1=ALU.subtract)
                link(ins)
                first = dtmp[:, :, 0:w - 1]
                link(v.tensor_tensor(first, src[:, :, PAD:PAD + w - 1], bc(icnt[:, 0:w - 1], [P, MT, w - 1]), ALU.mult))
                v.tensor_tensor(first, first, u[:, :, PAD:PAD + w - 1], ALU.subtract).then_inc(d_ok, 1)
                v.wait_ge(d_hi_ok, g + 1)
                v.tensor_tensor(a_lo[:, 4 * g:4 * g + 4, :], dtmp[:, :, :], a_hi[:, 4 * g:4 * g + 4, :].bitcast(F32),
                                ALU.subtract).then_inc(d_lo_ok, 1)

            def op_split(j, k, col):
                v.wait_ge(op_hi_ok, KT * j + k + 1)
                v.scalar_tensor_tensor(out=op_lo[:, k, :], in0=hT[:, k, :], scalar=vec(col + k),
                                       in1=op_hi[:, k, :].bitcast(F32), op0=ALU.mult, op1=ALU.subtract).then_inc(op_lo_ok, 1)

            pooled(0)
            pooled(1)
            for g in range(GROUPS):
                for n in (2 * g + LEAD, 2 * g + LEAD + 1):
                    split_pool(n) if n < 8 else split(0, n - 8)
                for m in range(MT):
                    k = 4 * g + m
                    v.wait_ge(gemm, pool_tile(g, m))
                    v.scalar_tensor_tensor(out=hT[:, k, :], in0=G[:, m, 0:T], scalar=vec(V_SCALE + k), in1=hT[:, k, :],
                                           op0=ALU.mult, op1=ALU.add).then_inc(evicted, 1)
                if g + 2 < GROUPS:
                    pooled(g + 2)
            for k in range(KT):
                op_split(0, k, V_FFN)

            def hidden(s, first):
                def evict(m):
                    if not (isinstance(first, int) and first == 0):
                        v.wait_ge(a_lo_ok, first + m - 3)
                        v.wait_ge(a_hi_ok, first + m - 3)
                    v.scalar_tensor_tensor(out=relu[:, m], in0=G[:, m, 0:T], scalar=0.0, in1=Rb[:, :], op0=ALU.max,
                                           op1=ALU.mult).then_inc(evicted, 1)
                return evict

            def add(k0):
                def evict(m):
                    h = hT[:, bass.ds(k0 + m, 1), :]
                    v.tensor_tensor(h, G[:, m:m + 1, 0:T], h, ALU.add).then_inc(evicted, 1)
                return evict

            def add_norm(s, j, col):
                k0 = (s % 4) * MT

                def evict(m):
                    h = hT[:, k0 + m, :]
                    v.tensor_tensor(h, G[:, m, 0:T], h, ALU.add).then_inc(evicted, 1)
                    if m:
                        op_split(j, k0 + m - 1, col)
                    if m == MT - 1:
                        op_split(j, k0 + m, col)
                return evict

            def ffn(layer, s0, rj):
                f0 = KT * SLICES * layer

                def norm():
                    v.wait_ge(r_sum, rj + 1)
                    inverse(rj, rv[:, :], X[3][:, 0:T], D)

                def ready():
                    v.wait_ge(r_ok, rj + 1)

                slab(s0, hidden(s0, f0), {5: norm, 7: ready})
                with v.Fori(1, MT) as j:
                    slab(s0 + j, hidden(s0 + j, f0 + j * MT))
                with v.Fori(0, MT) as j:
                    slab(s0 + 4 + j, add(j * MT))
                with v.Fori(1, SLICES - 1) as sl:
                    with v.Fori(0, MT) as j:
                        slab(s0 + sl * 8 + j, hidden(s0 + sl * 8 + j, f0 + sl * KT + j * MT))
                    with v.Fori(0, MT) as j:
                        slab(s0 + 4 + sl * 8 + j, add(j * MT))
                sl = SLICES - 1
                with v.Fori(0, MT) as j:
                    slab(s0 + sl * 8 + j, hidden(s0 + sl * 8 + j, f0 + sl * KT + j * MT))

            ffn(0, S_FFN0, 1)
            for j in range(MT):
                s = S_QKV - MT + j
                slab(s, add_norm(s, 1, V_MIX + KT))

            def proj(pos):
                def evict(m):
                    v.tensor_tensor(qkv[:, bass.ds(pos(m), 1), :], G[:, m:m + 1, 0:T], bc(Rb[:, :], [P, 1, T]),
                                    ALU.mult).then_inc(evicted, 1)
                return evict

            q_pos = lambda j: lambda m: j * 8 + (4 * (m // 2) + m % 2)
            k_pos = lambda j: lambda m: j * 8 + (4 * (m // 2) + 2 + m % 2)

            def norm():
                v.wait_ge(r_sum, 3)
                inverse(2, rv[:, :], X[3][:, 0:T], D)

            def gate_rows():
                v.wait_ge(small_in, 32)
                v.tensor_scalar(bgate[:, :], bgate[:, :], 1.0 / CAP, None, ALU.mult).then_inc(gz_ok, 1)
                v.wait_ge(gates_sum, 1)
                v.wait_ge(r_ok, 3)
                v.tensor_tensor(gz[:, 0, :], X[0][GP:GP + HEADS, 0:T], Rb[GP:GP + HEADS, :], ALU.mult).then_inc(gz_ok, 1)
                v.tensor_tensor(gz[:, 1, :], X[0][64:64 + HEADS, 0:T], Rb[64:64 + HEADS, :], ALU.mult).then_inc(gz_ok, 1)

            slab(S_QKV, proj(q_pos(0)), {5: norm, 7: gate_rows})
            slab(S_QKV + 1, proj(q_pos(1)))
            with v.Fori(0, 2) as j:
                slab(S_QKV + 2 + j, proj(k_pos(j)))
            v.wait_ge(g_ok, 1)
            scan(v, link, ALU.max)
            v.tensor_scalar(mrow[:, 0:TP], scan_p[0][:, P:], 0.0, None, ALU.max).then_inc(m_ok, 1)
            v.tensor_tensor(seqs(mrow), scan_s[1][:, :, 4:], m0[:, :].unsqueeze(2).broadcast_to([HEADS, NSEQ, TS]),
                            ALU.max).then_inc(m_ok, 1)
            with v.Fori(0, 4) as j:
                slab(S_QKV + 4 + j, proj(lambda m: j * MT + (KT + m)))

            v.wait_ge(filled, FILL["cols", 0, 0])
            v.tensor_copy(cols[:, 0:4, :], X[0][:, 0:16].rearrange("p (a h) -> p a h", h=HEADS))
            v.tensor_copy(cols[0:NS, 4:6, :], X[0][0:NS, 16:24].rearrange("p (a h) -> p a h", h=HEADS))
            v.tensor_copy(dect[:, :], X[1][0:1 + NSEQ, 0:HEADS]).then_inc(drained, 1)
            v.wait_ge(drained, FILL["cols", 0, 0])

            def prep(h, i):
                p = h % 2
                if i < TT:
                    v.wait_ge(filled, FILL["turn", h, i])
                    v.tensor_copy(kv[0:ROWS[i], p, i, DV:], X[1][0:ROWS[i], 0:DK]).then_inc(drained, 1)
                elif i == TT:
                    v.wait_ge(filled, FILL["rows", h, 0])
                    if h:
                        v.wait_ge(prep_ok, h)
                    negm = X[0]
                    v.scalar_tensor_tensor(out=eb[:, 0:P], in0=negm[:, 0:P], scalar=cols[:, 0, h:h + 1], in1=causal[:, :],
                                           op0=ALU.add, op1=ALU.add)
                    v.tensor_scalar(eb[:, P:TP], negm[:, P:TP], cols[:, 0, h:h + 1], None, ALU.add)
                    v.scalar_tensor_tensor(out=eb[:, TP:384], in0=negm[:, P:TP], scalar=cols[:, 2, h:h + 1],
                                           in1=causal[:, :], op0=ALU.add, op1=ALU.add)
                    v.scalar_tensor_tensor(out=eb[0:NS, 384:448], in0=negm[0:NS, TP:T], scalar=cols[0:NS, 4, h:h + 1],
                                           in1=causal_s[0:NS, :], op0=ALU.add, op1=ALU.add).then_inc(drained, 1)
                else:
                    v.wait_ge(filled, FILL["score", h, 0])
                    v.wait_ge(eb_exp, 2 * h + 2)
                    v.scalar_tensor_tensor(out=ST[:, p, 0:384], in0=X[0][:, 0:384], scalar=QSCALE, in1=eb[:, 0:384],
                                           op0=ALU.mult, op1=ALU.mult)
                    v.scalar_tensor_tensor(out=ST[0:NS, p, 384:448], in0=X[0][0:NS, 384:448], scalar=QSCALE,
                                           in1=eb[0:NS, 384:448], op0=ALU.mult, op1=ALU.mult)
                    v.tensor_copy(nts[:, :], X[1][:, 0:18]).then_inc(drained, 1)
                    v.wait_ge(drained_a, ACT_FILL["rows", h, 0])
                    for t in range(2):
                        ins = v.scalar_tensor_tensor(out=qw[:, p, t, :], in0=qkv[:, head_block(h) + t, TP:T], scalar=QSCALE,
                                                     in1=EW[:, p, T:T + NS], op0=ALU.mult, op1=ALU.mult)
                    link(ins)
                    v.wait_ge(drained, FILL["score", h, 0])
                    for t in range(2):
                        ins = v.tensor_tensor(qn[:, p, t, :].rearrange("p (b t) -> p b t", t=TS),
                                              qw[:, p, t, :].rearrange("p (b t) -> p b t", t=TS),
                                              nts[:, 9 * t + 1:9 * t + 9].unsqueeze(2).broadcast_to([P, NSEQ, TS]), ALU.mult)
                    ins.then_inc(prep_ok, 1)

            for i in range(TT + 2):
                prep(0, i)

            def mean_square(h):
                v.wait_ge(x3_filled, X3_USES[f"ms{h}"])
                v.tensor_scalar(r2b[:, :], X[3][:, 0:T], 1.0 / DV, EPS, ALU.mult, ALU.add).then_inc(x3_read, 1)
                v.wait_ge(x3_read, X3_USES[f"ms{h}"])
                v.reciprocal(r2b[:, :], r2b[:, :]).then_inc(r2_inv, 1)

            def gated(h):
                z4 = qkv[:, z_block(h):z_block(h) + 4, :]
                v.wait_ge(ez1_ok, h + 1)
                link(v.reciprocal(z4, z4))
                v.wait_ge(r2_ok, h + 1)
                for i in range(4):
                    ins = v.scalar_tensor_tensor(out=att(h)[:, i], in0=att(h)[:, i], scalar=vec(V_HEAD + 4 * h + i),
                                                 in1=r2b[:, :], op0=ALU.mult, op1=ALU.mult)
                link(ins)
                v.tensor_tensor(att(h), att(h), z4, ALU.mult).then_inc(att_ok, 1)

            def a_lo_of(k):
                v.wait_ge(att_hi_ok, k + 1)
                v.tensor_tensor(a_lo[:, k, :], qkv[:, KT + k, :], a_hi[:, k, :].bitcast(F32), ALU.subtract).then_inc(att_lo_ok, 1)

            for h in range(HEADS):
                p = h % 2
                v.wait_ge(x3_filled, X3_USES[f"den{h}"])
                v.wait_ge(drained_a, ACT_FILL["rows", h, 0])
                if h:
                    v.wait_ge(att_s, h)
                link(v.scalar_tensor_tensor(out=rden[:, :], in0=X[3][:, 0:T], scalar=-1.0, in1=EW[:, p, 0:T],
                                            op0=ALU.mult, op1=ALU.max))
                v.tensor_tensor(rden[:, :], X[3][:, 0:T], rden[:, :], ALU.max).then_inc(x3_read, 1)
                v.wait_ge(x3_read, X3_USES[f"den{h}"])
                link(v.reciprocal(rden[:, :], rden[:, :]))
                v.wait_ge(filled, FILL["num", h, 0])
                for i in range(2):
                    ins = v.tensor_tensor(att(h)[:, 2 * i:2 * i + 2, 0:TP], X[i][:, :].rearrange("p (a t) -> p a t", t=TP),
                                          bc(rden[:, 0:TP], [P, 2, TP]), ALU.mult)
                ins.then_inc(drained, 1)
                for c in range(CH):
                    n = LEAD + c
                    split(S_O + h, n) if n < CH else split(S_O + h + 1, n - CH)
                    if h + 1 < HEADS and c <= TT + 1:
                        prep(h + 1, c)
                    if h and c == 2:
                        mean_square(h - 1)
                    if h and c == 4:
                        gated(h - 1)
                    if c == 5:
                        v.wait_ge(filled, FILL["n", h, 0])
                        nh = nrow[:, h * DK:(h + 1) * DK]
                        v.scalar_tensor_tensor(out=nh, in0=nh, scalar=dect[:, h:h + 1], in1=X[0][0:1 + NSEQ, 0:DK],
                                               op0=ALU.mult, op1=ALU.add).then_inc(drained, 1)
                    if c == CH - 1:
                        for m in range(MT):
                            v.wait_ge(gemm, tile_done(S_O + h, m))
                            v.tensor_tensor(qkv[:, z_block(h) + m, :], G[:, m, 0:T], Rb[:, :], ALU.mult).then_inc(evicted, 1)
                    v.wait_ge(filled, FILL["upd", h, c])
                    for t in range(2):
                        st = cst[:, c_slot(c), t, :]
                        ins = v.scalar_tensor_tensor(out=st, in0=st, scalar=EW[:, p, T + NS + 1 + c:T + NS + 2 + c],
                                                     in1=X[t][:, :], op0=ALU.mult, op1=ALU.add)
                    ins.then_inc(drained, 1)
                v.wait_ge(x2_filled, h + 1)
                v.tensor_tensor(att(h)[:, :, TP:T], X[2][:, 0:4 * NS].rearrange("p (a t) -> p a t", t=NS),
                                bc(rden[:, TP:T], [P, 4, NS]), ALU.mult).then_inc(att_s, 1)
                v.wait_ge(filled, FILL["updp", h, 0])
                v.wait_ge(c_out[2], 16 * c_stores(h, 5))
                v.tensor_copy(cst[:, 2, 0, :], X[0][:, :]).then_inc(drained, 1)
            for k in range(12):
                a_lo_of(k)
            mean_square(HEADS - 1)
            gated(HEADS - 1)
            for k in range(12, KT):
                a_lo_of(k)
            for j in range(MT):
                s = S_OUT + j
                slab(s, add_norm(s, 2, V_FFN + KT))
            for i in range(3):
                v.wait_ge(c_out[i], 16 * 3 * HEADS)
            v.wait_ge(outs, 16 * (1 + NSEQ + 2 + 2))
            ffn(1, S_FFN1, 3)
            for j in range(MT):
                s = S_END - MT + j

                def evict(m, j=j):
                    k = j * MT + m
                    h = hT[:, k, :]
                    v.tensor_tensor(h, G[:, m, 0:T], h, ALU.add).then_inc(evicted, 1)
                    v.wait_ge(evicted, tiles_out(S_END - MT + j, m))
                    v.tensor_scalar(yT[:, k, :], h, vec(V_FIN + k), None, ALU.mult).then_inc(y_ok, 1)
                    if m == MT - 1:
                        v.wait_ge(y_turned, j + 1)
                        v.tensor_copy(yrow[:, 1, j * NC:(j + 1) * NC], X[1][:, :]).then_inc(y_kept_d, 1)
                slab(s, evict, last=j == MT - 1)
            v.wait_ge(r_sum, 5)
            v.tensor_scalar(rcol[:, 0:2], X[3][:, 0:2], 1.0 / D, EPS, ALU.mult, ALU.add)
            v.tensor_scalar(rcol[0:NS, 2:3], X[3][0:NS, 2:3], 1.0 / D, EPS, ALU.mult, ALU.add).then_inc(r_inv, 1)
            v.wait_ge(r_inv, 9)
            v.reciprocal(rcol[:, 0:TT], rcol[:, 0:TT]).then_inc(r_inv, 1)
            v.wait_ge(r_ok, 5)
            v.wait_ge(y_kept_d, MT)
            v.tensor_scalar(yrow[:, 1, :], yrow[:, 1, :], rcol[:, 1:2], None, ALU.mult).then_inc(y_done[1], 1)

        @block.tensor
        def _(pe):
            def turn(out, in_, rows=P):
                if in_.shape[-1] == P:
                    return pe.transpose(out, in_, ident[0:rows, 0:rows])
                return pe.matmul(out, in_, ident[0:rows, 0:rows], start=True, stop=True, skip_group_check=True)

            def chunk(slot, hi, lo, k0, first, last, tile=None, ready=None):
                for m in range(MT):
                    if tile:
                        tile(m)
                    for t in range(CK):
                        k = k0 + t
                        if ready and m == 0:
                            ready(k)
                        w = slice(m * P, (m + 1) * P)
                        pe.matmul(G[:, m, 0:T], w_hi[:, slot, t, w], hi[:, k, :], start=first and t == 0, stop=False)
                        pe.matmul(G[:, m, 0:T], w_hi[:, slot, t, w], lo[:, k, :], start=False, stop=False)
                        ins = pe.matmul(G[:, m, 0:T], w_lo[:, slot, t, w], hi[:, k, :], start=False,
                                        stop=last and t == CK - 1)
                    if last:
                        ins.then_inc(gemm, 1)
                if not last:
                    ins.then_inc(gemm, 1)

            def slab(s, hi, lo, ready=None, mid=None):
                for c in range(CH):
                    pe.wait_ge(w_lo_ok, chunk_no(s, c) + 1)
                    free = (lambda m: pe.wait_ge(evicted, s * MT + (MT * (GROUPS - 1) + m + 1))) if c == 0 else None
                    chunk(c % RING, hi, lo, CK * c, c == 0, c == CH - 1, free, ready)
                    if mid:
                        mid(c)

            pe.wait_ge(consts, 1)
            pe.wait_ge(vecs_in, 16 * 5)
            pe.transpose(X[3][:, T:T + V_ALL], vrow[0:V_ALL, :], ident[0:V_ALL, 0:V_ALL]).then_inc(vec_turned, 1)
            for t in range(TT):
                pe.wait_ge(x_in[t], 16)
            for k in range(KT):
                if k >= 3:
                    pe.wait_ge(x_kept, k - 2)
                for t in range(TT):
                    ins = pe.transpose(X[k % 3][:, t * P:t * P + ROWS[t]], xrow[0:ROWS[t], t, k * P:(k + 1) * P],
                                       ident[0:ROWS[t], 0:ROWS[t]])
                ins.then_inc(x_turned, 1)
                if k == 4:
                    pe.wait_ge(dve, 2)
                    for t in range(TT):
                        ins = pe.matmul(X[3][:, t * P:t * P + ROWS[t]], ones[0:ROWS[t], :], diag[0:ROWS[t], t, 0:ROWS[t]],
                                        start=t == 0, stop=True, skip_group_check=True)
                    ins.then_inc(r_sum, 1)
            pe.wait_ge(state_in, 16)
            pe.wait_ge(x_kept, KT)
            for g in range(GROUPS):
                if g > 1:
                    pe.wait_ge(s_kept, g - 1)
                for i in range(4):
                    ins = pe.transpose(X[g % 2][:, i * NSEQ * PAD:(i + 1) * NSEQ * PAD],
                                       srow[0:NSEQ * PAD, (4 * g + i) * P:(4 * g + i + 1) * P],
                                       ident[0:NSEQ * PAD, 0:NSEQ * PAD])
                ins.then_inc(s_turned, 1)
            pe.wait_ge(s_kept, GROUPS)

            for g in range(GROUPS):
                pe.wait_ge(d_lo_ok, g + 1)
                for c in range(2):
                    n = 2 * g + c
                    pe.wait_ge(w_lo_ok, n + 1)
                    free = (lambda m: pe.wait_ge(evicted, 4 * (g - 1) + m + 1)) if g and c == 0 else None
                    chunk(n % RING, a_hi, a_lo, 4 * g + CK * c, c == 0, c == 1, free)
                if g:
                    pe.wait_ge(np_kept, 2 * g)
                pe.wait_ge(us_ok, g + 1)
                for i in range(4):
                    k = 4 * g + i
                    pe.transpose(X[0][:, i * P:(i + 1) * P], uext[:, k, PAD + TP - P:PAD + TP], ident[:, :])
                    ins = pe.matmul(X[1][0:NS, i * P:(i + 1) * P], us[:, k, :], ident[:, :], start=True, stop=True,
                                    skip_group_check=True)
                ins.then_inc(np_turned, 1)

            def norm_sum(j):
                pe.wait_ge(ssq_ok, KT * j + KT)
                pe.matmul(X[3][:, 0:T], ones[:, :], acc[:, :], start=True, stop=True).then_inc(r_sum, 1)

            def op_ready(j):
                return lambda k: pe.wait_ge(op_lo_ok, KT * j + k + 1)

            def down_ready(first):
                return lambda k: pe.wait_ge(a_lo_ok, first + (k + 1))

            def ffn(layer, s0, j_op):
                f0 = KT * SLICES * layer
                slab(s0, op_hi, op_lo, op_ready(j_op), lambda c: norm_sum(j_op) if c == 4 else None)
                with pe.Fori(1, MT) as j:
                    slab(s0 + j, op_hi, op_lo)
                with pe.Fori(0, MT) as j:
                    slab(s0 + 4 + j, a_hi, a_lo, down_ready(f0))
                with pe.Fori(1, SLICES - 1) as sl:
                    with pe.Fori(0, MT) as j:
                        slab(s0 + sl * 8 + j, op_hi, op_lo)
                    with pe.Fori(0, MT) as j:
                        slab(s0 + 4 + sl * 8 + j, a_hi, a_lo, down_ready(f0 + sl * KT))
                sl = SLICES - 1
                with pe.Fori(0, MT) as j:
                    slab(s0 + sl * 8 + j, op_hi, op_lo)

            ffn(0, S_FFN0, 0)
            with pe.Fori(0, MT) as j:
                slab(S_QKV - MT + j, a_hi, a_lo, down_ready(KT * (SLICES - 1)))

            pe.wait_ge(gw_lo_ok, 4)
            for k in range(KT):
                pe.wait_ge(op_lo_ok, KT + k + 1)
                for w, x in ((gw_hi, op_hi), (gw_hi, op_lo), (gw_lo, op_hi)):
                    ins = pe.matmul(X[0][0:68, 0:T], w[:, k, :], x[:, k, :], start=k == 0 and w is gw_hi and x is op_hi,
                                    stop=k == KT - 1 and w is gw_lo)
            ins.then_inc(gates_sum, 1)
            slab(S_QKV, op_hi, op_lo, None, lambda c: norm_sum(1) if c == 4 else None)
            with pe.Fori(1, 8) as j:
                slab(S_QKV + j, op_hi, op_lo)

            order = fill_list()

            def bank_free(f):
                n = order.index(f)
                if n:
                    pe.wait_ge(drained, n)
                    for e in reversed(order[:n]):
                        if e in ACT_FILL:
                            pe.wait_ge(drained_a, ACT_FILL[e])
                            break

            pe.wait_ge(gates_exp, 1)
            pe.wait_ge(gz_ok, 3)
            for t in range(TT):
                for n, row in enumerate((grow[:, tok(t)], gates[:, R_WK + t * P:R_WK + t * P + ROWS[t]])):
                    at = 4 * (2 * t + n)
                    pe.matmul(X[0][0:ROWS[t], at:at + HEADS], row, ident[GP:GP + HEADS, GP:GP + HEADS], start=at == 0, stop=True,
                              skip_group_check=True)
            pe.matmul(X[1][0:1 + NSEQ, 0:HEADS], gates[:, R_DEC:R_DEC + 1 + NSEQ], ident[GP:GP + HEADS, GP:GP + HEADS],
                      start=True, stop=True).then_inc(filled, 1)

            def prep(h, i):
                q = head_block(h)
                if i < TT:
                    bank_free(("turn", h, i))
                    pe.wait_ge(evicted, tiles_out(S_QKV + 7, MT - 1))
                    for n in range(4):
                        turn(X[0][0:ROWS[i], n * P:(n + 1) * P], qkv[:, KT + 4 * h + n, tok(i)])
                    for n in range(2):
                        ins = turn(X[1][0:ROWS[i], n * P:(n + 1) * P], qkv[:, q + 2 + n, tok(i)])
                elif i == TT:
                    bank_free(("rows", h, 0))
                    pe.matmul(X[0][:, 0:T], sel[:, h, :], gates[:, R_NEGM:R_E], start=True, stop=True)
                    ins = pe.matmul(X[1][:, 0:BC], sel[:, h, :], gates[:, R_E:R_WK], start=True, stop=True)
                else:
                    bank_free(("score", h, 0))
                    first = True
                    for rows, a, b, at in ((P, 0, TP, 0), (P, P, TP, TP), (NS, TP, T, 384)):
                        for t in range(2):
                            pe.matmul(X[0][0:rows, at:at + b - a], qkv[:, q + 2 + t, a:a + rows], qkv[:, q + t, a:b],
                                      start=first, stop=t == 1, skip_group_check=True)
                            first = False
                    pe.wait_ge(small_in, 16 * 4)
                    for t in range(2):
                        ins = pe.matmul(X[1][:, 9 * t:9 * t + 9], nrow[:, h * DK + t * P:h * DK + (t + 1) * P],
                                        ident[0:9, 0:9], start=t == 0, stop=True, skip_group_check=True)
                ins.then_inc(filled, 1)

            for i in range(TT + 2):
                prep(0, i)

            def head_norm_sum(h):
                use = X3_USES[f"ms{h}"]
                pe.wait_ge(hss_ok, h + 1)
                pe.wait_ge(x3_read, use - 1)
                pe.matmul(X[3][:, 0:T], ones[:, :], hss[:, :], start=True, stop=True).then_inc(x3_filled, 1)

            for h in range(HEADS):
                p = h % 2
                pe.wait_ge(prep_ok, h + 1)
                if h:
                    pe.wait_ge(x3_read, X3_USES[f"den{h}"] - 1)
                pe.matmul(X[3][:, 0:TP], ones[:, :], ST[:, p, 0:TP], start=True, stop=False, skip_group_check=True)
                pe.matmul(X[3][:, P:TP], ones[:, :], ST[:, p, TP:384], start=False, stop=False, skip_group_check=True)
                pe.matmul(X[3][:, TP:T], ones[0:NS, :], ST[0:NS, p, 384:448], start=False, stop=False, skip_group_check=True)
                for t in range(2):
                    ins = pe.matmul(X[3][:, TP:T], ones[:, :], qn[:, p, t, :], start=False, stop=t == 1, skip_group_check=True)
                ins.then_inc(x3_filled, 1)
                bank_free(("num", h, 0))
                for n in range(4):
                    w = slice(n * P, (n + 1) * P)
                    at = (n % 2) * TP
                    pe.matmul(X[n // 2][:, at:at + TP], kv[:, p, 0, w], ST[:, p, 0:TP], start=n % 2 == 0, stop=False,
                              skip_group_check=True)
                    ins = pe.matmul(X[n // 2][:, at + P:at + TP], kv[:, p, 1, w], ST[:, p, TP:384], start=False, stop=True,
                                    skip_group_check=True)
                ins.then_inc(filled, 1)
                if h:
                    pe.wait_ge(att_s, h)
                for n in range(4):
                    pe.matmul(X[2][:, n * NS:(n + 1) * NS], kv[0:NS, p, 2, n * P:(n + 1) * P], ST[0:NS, p, 384:448],
                              start=n == 0, stop=False, skip_group_check=True)
                for c in range(CH):
                    s = S_O + h
                    pe.wait_ge(w_lo_ok, chunk_no(s, c) + 1)
                    free = (lambda m: pe.wait_ge(evicted, tiles_out(s - 1, m))) if c == 0 else None
                    chunk(c % RING, op_hi, op_lo, CK * c, c == 0, c == CH - 1, free)
                    if h and c == 1:
                        head_norm_sum(h - 1)
                    if h + 1 < HEADS and c <= TT + 1:
                        prep(h + 1, c)
                    if c == 5:
                        bank_free(("n", h, 0))
                        pe.wait_ge(kw_ok, 10 * h + 1)
                        for t in range(TT):
                            ins = pe.matmul(X[0][0:1 + NSEQ, 0:DK], wkm[0:ROWS[t], t, :], kv[0:ROWS[t], p, t, DV:],
                                            start=t == 0, stop=t == TT - 1)
                        ins.then_inc(filled, 1)
                    pe.wait_ge(c_in[c_slot(c)], 16 * c_loads(h, c))
                    for n in range(4):
                        for t in range(2):
                            at = n * NS + c * TS
                            ins = pe.matmul(X[2][:, at:at + TS], cst[:, c_slot(c), t, n * P:(n + 1) * P],
                                            qw[:, p, t, c * TS:(c + 1) * TS], start=False, stop=t == 1, skip_group_check=True)
                    if c == CH - 1:
                        ins.then_inc(x2_filled, 1)
                    bank_free(("upd", h, c))
                    pe.wait_ge(kw_ok, 10 * h + 3 + c)
                    for t in range(2):
                        ins = pe.matmul(X[t][:, :], kwb[0:NS, c % 2, t * P:(t + 1) * P], kv[0:NS, p, 2, 0:DV],
                                        start=True, stop=True)
                    ins.then_inc(filled, 1)
                bank_free(("updp", h, 0))
                for t in range(2):
                    for i in range(2):
                        ins = pe.matmul(X[t][:, :], kwp[:, i, t * P:(t + 1) * P], kv[:, p, i, 0:DV], start=i == 0, stop=i == 1)
                ins.then_inc(filled, 1)
            head_norm_sum(HEADS - 1)
            slab(S_OUT, a_hi, a_lo, lambda k: pe.wait_ge(att_lo_ok, k + 1))
            with pe.Fori(1, MT) as j:
                slab(S_OUT + j, a_hi, a_lo)
            ffn(1, S_FFN1, 2)
            for j in range(MT):
                slab(S_END - MT + j, a_hi, a_lo, down_ready(KT * (2 * SLICES - 1)))
                pe.wait_ge(y_ok, (j + 1) * MT)
                if j:
                    pe.wait_ge(y_kept_a, 2 * j)
                    pe.wait_ge(y_kept_d, j)
                for t in range(TT):
                    for m in range(MT):
                        ins = turn(X[t][0:ROWS[t], m * P:(m + 1) * P], yT[:, j * MT + m, tok(t)])
                ins.then_inc(y_turned, 1)
            pe.wait_ge(ssq_ok, 4 * KT)
            for t in range(TT):
                ins = pe.matmul(X[3][0:ROWS[t], t:t + 1], acc[:, tok(t)], ones[:, 0:1], start=t == 0, stop=True,
                                skip_group_check=True)
            ins.then_inc(r_sum, 1)


_INS = ["x_prompt", "x_sample", "state_pool", "state_mlstm_C", "state_mlstm_n", "state_mlstm_m", "norm_mix",
        "norm_ffn", "norm_final", "pool_w", "pool_scale", "mlstm_w_in", "mlstm_b_gate", "mlstm_head_norm",
        "mlstm_w_out", "ffn_w_up", "ffn_w_down"]
_OUTS = [("y_prompt", (1, TP, D)), ("y_sample", (NSEQ, TS, D)), ("pool_prompt", (1, 1, PAD, D)),
         ("pool_sample", (1, NSEQ, PAD, D)), ("C_prompt", (1, 1, HEADS, DK, DV)), ("n_prompt", (1, 1, HEADS, DK)),
         ("m_prompt", (1, 1, HEADS)), ("C_sample", (1, NSEQ, HEADS, DK, DV)), ("n_sample", (1, NSEQ, HEADS, DK)),
         ("m_sample", (1, NSEQ, HEADS))]


def kernel(**inputs):
    import concourse.bacc as bacc
    from concourse.bass_utils import run_bass_kernel_spmd

    nc = bacc.Bacc("TRN2", target_bir_lowering=False, num_devices=1)
    arrays, ins, outs = {}, {}, {}
    for name in _INS:
        a = np.ascontiguousarray(inputs[name])
        arrays[f"in_{name}"] = a
        ins[name] = nc.dram_tensor(f"in_{name}", a.shape, F32, kind="ExternalInput").ap()
    for name, shape in _OUTS:
        outs[name] = nc.dram_tensor(f"out_{name}", shape, F32, kind="ExternalOutput").ap()
    build(nc, ins, outs)
    r = run_bass_kernel_spmd(nc, [arrays], core_ids=[0])
    return tuple(r.results[0][f"out_{name}"] for name, _ in _OUTS)
```

```python
from contextlib import ExitStack

import numpy as np

import concourse.bass as bass
from concourse import mybir

F32 = mybir.dt.float32
F32R = mybir.dt.float32r
ACT = mybir.ActivationFunctionType
ALU = mybir.AluOpType

P = 128
D = 2048
KT = D // P
TP, NSEQ, TS = 256, 8, 8
NS = NSEQ * TS
T = TP + NS
TT = 3
ROWS = (P, P, NS)
EPS = 1e-6

RING = 4
CK = 2
NC = 512
MT = NC // P
CH = KT // CK
LEAD = 3

GROUPS = 4
PAD = 15
SEG = PAD + TS
UX = PAD + TP + NSEQ * SEG

HEADS, DK, DV = 4, 256, 512
QSCALE = DK ** -0.5
CAP = 15.0
NEG = -1e30
GP = 32
D_FF = 4 * D
SLICES = D_FF // D

V_MIX, V_FFN, V_FIN, V_SCALE, V_HEAD, V_ALL = 0, 32, 64, 80, 96, 112

S_FFN0, S_QKV, S_O, S_OUT, S_FFN1, S_END = 0, 32, 40, 44, 48, 80

R_NEGM, R_E, R_WI, R_DEC, R_WK, R_ALL = 0, T, 2 * T, 2 * T + NS, 2 * T + NS + 16, 3 * T + NS + 16
BC = T + NS + 16


def chunk_no(s, c):
    return s * CH + (2 * GROUPS + c)


def used(s, c):
    return s * (CH + MT - 1) + (5 * GROUPS + (c + 1 if c < CH - 1 else CH + MT - 1))


def tile_done(s, m):
    return s * (CH + MT - 1) + (5 * GROUPS + CH + m)


def pool_used(g, c):
    return 5 * g + (1 if c == 0 else 5)


def pool_tile(g, m):
    return 5 * g + 2 + m


def used_before(s, c):
    if c >= RING:
        return used(s, c - RING)
    if isinstance(s, int) and s == 0:
        return pool_used((RING + c) // 2, c % 2)
    return used(s - 1, c + CH - RING)


def tiles_out(s, m):
    return s * MT + (MT * GROUPS + m + 1)


def fill_list():
    prep = lambda h: [("turn", h, t) for t in range(TT)] + [("rows", h, 0), ("score", h, 0)]
    out = [("cols", 0, 0)] + prep(0)
    for h in range(HEADS):
        out += [("num", h, 0), ("updp", h, 0)]
        pieces = prep(h + 1) if h + 1 < HEADS else []
        for b in range(NSEQ):
            if 1 <= b <= len(pieces):
                out.append(pieces[b - 1])
            out.append(("upd", h, b))
    return out


FILL = {f: n + 1 for n, f in enumerate(fill_list())}
ACT_FILL = {f: n + 1 for n, f in enumerate([f for f in fill_list() if f[0] in ("turn", "rows", "updp")])}
X3_USES = {u: n + 1 for n, u in enumerate(["den0", "n0", "den1", "n1", "ms0", "den2", "n2", "ms1", "den3", "n3", "ms2", "ms3"])}


def item(b):
    return 0 if b == "prompt" else b + 1


def c_slot(b):
    return item(b) % 3


def c_loads(h, b):
    return (3 if c_slot(b) else 2) * h + b // 3 + 1


def c_stores(h, b):
    return 3 * h + item(b) // 3 + 1


def bc(ap, shape):
    return ap.unsqueeze(1).broadcast_to(shape)


def build(nc, A, O):
    with ExitStack() as ctx:
        def sb(name, shape, dt=F32, where=ctx):
            return where.enter_context(nc.sbuf_tensor(name, shape, dt))

        def head_rows(name, shape, where=ctx):
            full = sb(name, [GP + HEADS] + shape, F32, where)
            return full[GP:GP + HEADS, :] if len(shape) == 1 else full[GP:GP + HEADS, :, :]

        def sem(name):
            return ctx.enter_context(nc.semaphore(name))

        hT = sb("hT", [P, KT, T])
        w_raw = sb("w_raw", [P, RING, CK, NC])
        w_hi = sb("w_hi", [P, RING, CK, NC], F32R)
        w_lo = sb("w_lo", [P, RING, CK, NC], F32R)
        ident = sb("ident", [P, P])
        ones = sb("ones", [P, P])
        causal = sb("causal", [P, P])
        causal_s = sb("causal_s", [P, NS])
        seqmask = sb("seqmask", [P, TT, 1 + NSEQ])
        sel = head_rows("sel", [HEADS, P])
        icnt = sb("icnt", [P, PAD])
        vrow = sb("vrow", [P, P])
        vecs = sb("vecs", [P, V_ALL])
        Rb = sb("Rb", [P, T])
        rv = sb("rv", [P, T])
        acc = sb("acc", [P, T])
        sqt = sb("sqt", [P, T])
        xcol = sb("xcol", [P, 4])
        rcol = sb("rcol", [P, 4])
        bgate = head_rows("bgate", [2])
        m0 = head_rows("m0", [NSEQ])
        mnew = head_rows("mnew", [1 + NSEQ])

        with ExitStack() as r:
            srow = sb("srow", [P, D], F32, r)
            with ExitStack() as r2:
                xrow = sb("xrow", [P, TT, D], F32, r2)
            win = [sb(f"win{i}", [P, GROUPS, UX], F32, r) for i in range(3)]
            ur_s = sb("ur_s", [P, D], F32, r)
            diag = sb("diag", [P, TT, P], F32, r)
        with ExitStack() as r:
            yT = sb("yT", [P, KT, T], F32, r)
        op_hi = sb("op_hi", [P, KT, T], F32R)
        op_lo = sb("op_lo", [P, KT, T], F32R)

        with ExitStack() as r:
            qkv = sb("qkv", [P, 2 * KT, T], F32, r)
        a_hi = sb("a_hi", [P, KT, T], F32R)
        a_lo = sb("a_lo", [P, KT, T], F32R)

        with ExitStack() as r:
            uext = sb("uext", [P, KT, UX], F32, r)
            win.append(sb("win3", [P, GROUPS, UX], F32, r))
            ur_p = sb("ur_p", [P, 2, NC], F32, r)
            dtmp = sb("dtmp", [P, MT, T], F32, r)
            us = sb("us", [P, KT, NS], F32, r)
        with ExitStack() as r:
            with ExitStack() as r2:
                gw_raw = sb("gw_raw", [P, KT, 2 * HEADS], F32, r2)
                gw_hi = sb("gw_hi", [P, KT, 68], F32R, r2)
                gw_lo = sb("gw_lo", [P, KT, 68], F32R, r2)
            with ExitStack() as r2:
                scan_p = [head_rows(f"scan_p{i}", [P + TP], r2) for i in range(2)]
                scan_s = [head_rows(f"scan_s{i}", [NSEQ, 4 + TS], r2) for i in range(2)]
                pad_ = sb("pad_", [P, 1500], F32, r2)
                grow = head_rows("grow", [T], r2)
                nbrow = head_rows("nbrow", [T], r2)
                mrow = head_rows("mrow", [T], r2)
                gz = head_rows("gz", [2, T], r2)
            pad2 = sb("pad2", [P, 4608], F32, r)
            relu = sb("relu", [P, MT, T], F32, r)
            sq = sb("sq", [P, 2, T], F32, r)
            yrow = sb("yrow", [P, TT, D], F32, r)
        with ExitStack() as r:
            kvp = sb("kvp", [P, 2, DV + DK], F32, r)
            kvs = sb("kvs", [P, 2, DV + DK], F32, r)
            v_hi = sb("v_hi", [P, DV], F32R, r)
            v_lo = sb("v_lo", [P, DV], F32R, r)
            kwb = sb("kwb", [P, 2, DK], F32R, r)
            cst = sb("cst", [P, 3, 2, DV], F32, r)
            ST = sb("ST", [P, 448], F32, r)
            EW = sb("EW", [P, 2, BC], F32, r)
            hs = sb("hs", [P, DV], F32, r)
            eb = hs[:, 0:448]
            qw = sb("qw", [P, 2, NS], F32, r)
            qn = sb("qn", [P, 2, NS], F32, r)
            qwm = sb("qwm", [P, 2, NSEQ * (NS + TS)], F32, r)
            nts = sb("nts", [P, 2 * (1 + NSEQ)], F32, r)
            rden_odd = sb("rden_odd", [P, T], F32, r)
            gates_n = sb("gates_n", [GP + HEADS, R_ALL], F32, r)
            nrow = gates_n[0:1 + NSEQ, 0:HEADS * DK]
            gates = gates_n[GP:GP + HEADS, :]
            cols = sb("cols", [P, 6, HEADS], F32, r)
            dect = sb("dect", [1 + NSEQ, HEADS], F32, r)
        rden, r2b, hss = (rv, rden_odd), sqt, acc

        G = ctx.enter_context(nc.psum_tensor("G", [P, MT, 512], F32))
        X = [ctx.enter_context(nc.psum_tensor(f"X{i}", [P, 512], F32)) for i in range(4)]

        x_in = [sem(f"x_in{t}") for t in range(TT)]
        state_in = sem("state_in")
        vecs_in = sem("vecs_in")
        small_in = sem("small_in")
        w_in = [sem(f"w_in{i}") for i in range(RING)]
        c_in = [sem(f"c_in{i}") for i in range(3)]
        c_out = [sem(f"c_out{i}") for i in range(3)]
        rows_out = [sem(f"rows_out{i}") for i in range(2)]
        outs = sem("outs")
        y_out = sem("y_out")
        consts = sem("consts")
        w_hi_ok = sem("w_hi_ok")
        w_lo_ok = sem("w_lo_ok")
        gemm = sem("gemm")
        evicted = sem("evicted")
        x_sq = sem("x_sq")
        x_turned = sem("x_turned")
        x_kept = sem("x_kept")
        s_turned = sem("s_turned")
        s_kept = sem("s_kept")
        r_sum = sem("r_sum")
        r_inv = sem("r_inv")
        r_ok = sem("r_ok")
        dve = sem("dve_chain")
        pool_c = sem("pool_chain")
        act_c = sem("act_chain")
        vec_turned = sem("vec_turned")
        u_ok = sem("u_ok")
        us_ok = sem("us_ok")
        win_ok = sem("win_ok")
        d_ok = sem("d_ok")
        d_hi_ok = sem("d_hi_ok")
        d_lo_ok = sem("d_lo_ok")
        np_turned = sem("np_turned")
        np_kept = sem("np_kept")
        op_hi_ok = sem("op_hi_ok")
        op_lo_ok = sem("op_lo_ok")
        sq_ok = sem("sq_ok")
        ssq_ok = sem("ssq_ok")
        a_hi_ok = sem("a_hi_ok")
        a_sq_ok = sem("a_sq_ok")
        a_lo_ok = sem("a_lo_ok")
        gw_hi_ok = sem("gw_hi_ok")
        gw_lo_ok = sem("gw_lo_ok")
        gates_sum = sem("gates_sum")
        gz_ok = sem("gz_ok")
        tanh_ok = sem("tanh_ok")
        g_ok = sem("g_ok")
        m_ok = sem("m_ok")
        rows_ok = sem("rows_ok")
        gates_exp = sem("gates_exp")
        filled = sem("filled")
        drained = sem("drained")
        drained_a = sem("drained_a")
        eb_exp = sem("eb_exp")
        prep_ok = sem("prep_ok")
        x3_filled = sem("x3_filled")
        x3_read = sem("x3_read")
        x2_filled = sem("x2_filled")
        att_s = sem("att_s")
        kw_ok = sem("kw_ok")
        hss_ok = sem("hss_ok")
        ez_ok = sem("ez_ok")
        v_hi_ok = sem("v_hi_ok")
        v_lo_ok = sem("v_lo_ok")
        kwb_hi_ok = sem("kwb_hi_ok")
        kwb_ok = sem("kwb_ok")
        qwm_ok = sem("qwm_ok")
        hs_kept = sem("hs_kept")
        x2_turned = sem("x2_turned")
        r2_inv = sem("r2_inv")
        r2_ok = sem("r2_ok")
        att_ok = sem("att_ok")
        att_hi_ok = sem("att_hi_ok")
        att_lo_ok = sem("att_lo_ok")
        y_ok = sem("y_ok")
        y_turned = sem("y_turned")
        y_kept_a = sem("y_kept_a")
        y_kept_d = sem("y_kept_d")
        y_done = [sem(f"y_done{t}") for t in range(TT)]

        w_up = [A["ffn_w_up"][i].rearrange("(c t p) n -> c p t n", t=CK, p=P) for i in range(2)]
        w_down = [A["ffn_w_down"][i].rearrange("(s c t p) n -> s c p t n", c=CH, t=CK, p=P) for i in range(2)]
        w_qkvo = A["mlstm_w_in"][0].rearrange("(c t p) n -> c p t n", t=CK, p=P)
        w_out = A["mlstm_w_out"][0].rearrange("(c t p) n -> c p t n", t=CK, p=P)
        w_pool = A["pool_w"][0].rearrange("g (c t p) n -> g c p t n", t=CK, p=P)
        w_gate = A["mlstm_w_in"][0].rearrange("(k p) n -> p k n", p=P)[:, :, 2 * HEADS * DK + 2 * D:]
        c_dram = A["state_mlstm_C"][0].rearrange("b h (t p) n -> b h p t n", p=P)
        c_new = O["C_sample"][0].rearrange("b h (t p) n -> b h p t n", p=P)
        c_new_p = O["C_prompt"][0, 0].rearrange("h (t p) n -> h p t n", p=P)

        def vec(n):
            return vecs[:, n:n + 1]

        def tok(t):
            return slice(t * P, t * P + ROWS[t])

        def head_block(h):
            return 4 * h

        def z_block(h):
            return 0 if h < 3 else 12

        def sq_block(h):
            return 4 if h < 3 else 8

        def att(h):
            return qkv[:, KT + 4 * h:KT + 4 * h + 4, :]

        def seqs(row, a=0):
            return row[:, a + TP:a + T].rearrange("h (b t) -> h b t", t=TS)

        def scan(eng, link, op):
            for n in range(8):
                w, a, b = 1 << n, scan_p[n % 2], scan_p[1 - n % 2]
                link(eng.tensor_tensor(b[:, P:], a[:, P:], a[:, P - w:P + TP - w], op))
            for n in range(3):
                w, a, b = 1 << n, scan_s[n % 2], scan_s[1 - n % 2]
                link(eng.tensor_tensor(b[:, :, 4:], a[:, :, 4:], a[:, :, 4 - w:4 + TS - w], op))

        block = ctx.enter_context(nc.Block())

        @block.sync
        def _(sp):
            for t in range(TT):
                src = A["x_prompt"][0, t * P:(t + 1) * P, :] if t < 2 else A["x_sample"].rearrange("b t d -> (b t) d")
                sp.dma_start(xrow[0:ROWS[t], t, :], src).then_inc(x_in[t], 16)
            sp.dma_start(srow[0:NSEQ * PAD, :], A["state_pool"][0].rearrange("b r d -> (b r) d")).then_inc(state_in, 16)

            def load(s, c, src):
                sp.wait_ge(w_lo_ok, chunk_no(s, c) - RING + 1)
                sp.dma_start(w_raw[:, c % RING], src).then_inc(w_in[c % RING], 16)

            def state_load(h, b):
                if b > 1:
                    sp.wait_ge(c_out[c_slot(b)], 16 * (c_stores(h, b) - 1))
                elif h:
                    sp.wait_ge(c_out[c_slot(b)], 16 * c_stores(h - 1, b + 6))
                sp.dma_start(cst[:, c_slot(b)], c_dram[b, h]).then_inc(c_in[c_slot(b)], 16)

            def state_store(h, b):
                if b == "prompt":
                    sp.wait_ge(drained, FILL["updp", h, 0])
                    sp.wait_ge(drained_a, ACT_FILL["updp", h, 0])
                    sp.dma_start(c_new_p[h], cst[:, 0]).then_inc(c_out[0], 16)
                else:
                    sp.wait_ge(drained, FILL["upd", h, b])
                    sp.dma_start(c_new[b, h], cst[:, c_slot(b)]).then_inc(c_out[c_slot(b)], 16)

            for g in range(GROUPS):
                for c in range(2):
                    n = 2 * g + c
                    if n >= RING:
                        sp.wait_ge(w_lo_ok, n - RING + 1)
                    sp.dma_start(w_raw[:, n % RING], w_pool[g, c]).then_inc(w_in[n % RING], 16)

            def ffn(layer, s0):
                with sp.Fori(0, SLICES) as sl:
                    with sp.Fori(0, MT) as j:
                        for c in range(CH):
                            load(s0 + sl * 8 + j, c, w_up[layer][c][:, :, bass.ds(sl * D + j * NC, NC)])
                    with sp.Fori(0, MT) as j:
                        for c in range(CH):
                            load(s0 + 4 + sl * 8 + j, c, w_down[layer][sl, c][:, :, bass.ds(j * NC, NC)])

            ffn(0, S_FFN0)
            with sp.Fori(0, 8) as j:
                for c in range(CH):
                    load(S_QKV + j, c, w_qkvo[c][:, :, bass.ds(j * NC, NC)])
            sp.wait_ge(op_lo_ok, 2 * KT)
            sp.wait_ge(a_lo_ok, SLICES * KT)
            for b in range(2):
                state_load(0, b)
            for q in range(HEADS + 1):
                for c in range(CH):
                    if q < HEADS:
                        load(S_O + q, c, w_qkvo[c][:, :, (8 + q) * NC:(9 + q) * NC])
                    else:
                        load(S_OUT, c, w_out[c][:, :, 0:NC])
                    if q == 0:
                        continue
                    if c == 0:
                        state_store(q - 1, "prompt")
                        state_load(q - 1, 2)
                    state_store(q - 1, c)
                    if c + 3 < NSEQ:
                        state_load(q - 1, c + 3)
                    elif c > 5 and q < HEADS:
                        state_load(q, c - 6)
            with sp.Fori(1, MT) as j:
                for c in range(CH):
                    load(S_OUT + j, c, w_out[c][:, :, bass.ds(j * NC, NC)])
            ffn(1, S_FFN1)
            for t in range(TT):
                sp.wait_ge(y_done[t], 1)
                dst = O["y_prompt"][0, t * P:(t + 1) * P, :] if t < 2 else O["y_sample"].rearrange("b t d -> (b t) d")
                sp.dma_start(dst, yrow[0:ROWS[t], t, :]).then_inc(y_out, 16)
            for i in range(3):
                sp.wait_ge(c_out[i], 16 * 3 * HEADS)
            for i in range(2):
                sp.wait_ge(rows_out[i], 16 * 2)
            sp.wait_ge(outs, 16 * (1 + NSEQ + 2 + 2))
            sp.wait_ge(y_out, 16 * TT)

        @block.gpsimd
        def _(pool):
            n_chain = [0]

            def link(ins):
                n_chain[0] += 1
                ins.then_inc(pool_c, 1)
                pool.wait_ge(pool_c, n_chain[0])

            for n, (name, at) in enumerate((("norm_mix", V_MIX), ("norm_ffn", V_FFN), ("norm_final", V_FIN),
                                            ("pool_scale", V_SCALE), ("mlstm_head_norm", V_HEAD))):
                src = A[name]
                src = src.rearrange("(k p) -> k p", p=P) if len(src.shape) == 1 else src.rearrange("l (k p) -> (l k) p", p=P)
                pool.dma_start(vrow[at:at + src.shape[0], :], src).then_inc(vecs_in, 16)
            def select(ap, pattern, cm, base=0, op=ALU.is_ge, fill=0.0):
                link(pool.affine_select(out=ap, in_=ap, compare_op=op, fill=fill, base=base, pattern=pattern,
                                        channel_multiplier=cm))

            link(pool.memset(ident[:, :], 0.0))
            select(ident[:, :], [[-1, P]], 1, op=ALU.not_equal, fill=1.0)
            link(pool.memset(ones[:, :], 1.0))
            link(pool.memset(uext[:, :, 0:PAD], 0.0))
            for n in range(PAD):
                link(pool.memset(icnt[:, n:n + 1], 1.0 / (n + 1)))
            link(pool.memset(causal[:, :], 0.0))
            select(causal[:, :], [[1, P]], -1, fill=NEG)
            link(pool.memset(causal_s[:, :], 0.0))
            select(causal_s[:, :], [[1, NS]], -1, fill=NEG)
            select(causal_s[:, :].rearrange("p (b t) -> p b t", t=TS), [[-TS, NSEQ], [0, TS]], 1, fill=NEG)
            link(pool.memset(seqmask[:, :, :], 0.0))
            link(pool.memset(seqmask[:, 0:2, 0:1], 1.0))
            link(pool.memset(seqmask[:, 2, 1:], 1.0))
            for at in (0, NS):
                select(seqmask[at:at + NS, 2, 1:], [[-TS, NSEQ]], 1)
                select(seqmask[at:at + NS, 2, 1:], [[TS, NSEQ]], -1, base=TS - 1)
            link(pool.memset(sel[:, :, :], 0.0))
            select(sel[:, :, :], [[-1, HEADS], [0, P]], 1, op=ALU.not_equal, fill=1.0)
            pool.memset(xcol[:, :], 1.0).then_inc(consts, 1)
            pool.wait_ge(consts, 1)
            pool.dma_start(O["pool_sample"][0, :, 0:PAD - TS, :], A["state_pool"][0, :, TS:PAD, :]).then_inc(outs, 16)
            with nc.allow_non_contiguous_dma("a few values"):
                pool.dma_start(bgate[:, :], A["mlstm_b_gate"][0].rearrange("(g h) -> h g", h=HEADS)).then_inc(small_in, 16)
                pool.dma_start(m0[:, :], A["state_mlstm_m"][0].rearrange("b h -> h b")).then_inc(small_in, 16)

            def pack(g):
                pool.wait_ge(u_ok, 2 * (4 * g + 4))
                src = uext[:, 4 * g:4 * g + 4, PAD + TP:].rearrange("p k (b r) -> p k b r", r=SEG)[:, :, :, PAD:]
                pool.tensor_copy(us[:, 4 * g:4 * g + 4, :].rearrange("p k (b t) -> p k b t", t=TS), src).then_inc(us_ok, 1)

            pack(0)
            pack(1)
            for g in (2, 3):
                pack(g)
                pool.wait_ge(u_ok, 2 * (4 * g + 4))
                pool.wait_ge(s_kept, g + 1)
                if g == 3:
                    pool.wait_ge(d_ok, 3)
                src = uext[:, 4 * g:4 * g + 4, :]
                for n in range(g + 1):
                    w = 1 << n
                    dst = win[1 + n % 2]
                    ins = pool.tensor_tensor(dst[:, :, 2 * w - 1:], src[:, :, 2 * w - 1:], src[:, :, w - 1:UX - w], ALU.add)
                    if n < g:
                        link(ins)
                    src = dst
                ins.then_inc(win_ok, 1)

            def new_pool_rows(g):
                pool.wait_ge(np_kept, 2 * g + 1)
                pool.dma_start(O["pool_prompt"][0, 0, :, g * NC:(g + 1) * NC],
                               ur_p[P - PAD:P, g % 2, :]).then_inc(rows_out[g % 2], 16)

            new_pool_rows(0)
            new_pool_rows(1)

            def squares(j, base):
                if j:
                    pool.wait_ge(r_inv, 2 * j)
                link(pool.memset(acc[:, :], 0.0))
                for k in range(KT):
                    pool.wait_ge(evicted, base + k + 1)
                    pool.tensor_tensor(sqt[:, :], hT[:, k, :], hT[:, k, :], ALU.mult).then_inc(sq_ok, 1)
                    pool.wait_ge(sq_ok, KT * j + k + 1)
                    pool.tensor_tensor(acc[:, :], acc[:, :], sqt[:, :], ALU.add).then_inc(ssq_ok, 1)
                    pool.wait_ge(ssq_ok, KT * j + k + 1)

            squares(0, 0)
            new_pool_rows(2)
            new_pool_rows(3)
            pool.wait_ge(np_kept, 8)
            for b in range(NSEQ):
                pool.dma_start(O["pool_sample"][0, b, PAD - TS:, :], ur_s[b * TS:(b + 1) * TS, :]).then_inc(outs, 16)

            def ffn(layer, s0):
                f0 = 16 * SLICES * layer
                with pool.Fori(0, SLICES) as sl:
                    with pool.Fori(0, MT) as j:
                        hidden_tiles(f0 + sl * KT + j * MT, s0 + sl * 8 + j, j * MT)

            def hidden_tiles(first, s, k0):
                for m in range(MT):
                    hi = a_hi[:, bass.ds(k0 + m, 1), :]
                    lo = a_lo[:, bass.ds(k0 + m, 1), :]
                    pool.wait_ge(evicted, tiles_out(s, m))
                    pool.tensor_tensor(sq[:, m % 2], relu[:, m], relu[:, m], ALU.mult).then_inc(a_sq_ok, 1)
                    pool.wait_ge(a_sq_ok, first + m + 1)
                    pool.wait_ge(a_hi_ok, first + m + 1)
                    pool.tensor_tensor(lo, sq[:, m % 2:m % 2 + 1], hi.bitcast(F32), ALU.subtract).then_inc(a_lo_ok, 1)

            pool.wait_ge(d_ok, 4)
            pool.wait_ge(outs, 16 * (1 + NSEQ))
            for i in range(2):
                pool.wait_ge(rows_out[i], 32)
            with nc.allow_non_contiguous_dma("8 columns"):
                pool.dma_start(gw_raw[:, :, :], w_gate).then_inc(small_in, 16)
            pool.memset(gw_hi[:, :, :].bitcast(F32), 0.0).then_inc(gw_lo_ok, 1)
            pool.memset(gw_lo[:, :, :].bitcast(F32), 0.0).then_inc(gw_lo_ok, 1)

            ffn(0, S_FFN0)
            pool.wait_ge(gw_hi_ok, 2)
            pool.wait_ge(gw_lo_ok, 2)
            for n, at in enumerate((GP, 64)):
                pool.tensor_tensor(gw_lo[:, :, at:at + HEADS], gw_raw[:, :, n * HEADS:(n + 1) * HEADS],
                                   gw_hi[:, :, at:at + HEADS].bitcast(F32), ALU.subtract).then_inc(gw_lo_ok, 1)
            squares(1, MT * GROUPS + MT * (S_QKV - MT))

            pool.wait_ge(gates_sum, 1)
            for i in range(2):
                link(pool.memset(scan_p[i][:, 0:P], 0.0))
                link(pool.memset(scan_s[i][:, :, 0:4], 0.0))
            pool.dma_start(nrow[1:, :], A["state_mlstm_n"][0].rearrange("b h d -> b (h d)")).then_inc(small_in, 16)
            pool.wait_ge(tanh_ok, 4)

            scan(pool, link, ALU.add)
            link(pool.tensor_copy(nbrow[:, 0:TP], scan_p[0][:, P:]))
            link(pool.tensor_copy(seqs(nbrow), scan_s[1][:, :, 4:]))
            link(pool.tensor_scalar(grow[:, :], grow[:, :], CAP, None, ALU.mult))
            link(pool.tensor_tensor(grow[:, :], grow[:, :], nbrow[:, :], ALU.add))
            for i in range(2):
                link(pool.memset(scan_p[i][:, 0:P], NEG))
                link(pool.memset(scan_s[i][:, :, 0:4], NEG))
            link(pool.tensor_copy(scan_p[0][:, P:], grow[:, 0:TP]))
            pool.tensor_copy(scan_s[0][:, :, 4:], seqs(grow)).then_inc(g_ok, 1)
            pool.wait_ge(m_ok, 2)
            m0b = m0[:, :].unsqueeze(2).broadcast_to([HEADS, NSEQ, TS])
            last_s = seqs(mrow)[:, :, TS - 1]
            last_p = mrow[:, TP - 1:TP]
            link(pool.memset(gates[:, R_DEC:R_WK], 0.0))
            link(pool.tensor_scalar(gates[:, R_NEGM:R_E], mrow[:, :], -1.0, None, ALU.mult))
            link(pool.tensor_tensor(gates[:, R_E:R_WI], nbrow[:, :], mrow[:, :], ALU.subtract))
            link(pool.tensor_tensor(gates[:, R_WI:R_DEC].rearrange("h (b t) -> h b t", t=TS), m0b, seqs(mrow), ALU.subtract))
            link(pool.tensor_scalar(gates[:, R_DEC:R_DEC + 1], last_p, -1.0, None, ALU.mult))
            link(pool.tensor_tensor(gates[:, R_DEC + 1:R_DEC + 1 + NSEQ], m0[:, :], last_s, ALU.subtract))
            link(pool.tensor_tensor(gates[:, R_WK:R_WK + TP], grow[:, 0:TP], last_p.broadcast_to([HEADS, TP]), ALU.subtract))
            link(pool.tensor_tensor(seqs(gates, R_WK), seqs(grow),
                                    last_s.unsqueeze(2).broadcast_to([HEADS, NSEQ, TS]), ALU.subtract))
            link(pool.tensor_tensor(mnew[:, 0:1], last_p, nbrow[:, TP - 1:TP], ALU.subtract))
            link(pool.tensor_tensor(mnew[:, 1:], last_s, seqs(nbrow)[:, :, TS - 1], ALU.subtract))
            link(pool.memset(cols[:, :, :], 0.0))
            link(pool.memset(qwm[:, :, :], 0.0))
            pool.memset(nrow[0:1, :], 0.0).then_inc(rows_ok, 1)
            with nc.allow_non_contiguous_dma("36 values"):
                pool.dma_start(O["m_prompt"][0].rearrange("b h -> h b"), mnew[:, 0:1]).then_inc(outs, 16)
                pool.dma_start(O["m_sample"][0].rearrange("b h -> h b"), mnew[:, 1:]).then_inc(outs, 16)

            def weigh_keys(h):
                pool.wait_ge(drained, FILL["turn", h, 2])
                kp, ks = kvp[:, :, DV:], kvs[:, h % 2, DV:]
                pool.tensor_tensor(kp, kp, cols[:, 1:4:2, h].unsqueeze(2).broadcast_to([P, 2, DK]),
                                   ALU.mult).then_inc(kw_ok, 1)
                pool.tensor_scalar(ks, ks, cols[:, 5, h:h + 1], None, ALU.mult).then_inc(kw_ok, 1)

            def head_squares(h):
                pool.wait_ge(att_s, h + 1)
                s4 = qkv[:, sq_block(h):sq_block(h) + 4, :]
                link(pool.tensor_tensor(s4, att(h), att(h), ALU.mult))
                link(pool.tensor_tensor(s4[:, 0:2], s4[:, 0:2], s4[:, 2:4], ALU.add))
                if h:
                    pool.wait_ge(x3_filled, X3_USES[f"ms{h - 1}"])
                pool.tensor_tensor(hss[:, :], s4[:, 0], s4[:, 1], ALU.add).then_inc(hss_ok, 1)

            weigh_keys(0)
            for h in range(HEADS):
                if h:
                    head_squares(h - 1)
                if h + 1 < HEADS:
                    weigh_keys(h + 1)
            head_squares(HEADS - 1)
            pool.wait_ge(x3_read, X3_USES[f"n{HEADS - 1}"])
            pool.dma_start(O["n_prompt"][0].rearrange("b h d -> b (h d)"), nrow[0:1, :]).then_inc(outs, 16)
            pool.dma_start(O["n_sample"][0].rearrange("b h d -> b (h d)"), nrow[1:, :]).then_inc(outs, 16)
            pool.wait_ge(x3_filled, X3_USES["ms3"])
            pool.wait_ge(att_ok, HEADS)
            pool.wait_ge(hss_ok, HEADS)
            squares(2, MT * GROUPS + MT * S_OUT)
            ffn(1, S_FFN1)
            squares(3, MT * GROUPS + MT * (S_END - MT))
            pool.wait_ge(r_ok, 5)
            pool.wait_ge(y_kept_a, 2 * MT)
            pool.tensor_scalar(yrow[0:NS, 2, :], yrow[0:NS, 2, :], rcol[0:NS, 2:3], None, ALU.mult).then_inc(y_done[2], 1)

        @block.scalar
        def _(act):
            def split(s, c):
                act.wait_ge(w_in[c % RING], (s * (CH // RING) + 2 + c // RING + 1) * 16)
                act.wait_ge(gemm, used_before(s, c))
                act.activation(w_hi[:, c % RING], w_raw[:, c % RING], ACT.Copy).then_inc(w_hi_ok, 1)

            def split_pool(n):
                act.wait_ge(w_in[n % RING], 16 * (n // RING + 1))
                if n >= RING:
                    act.wait_ge(gemm, pool_used((n - RING) // 2, n % 2))
                act.activation(w_hi[:, n % RING], w_raw[:, n % RING], ACT.Copy).then_inc(w_hi_ok, 1)

            def slab(s, after=None, mid=None, last=False):
                for i in range(CH):
                    c = LEAD + i
                    if c < CH:
                        split(s, c)
                    elif not last:
                        split(s + 1, c - CH)
                    if mid and i in mid:
                        mid[i]()
                for m in range(MT):
                    if after:
                        after(m)

            def root(j, dst, src):
                act.wait_ge(r_inv, 2 * j + 2)
                act.activation(dst, src, ACT.Sqrt).then_inc(r_ok, 1)

            for t in range(TT):
                act.wait_ge(x_in[t], 16)
                act.wait_ge(consts, 1)
                if t:
                    act.wait_ge(x_sq, t)
                act.activation(G[0:ROWS[t], :, :], xrow[0:ROWS[t], t, :].rearrange("p (a n) -> p a n", n=512), ACT.Square,
                               accum_out=xcol[0:ROWS[t], t:t + 1]).then_inc(x_sq, 1)
            for k in range(3):
                act.wait_ge(x_turned, k + 1)
                act.activation(hT[:, k, :], X[k % 3][:, 0:T], ACT.Copy).then_inc(x_kept, 1)
            root(0, rcol[:, 0:TT], rcol[:, 0:TT])
            for k in range(3, KT):
                act.wait_ge(x_turned, k + 1)
                act.activation(hT[:, k, :], X[k % 3][:, 0:T], ACT.Copy).then_inc(x_kept, 1)
                if k >= 13:
                    split_pool(k - 13)
            for g in range(GROUPS):
                act.wait_ge(s_turned, g + 1)
                dst = uext[:, 4 * g:4 * g + 4, PAD + TP:].rearrange("p k (b r) -> p k b r", r=SEG)[:, :, :, 0:PAD]
                for i in range(4):
                    ins = act.activation(dst[:, i], X[g % 2][:, i * NSEQ * PAD:(i + 1) * NSEQ * PAD].rearrange("p (b r) -> p b r", r=PAD), ACT.Copy)
                ins.then_inc(s_kept, 1)

            def d_hi(g):
                act.wait_ge(d_ok, g + 1)
                act.activation(a_hi[:, 4 * g:4 * g + 4, :], dtmp[:, :, :], ACT.Copy).then_inc(d_hi_ok, 1)

            def keep_new_pool(g):
                act.wait_ge(np_turned, g + 1)
                if g > 1:
                    act.wait_ge(rows_out[g % 2], 16)
                act.activation(ur_p[:, g % 2, :], X[0][:, :], ACT.Copy).then_inc(np_kept, 1)
                act.activation(ur_s[0:NS, g * NC:(g + 1) * NC], X[1][0:NS, :], ACT.Copy).then_inc(np_kept, 1)

            def op_split(j, k, scale):
                act.activation(op_hi[:, k, :], hT[:, k, :], ACT.Copy, scale=scale).then_inc(op_hi_ok, 1)

            d_hi(0)
            d_hi(1)
            for g in range(GROUPS):
                for n in (2 * g + LEAD, 2 * g + LEAD + 1):
                    split_pool(n) if n < 8 else split(0, n - 8)
                keep_new_pool(g)
                if g + 2 < GROUPS:
                    d_hi(g + 2)
            act.wait_ge(np_kept, 8)
            act.wait_ge(outs, 16 * (1 + NSEQ))
            act.wait_ge(d_lo_ok, 4)
            for k in range(KT):
                act.wait_ge(evicted, k + 1)
                op_split(0, k, vec(V_FFN + k))

            def hidden(s, first, k0):
                def after(m):
                    act.wait_ge(evicted, tiles_out(s, m))
                    act.activation(a_hi[:, bass.ds(k0 + m, 1), :], relu[:, m:m + 1], ACT.Square).then_inc(a_hi_ok, 1)
                return after

            def norm_op(s, j, col):
                def after(m):
                    act.wait_ge(evicted, tiles_out(s, m))
                    op_split(j, (s % 4) * MT + m, vec(col + (s % 4) * MT + m))
                return after

            def ffn(layer, s0, rj):
                f0 = KT * SLICES * layer
                slab(s0, hidden(s0, f0, 0), {6: lambda: root(rj, Rb[:, :], rv[:, :])})
                with act.Fori(1, MT) as j:
                    slab(s0 + j, hidden(s0 + j, f0 + j * MT, j * MT))
                with act.Fori(0, MT) as j:
                    slab(s0 + 4 + j)
                with act.Fori(1, SLICES - 1) as sl:
                    with act.Fori(0, MT) as j:
                        slab(s0 + sl * 8 + j, hidden(s0 + sl * 8 + j, f0 + sl * KT + j * MT, j * MT))
                    with act.Fori(0, MT) as j:
                        slab(s0 + 4 + sl * 8 + j)
                sl = SLICES - 1
                with act.Fori(0, MT) as j:
                    slab(s0 + sl * 8 + j, hidden(s0 + sl * 8 + j, f0 + sl * KT + j * MT, j * MT))

            ffn(0, S_FFN0, 1)
            for j in range(MT):
                s = S_QKV - MT + j
                slab(s, norm_op(s, 1, V_MIX + KT))
                if j == 0:
                    act.wait_ge(small_in, 48)
                    act.wait_ge(gw_lo_ok, 2)
                    for n, at in enumerate((GP, 64)):
                        act.activation(gw_hi[:, :, at:at + HEADS], gw_raw[:, :, n * HEADS:(n + 1) * HEADS],
                                       ACT.Copy).then_inc(gw_hi_ok, 1)
            slab(S_QKV, None, {6: lambda: root(2, Rb[:, :], rv[:, :])})
            act.wait_ge(gz_ok, 3)
            act.activation(grow[:, :], gz[:, 0, :], ACT.Tanh, scale=1.0 / CAP, bias=bgate[:, 0:1]).then_inc(tanh_ok, 1)
            act.activation(gz[:, 1, :], gz[:, 1, :], ACT.Tanh, scale=1.0 / CAP, bias=bgate[:, 1:2]).then_inc(act_c, 1)
            act.wait_ge(act_c, 1)
            act.activation(gz[:, 1, :], gz[:, 1, :], ACT.Exp, scale=-CAP).then_inc(tanh_ok, 1)
            act.wait_ge(tanh_ok, 2)
            act.activation(scan_p[0][:, P:], gz[:, 1, 0:TP], ACT.Ln, bias=1.0).then_inc(tanh_ok, 1)
            act.activation(scan_s[0][:, :, 4:], gz[:, 1, TP:].rearrange("h (b t) -> h b t", t=TS), ACT.Ln,
                           bias=1.0).then_inc(tanh_ok, 1)
            with act.Fori(1, 7) as j:
                slab(S_QKV + j)
            act.wait_ge(rows_ok, 1)
            act.activation(gates[:, R_E:], gates[:, R_E:], ACT.Exp).then_inc(gates_exp, 1)

            def prep(h, i):
                p = h % 2
                if i < TT:
                    act.wait_ge(filled, FILL["turn", h, i])
                    dst = kvp[:, i, 0:DV] if i < 2 else kvs[:, p, 0:DV]
                    act.activation(dst, X[0][:, :], ACT.Copy).then_inc(drained_a, 1)
                elif i == TT:
                    act.wait_ge(filled, FILL["rows", h, 0])
                    act.activation(EW[:, p, :], X[1][:, 0:BC], ACT.Copy).then_inc(drained_a, 1)
                    act.wait_ge(drained, FILL["rows", h, 0])
                    act.activation(eb[:, 0:384], eb[:, 0:384], ACT.Exp).then_inc(eb_exp, 1)
                    act.activation(eb[0:NS, 384:448], eb[0:NS, 384:448], ACT.Exp).then_inc(eb_exp, 1)

            slab(S_QKV + 7, None, {i + 1: (lambda i=i: prep(0, i)) for i in range(TT + 1)})

            def root2(h):
                act.wait_ge(r2_inv, h + 1)
                act.activation(r2b[:, :], r2b[:, :], ACT.Sqrt).then_inc(r2_ok, 1)

            def key_hi(h, b):
                if b > 1:
                    act.wait_ge(filled, FILL["upd", h, b - 2])
                act.activation(kwb[:, b % 2, :], kvs[:, h % 2, DV:], ACT.Copy,
                               scale=seqmask[:, 2, 1 + b:2 + b]).then_inc(kwb_hi_ok, 1)

            def att_hi(k):
                act.wait_ge(att_ok, k // 4 + 1)
                act.activation(a_hi[:, k, :], qkv[:, KT + k, :], ACT.Copy).then_inc(att_hi_ok, 1)

            for h in range(HEADS):
                if h:
                    act.wait_ge(filled, FILL["upd", h - 1, NSEQ - 1])
                act.wait_ge(drained_a, ACT_FILL["turn", h, 2])
                act.activation(v_hi[:, :], kvs[:, h % 2, 0:DV], ACT.Copy).then_inc(v_hi_ok, 1)
                act.wait_ge(kw_ok, 2 * h + 2)
                key_hi(h, 0)
                for c in range(CH):
                    n = LEAD + c
                    split(S_O + h, n) if n < CH else split(S_O + h + 1, n - CH)
                    if c == 0:
                        act.wait_ge(filled, FILL["updp", h, 0])
                        if h:
                            act.wait_ge(c_out[0], 16 * c_stores(h - 1, 5))
                        act.activation(cst[:, 0, 1, :], X[1][:, :], ACT.Copy).then_inc(drained_a, 1)
                    if c + 1 < NSEQ:
                        key_hi(h, c + 1)
                    if h + 1 < HEADS and 1 <= c <= TT + 1:
                        prep(h + 1, c - 1)
                    if h and c == 4:
                        root2(h - 1)
                    if h == HEADS - 1 and c >= 6:
                        act.wait_ge(hss_ok, h)
                        act.wait_ge(att_ok, h)
                        for k in range(4 * (c - 6), 4 * (c - 5)):
                            att_hi(k)
                act.wait_ge(x2_filled, h + 1)
                if h + 1 < HEADS:
                    act.wait_ge(drained, FILL["score", h + 1, 0])
                act.activation(hs[0:NS, :], X[2][0:NS, :], ACT.Copy).then_inc(hs_kept, 1)
                act.wait_ge(evicted, tiles_out(S_O + h, MT - 1))
                z4 = qkv[:, z_block(h):z_block(h) + 4, :]
                act.activation(z4, z4, ACT.Sigmoid).then_inc(ez_ok, 1)

            def third_head_hi():
                act.wait_ge(hss_ok, HEADS)
                for k in range(8, 12):
                    att_hi(k)

            def last_head_hi():
                for k in range(12, KT):
                    att_hi(k)

            slab(S_OUT, norm_op(S_OUT, 2, V_FFN + KT),
                 {2: third_head_hi, 3: lambda: root2(HEADS - 1), 4: last_head_hi})
            for j in range(1, MT):
                s = S_OUT + j
                slab(s, norm_op(s, 2, V_FFN + KT))
            ffn(1, S_FFN1, 3)
            for j in range(MT):
                s = S_END - MT + j

                def keep(m, j=j):
                    if m == MT - 1:
                        act.wait_ge(y_turned, j + 1)
                        act.activation(yrow[:, 0, j * NC:(j + 1) * NC], X[0][:, :], ACT.Copy).then_inc(y_kept_a, 1)
                        act.activation(yrow[0:NS, 2, j * NC:(j + 1) * NC], X[2][0:NS, :], ACT.Copy).then_inc(y_kept_a, 1)
                slab(s, keep, last=j == MT - 1)
            root(4, rcol[:, 0:TT], rcol[:, 0:TT])
            act.wait_ge(r_ok, 5)
            act.wait_ge(y_kept_a, 2 * MT)
            act.activation(yrow[:, 0, :], yrow[:, 0, :], ACT.Copy, scale=rcol[:, 0:1]).then_inc(y_done[0], 1)

        @block.vector
        def _(v):
            n_chain = [0]

            def link(ins):
                n_chain[0] += 1
                ins.then_inc(dve, 1)
                v.wait_ge(dve, n_chain[0])

            def lo_of(slot):
                v.tensor_tensor(w_lo[:, slot], w_raw[:, slot], w_hi[:, slot].bitcast(F32), ALU.subtract).then_inc(w_lo_ok, 1)

            def split(s, c):
                v.wait_ge(w_hi_ok, chunk_no(s, c) + 1)
                lo_of(c % RING)

            def split_pool(n):
                v.wait_ge(w_hi_ok, n + 1)
                lo_of(n % RING)

            def slab(s, evict, mid=None, last=False):
                for i in range(CH):
                    c = LEAD + i
                    if c < CH:
                        split(s, c)
                    elif not last:
                        split(s + 1, c - CH)
                    if mid and i in mid:
                        mid[i]()
                for m in range(MT):
                    v.wait_ge(gemm, tile_done(s, m))
                    evict(m)

            def inverse(j, dst, src, n):
                v.tensor_scalar(dst, src, 1.0 / n, EPS, ALU.mult, ALU.add).then_inc(r_inv, 1)
                v.wait_ge(r_inv, 2 * j + 1)
                v.reciprocal(dst, dst).then_inc(r_inv, 1)

            v.wait_ge(consts, 1)
            v.wait_ge(x_sq, TT)
            inverse(0, rcol[:, 0:TT], xcol[:, 0:TT], D)
            v.wait_ge(r_ok, 1)
            for t in range(TT):
                ins = v.tensor_scalar(diag[:, t, :], ident[:, :], rcol[:, t:t + 1], None, ALU.mult)
            link(ins)
            v.wait_ge(vec_turned, 1)
            link(v.tensor_copy(vecs[:, :], X[3][:, T:T + V_ALL]))
            v.wait_ge(r_sum, 1)
            link(v.tensor_copy(Rb[:, :], X[3][:, 0:T]))
            for k in range(KT):
                v.wait_ge(x_kept, k + 1)
                v.scalar_tensor_tensor(out=uext[:, k, PAD:PAD + TP], in0=hT[:, k, 0:TP], scalar=vec(V_MIX + k),
                                       in1=Rb[:, 0:TP], op0=ALU.mult, op1=ALU.mult).then_inc(u_ok, 1)
                dst = uext[:, k, PAD + TP:].rearrange("p (b r) -> p b r", r=SEG)[:, :, PAD:]
                v.scalar_tensor_tensor(out=dst, in0=hT[:, k, TP:].rearrange("p (b t) -> p b t", t=TS), scalar=vec(V_MIX + k),
                                       in1=Rb[:, TP:].rearrange("p (b t) -> p b t", t=TS), op0=ALU.mult,
                                       op1=ALU.mult).then_inc(u_ok, 1)
                if k >= 13:
                    split_pool(k - 13)

            def pooled(g):
                w = 2 << g
                u = uext[:, 4 * g:4 * g + 4, :]
                v.wait_ge(u_ok, 2 * (4 * g + 4))
                v.wait_ge(s_kept, g + 1)
                if g:
                    v.wait_ge(d_lo_ok, g)
                if g < 2:
                    src = u
                    for n in range(g + 1):
                        s = 1 << n
                        dst = (win[0], win[3])[n % 2]
                        link(v.tensor_tensor(dst[:, :, 2 * s - 1:], src[:, :, 2 * s - 1:], src[:, :, s - 1:UX - s], ALU.add))
                        src = dst
                else:
                    v.wait_ge(win_ok, g - 1)
                    src = win[1 + g % 2]
                for i in range(MT):
                    v.scalar_tensor_tensor(out=dtmp[:, i, 0:TP], in0=src[:, i, PAD:PAD + TP], scalar=1.0 / w,
                                           in1=u[:, i, PAD:PAD + TP], op0=ALU.mult, op1=ALU.subtract)
                    seg = lambda a: a[:, i, PAD + TP:].rearrange("p (b r) -> p b r", r=SEG)[:, :, PAD:]
                    ins = v.scalar_tensor_tensor(out=dtmp[:, i, TP:].rearrange("p (b t) -> p b t", t=TS), in0=seg(src),
                                                 scalar=1.0 / w, in1=seg(u), op0=ALU.mult, op1=ALU.subtract)
                link(ins)
                first = dtmp[:, :, 0:w - 1]
                link(v.tensor_tensor(first, src[:, :, PAD:PAD + w - 1], bc(icnt[:, 0:w - 1], [P, MT, w - 1]), ALU.mult))
                v.tensor_tensor(first, first, u[:, :, PAD:PAD + w - 1], ALU.subtract).then_inc(d_ok, 1)
                v.wait_ge(d_hi_ok, g + 1)
                v.tensor_tensor(a_lo[:, 4 * g:4 * g + 4, :], dtmp[:, :, :], a_hi[:, 4 * g:4 * g + 4, :].bitcast(F32),
                                ALU.subtract).then_inc(d_lo_ok, 1)

            def op_split(j, k, col):
                v.wait_ge(op_hi_ok, KT * j + k + 1)
                v.scalar_tensor_tensor(out=op_lo[:, k, :], in0=hT[:, k, :], scalar=vec(col + k),
                                       in1=op_hi[:, k, :].bitcast(F32), op0=ALU.mult, op1=ALU.subtract).then_inc(op_lo_ok, 1)

            pooled(0)
            pooled(1)
            for g in range(GROUPS):
                for n in (2 * g + LEAD, 2 * g + LEAD + 1):
                    split_pool(n) if n < 8 else split(0, n - 8)
                for m in range(MT):
                    k = 4 * g + m
                    v.wait_ge(gemm, pool_tile(g, m))
                    v.scalar_tensor_tensor(out=hT[:, k, :], in0=G[:, m, 0:T], scalar=vec(V_SCALE + k), in1=hT[:, k, :],
                                           op0=ALU.mult, op1=ALU.add).then_inc(evicted, 1)
                if g + 2 < GROUPS:
                    pooled(g + 2)
            for k in range(KT):
                op_split(0, k, V_FFN)

            def hidden(s, first):
                def evict(m):
                    if not (isinstance(first, int) and first == 0):
                        v.wait_ge(a_lo_ok, first + m - 3)
                        v.wait_ge(a_hi_ok, first + m - 3)
                    v.scalar_tensor_tensor(out=relu[:, m], in0=G[:, m, 0:T], scalar=0.0, in1=Rb[:, :], op0=ALU.max,
                                           op1=ALU.mult).then_inc(evicted, 1)
                return evict

            def add(k0):
                def evict(m):
                    h = hT[:, bass.ds(k0 + m, 1), :]
                    v.tensor_tensor(h, G[:, m:m + 1, 0:T], h, ALU.add).then_inc(evicted, 1)
                return evict

            def add_norm(s, j, col):
                k0 = (s % 4) * MT

                def evict(m):
                    h = hT[:, k0 + m, :]
                    v.tensor_tensor(h, G[:, m, 0:T], h, ALU.add).then_inc(evicted, 1)
                    if m:
                        op_split(j, k0 + m - 1, col)
                    if m == MT - 1:
                        op_split(j, k0 + m, col)
                return evict

            def ffn(layer, s0, rj):
                f0 = KT * SLICES * layer

                def norm():
                    v.wait_ge(r_sum, rj + 1)
                    inverse(rj, rv[:, :], X[3][:, 0:T], D)

                def ready():
                    v.wait_ge(r_ok, rj + 1)

                slab(s0, hidden(s0, f0), {5: norm, 7: ready})
                with v.Fori(1, MT) as j:
                    slab(s0 + j, hidden(s0 + j, f0 + j * MT))
                with v.Fori(0, MT) as j:
                    slab(s0 + 4 + j, add(j * MT))
                with v.Fori(1, SLICES - 1) as sl:
                    with v.Fori(0, MT) as j:
                        slab(s0 + sl * 8 + j, hidden(s0 + sl * 8 + j, f0 + sl * KT + j * MT))
                    with v.Fori(0, MT) as j:
                        slab(s0 + 4 + sl * 8 + j, add(j * MT))
                sl = SLICES - 1
                with v.Fori(0, MT) as j:
                    slab(s0 + sl * 8 + j, hidden(s0 + sl * 8 + j, f0 + sl * KT + j * MT))

            ffn(0, S_FFN0, 1)
            for j in range(MT):
                s = S_QKV - MT + j
                slab(s, add_norm(s, 1, V_MIX + KT))

            def proj(pos):
                def evict(m):
                    v.tensor_tensor(qkv[:, bass.ds(pos(m), 1), :], G[:, m:m + 1, 0:T], bc(Rb[:, :], [P, 1, T]),
                                    ALU.mult).then_inc(evicted, 1)
                return evict

            q_pos = lambda j: lambda m: j * 8 + (4 * (m // 2) + m % 2)
            k_pos = lambda j: lambda m: j * 8 + (4 * (m // 2) + 2 + m % 2)

            def norm():
                v.wait_ge(r_sum, 3)
                inverse(2, rv[:, :], X[3][:, 0:T], D)

            def gate_rows():
                v.wait_ge(small_in, 32)
                v.tensor_scalar(bgate[:, :], bgate[:, :], 1.0 / CAP, None, ALU.mult).then_inc(gz_ok, 1)
                v.wait_ge(gates_sum, 1)
                v.wait_ge(r_ok, 3)
                v.tensor_tensor(gz[:, 0, :], X[0][GP:GP + HEADS, 0:T], Rb[GP:GP + HEADS, :], ALU.mult).then_inc(gz_ok, 1)
                v.tensor_tensor(gz[:, 1, :], X[0][64:64 + HEADS, 0:T], Rb[64:64 + HEADS, :], ALU.mult).then_inc(gz_ok, 1)

            slab(S_QKV, proj(q_pos(0)), {5: norm, 7: gate_rows})
            slab(S_QKV + 1, proj(q_pos(1)))
            with v.Fori(0, 2) as j:
                slab(S_QKV + 2 + j, proj(k_pos(j)))
            v.wait_ge(g_ok, 1)
            scan(v, link, ALU.max)
            v.tensor_scalar(mrow[:, 0:TP], scan_p[0][:, P:], 0.0, None, ALU.max).then_inc(m_ok, 1)
            v.tensor_tensor(seqs(mrow), scan_s[1][:, :, 4:], m0[:, :].unsqueeze(2).broadcast_to([HEADS, NSEQ, TS]),
                            ALU.max).then_inc(m_ok, 1)
            with v.Fori(0, 3) as j:
                slab(S_QKV + 4 + j, proj(lambda m: j * MT + (KT + m)))

            def token_gates():
                v.wait_ge(filled, FILL["cols", 0, 0])
                v.tensor_copy(cols[:, :, :], X[0][:, 0:24].rearrange("p (a h) -> p a h", h=HEADS))
                v.tensor_copy(dect[:, :], X[1][0:1 + NSEQ, 0:HEADS]).then_inc(drained, 1)
                v.wait_ge(drained, FILL["cols", 0, 0])

            def prep(h, i):
                p = h % 2
                if i < TT:
                    v.wait_ge(filled, FILL["turn", h, i])
                    dst = kvp[:, i, DV:] if i < 2 else kvs[:, p, DV:]
                    v.tensor_copy(dst, X[1][:, 0:DK]).then_inc(drained, 1)
                elif i == TT:
                    v.wait_ge(filled, FILL["rows", h, 0])
                    if h:
                        v.wait_ge(prep_ok, h)
                    negm = X[0]
                    v.scalar_tensor_tensor(out=eb[:, 0:P], in0=negm[:, 0:P], scalar=cols[:, 0, h:h + 1], in1=causal[:, :],
                                           op0=ALU.add, op1=ALU.add)
                    v.tensor_scalar(eb[:, P:TP], negm[:, P:TP], cols[:, 0, h:h + 1], None, ALU.add)
                    v.scalar_tensor_tensor(out=eb[:, TP:384], in0=negm[:, P:TP], scalar=cols[:, 2, h:h + 1],
                                           in1=causal[:, :], op0=ALU.add, op1=ALU.add)
                    v.scalar_tensor_tensor(out=eb[0:NS, 384:448], in0=negm[0:NS, TP:T], scalar=cols[0:NS, 4, h:h + 1],
                                           in1=causal_s[0:NS, :], op0=ALU.add, op1=ALU.add).then_inc(drained, 1)
                else:
                    v.wait_ge(filled, FILL["score", h, 0])
                    v.wait_ge(eb_exp, 2 * h + 2)
                    v.scalar_tensor_tensor(out=ST[:, 0:384], in0=X[0][:, 0:384], scalar=QSCALE, in1=eb[:, 0:384],
                                           op0=ALU.mult, op1=ALU.mult)
                    v.scalar_tensor_tensor(out=ST[0:NS, 384:448], in0=X[0][0:NS, 384:448], scalar=QSCALE,
                                           in1=eb[0:NS, 384:448], op0=ALU.mult, op1=ALU.mult)
                    v.tensor_copy(nts[:, :], X[1][:, 0:18]).then_inc(drained, 1)
                    v.wait_ge(drained_a, ACT_FILL["rows", h, 0])
                    for t in range(2):
                        ins = v.scalar_tensor_tensor(out=qw[:, t, :], in0=qkv[:, head_block(h) + t, TP:T], scalar=QSCALE,
                                                     in1=EW[:, p, T:T + NS], op0=ALU.mult, op1=ALU.mult)
                    link(ins)
                    v.wait_ge(drained, FILL["score", h, 0])
                    for t in range(2):
                        ins = v.tensor_tensor(qn[:, t, :].rearrange("p (b t) -> p b t", t=TS),
                                              qw[:, t, :].rearrange("p (b t) -> p b t", t=TS),
                                              nts[:, 9 * t + 1:9 * t + 9].unsqueeze(2).broadcast_to([P, NSEQ, TS]), ALU.mult)
                    ins.then_inc(prep_ok, 1)

            slab(S_QKV + 7, proj(lambda m: KT + 12 + m),
                 {0: token_gates, **{i + 1: (lambda i=i: prep(0, i)) for i in range(TT + 2)}})

            def mean_square(h):
                v.wait_ge(x3_filled, X3_USES[f"ms{h}"])
                v.tensor_scalar(r2b[:, :], X[3][:, 0:T], 1.0 / DV, EPS, ALU.mult, ALU.add).then_inc(x3_read, 1)
                v.wait_ge(x3_read, X3_USES[f"ms{h}"])
                v.reciprocal(r2b[:, :], r2b[:, :]).then_inc(r2_inv, 1)

            def gated(h):
                z4 = qkv[:, z_block(h):z_block(h) + 4, :]
                v.wait_ge(ez_ok, h + 1)
                v.wait_ge(r2_ok, h + 1)
                for i in range(4):
                    ins = v.scalar_tensor_tensor(out=att(h)[:, i], in0=att(h)[:, i], scalar=vec(V_HEAD + 4 * h + i),
                                                 in1=r2b[:, :], op0=ALU.mult, op1=ALU.mult)
                link(ins)
                v.tensor_tensor(att(h), att(h), z4, ALU.mult).then_inc(att_ok, 1)

            def a_lo_of(k):
                v.wait_ge(att_hi_ok, k + 1)
                v.tensor_tensor(a_lo[:, k, :], qkv[:, KT + k, :], a_hi[:, k, :].bitcast(F32), ALU.subtract).then_inc(att_lo_ok, 1)

            def samples_out(h):
                v.wait_ge(x2_turned, h + 1)
                v.tensor_tensor(att(h)[:, :, TP:T], X[2][:, 0:4 * NS].rearrange("p (a t) -> p a t", t=NS),
                                bc(rden[h % 2][:, TP:T], [P, 4, NS]), ALU.mult).then_inc(att_s, 1)

            def key_lo(h, b):
                v.wait_ge(kwb_hi_ok, NSEQ * h + b + 1)
                half = slice(NS, 2 * NS)
                v.scalar_tensor_tensor(out=kwb[half, b % 2, :], in0=kvs[half, h % 2, DV:],
                                       scalar=seqmask[half, 2, 1 + b:2 + b], in1=kwb[half, b % 2, :].bitcast(F32),
                                       op0=ALU.mult, op1=ALU.subtract).then_inc(kwb_ok, 1)

            for h in range(HEADS):
                p = h % 2
                rd = rden[p]
                v.wait_ge(x3_filled, X3_USES[f"den{h}"])
                v.wait_ge(drained_a, ACT_FILL["rows", h, 0])
                link(v.scalar_tensor_tensor(out=rd[:, :], in0=X[3][:, 0:T], scalar=-1.0, in1=EW[:, p, 0:T],
                                            op0=ALU.mult, op1=ALU.max))
                v.tensor_tensor(rd[:, :], X[3][:, 0:T], rd[:, :], ALU.max).then_inc(x3_read, 1)
                v.wait_ge(x3_read, X3_USES[f"den{h}"])
                link(v.reciprocal(rd[:, :], rd[:, :]))
                v.wait_ge(filled, FILL["num", h, 0])
                for i in range(2):
                    ins = v.tensor_tensor(att(h)[:, 2 * i:2 * i + 2, 0:TP], X[i][:, :].rearrange("p (a t) -> p a t", t=TP),
                                          bc(rd[:, 0:TP], [P, 2, TP]), ALU.mult)
                ins.then_inc(drained, 1)
                if h:
                    v.wait_ge(x2_filled, h)
                for t in range(2):
                    ins = v.tensor_copy(qwm[:, t, :].rearrange("p (b r) -> p b r", r=NS + TS)[:, :, 0:TS],
                                        qw[:, t, :].rearrange("p (b t) -> p b t", t=TS))
                ins.then_inc(qwm_ok, 1)
                v.wait_ge(v_hi_ok, h + 1)
                v.tensor_tensor(v_lo[:, :], kvs[:, p, 0:DV], v_hi[:, :].bitcast(F32), ALU.subtract).then_inc(v_lo_ok, 1)
                key_lo(h, 0)
                if h:
                    samples_out(h - 1)
                v.wait_ge(x3_filled, X3_USES[f"n{h}"])
                nh = nrow[:, h * DK:(h + 1) * DK]
                v.scalar_tensor_tensor(out=nh, in0=nh, scalar=dect[:, h:h + 1], in1=X[3][0:1 + NSEQ, 0:DK],
                                       op0=ALU.mult, op1=ALU.add).then_inc(x3_read, 1)
                for c in range(CH):
                    n = LEAD + c
                    split(S_O + h, n) if n < CH else split(S_O + h + 1, n - CH)
                    if c == 0:
                        v.wait_ge(filled, FILL["updp", h, 0])
                        if h:
                            v.wait_ge(c_out[0], 16 * c_stores(h - 1, 5))
                        v.tensor_copy(cst[:, 0, 0, :], X[0][:, :]).then_inc(drained, 1)
                    if c + 1 < NSEQ:
                        key_lo(h, c + 1)
                    if h + 1 < HEADS and 1 <= c <= TT + 2:
                        prep(h + 1, c - 1)
                    if h and c == 3:
                        mean_square(h - 1)
                    if h and c == 5:
                        gated(h - 1)
                    if h == HEADS - 1 and c >= 6:
                        for k in range(4 * (c - 6), 4 * (c - 5)):
                            a_lo_of(k)
                    if c == CH - 1:
                        for m in range(MT):
                            v.wait_ge(gemm, tile_done(S_O + h, m))
                            v.tensor_tensor(qkv[:, z_block(h) + m, :], G[:, m, 0:T], Rb[:, :], ALU.mult).then_inc(evicted, 1)
                    v.wait_ge(filled, FILL["upd", h, c])
                    for t in range(2):
                        st = cst[:, c_slot(c), t, :]
                        ins = v.scalar_tensor_tensor(out=st, in0=st, scalar=EW[:, p, T + NS + 1 + c:T + NS + 2 + c],
                                                     in1=X[t][:, :], op0=ALU.mult, op1=ALU.add)
                    ins.then_inc(drained, 1)
            samples_out(HEADS - 1)

            def third_head_lo():
                for k in range(8, 12):
                    a_lo_of(k)
                mean_square(HEADS - 1)

            def last_head_lo():
                for k in range(12, KT):
                    a_lo_of(k)

            for j in range(MT):
                s = S_OUT + j
                slab(s, add_norm(s, 2, V_FFN + KT),
                     {2: third_head_lo, 3: lambda: gated(HEADS - 1), 4: last_head_lo} if j == 0 else None)
            for i in range(3):
                v.wait_ge(c_out[i], 16 * 3 * HEADS)
            v.wait_ge(outs, 16 * (1 + NSEQ + 2 + 2))
            ffn(1, S_FFN1, 3)
            for j in range(MT):
                s = S_END - MT + j

                def evict(m, j=j):
                    k = j * MT + m
                    h = hT[:, k, :]
                    v.tensor_tensor(h, G[:, m, 0:T], h, ALU.add).then_inc(evicted, 1)
                    v.wait_ge(evicted, tiles_out(S_END - MT + j, m))
                    v.tensor_scalar(yT[:, k, :], h, vec(V_FIN + k), None, ALU.mult).then_inc(y_ok, 1)
                    if m == MT - 1:
                        v.wait_ge(y_turned, j + 1)
                        v.tensor_copy(yrow[:, 1, j * NC:(j + 1) * NC], X[1][:, :]).then_inc(y_kept_d, 1)
                slab(s, evict, last=j == MT - 1)
            v.wait_ge(r_sum, 5)
            v.tensor_scalar(rcol[:, 0:2], X[3][:, 0:2], 1.0 / D, EPS, ALU.mult, ALU.add)
            v.tensor_scalar(rcol[0:NS, 2:3], X[3][0:NS, 2:3], 1.0 / D, EPS, ALU.mult, ALU.add).then_inc(r_inv, 1)
            v.wait_ge(r_inv, 9)
            v.reciprocal(rcol[:, 0:TT], rcol[:, 0:TT]).then_inc(r_inv, 1)
            v.wait_ge(r_ok, 5)
            v.wait_ge(y_kept_d, MT)
            v.tensor_scalar(yrow[:, 1, :], yrow[:, 1, :], rcol[:, 1:2], None, ALU.mult).then_inc(y_done[1], 1)

        @block.tensor
        def _(pe):
            def turn(out, in_, rows=P):
                if in_.shape[-1] == P:
                    return pe.transpose(out, in_, ident[0:rows, 0:rows])
                return pe.matmul(out, in_, ident[0:rows, 0:rows], start=True, stop=True, skip_group_check=True)

            def chunk(slot, hi, lo, k0, first, last, tile=None, ready=None):
                for m in range(MT):
                    if tile:
                        tile(m)
                    for t in range(CK):
                        k = k0 + t
                        if ready and m == 0:
                            ready(k)
                        w = slice(m * P, (m + 1) * P)
                        pe.matmul(G[:, m, 0:T], w_hi[:, slot, t, w], hi[:, k, :], start=first and t == 0, stop=False)
                        pe.matmul(G[:, m, 0:T], w_hi[:, slot, t, w], lo[:, k, :], start=False, stop=False)
                        ins = pe.matmul(G[:, m, 0:T], w_lo[:, slot, t, w], hi[:, k, :], start=False,
                                        stop=last and t == CK - 1)
                    if last:
                        ins.then_inc(gemm, 1)
                if not last:
                    ins.then_inc(gemm, 1)

            def slab(s, hi, lo, ready=None, mid=None):
                for c in range(CH):
                    pe.wait_ge(w_lo_ok, chunk_no(s, c) + 1)
                    free = (lambda m: pe.wait_ge(evicted, s * MT + (MT * (GROUPS - 1) + m + 1))) if c == 0 else None
                    chunk(c % RING, hi, lo, CK * c, c == 0, c == CH - 1, free, ready)
                    if mid:
                        mid(c)

            pe.wait_ge(consts, 1)
            pe.wait_ge(vecs_in, 16 * 5)
            pe.transpose(X[3][:, T:T + V_ALL], vrow[0:V_ALL, :], ident[0:V_ALL, 0:V_ALL]).then_inc(vec_turned, 1)
            for t in range(TT):
                pe.wait_ge(x_in[t], 16)
            for k in range(KT):
                if k >= 3:
                    pe.wait_ge(x_kept, k - 2)
                for t in range(TT):
                    ins = pe.transpose(X[k % 3][:, t * P:t * P + ROWS[t]], xrow[0:ROWS[t], t, k * P:(k + 1) * P],
                                       ident[0:ROWS[t], 0:ROWS[t]])
                ins.then_inc(x_turned, 1)
                if k == 4:
                    pe.wait_ge(dve, 2)
                    for t in range(TT):
                        ins = pe.matmul(X[3][:, t * P:t * P + ROWS[t]], ones[0:ROWS[t], :], diag[0:ROWS[t], t, 0:ROWS[t]],
                                        start=t == 0, stop=True, skip_group_check=True)
                    ins.then_inc(r_sum, 1)
            pe.wait_ge(state_in, 16)
            pe.wait_ge(x_kept, KT)
            for g in range(GROUPS):
                if g > 1:
                    pe.wait_ge(s_kept, g - 1)
                for i in range(4):
                    ins = pe.transpose(X[g % 2][:, i * NSEQ * PAD:(i + 1) * NSEQ * PAD],
                                       srow[0:NSEQ * PAD, (4 * g + i) * P:(4 * g + i + 1) * P],
                                       ident[0:NSEQ * PAD, 0:NSEQ * PAD])
                ins.then_inc(s_turned, 1)
            pe.wait_ge(s_kept, GROUPS)

            for g in range(GROUPS):
                pe.wait_ge(d_lo_ok, g + 1)
                for c in range(2):
                    n = 2 * g + c
                    pe.wait_ge(w_lo_ok, n + 1)
                    free = (lambda m: pe.wait_ge(evicted, 4 * (g - 1) + m + 1)) if g and c == 0 else None
                    chunk(n % RING, a_hi, a_lo, 4 * g + CK * c, c == 0, c == 1, free)
                if g:
                    pe.wait_ge(np_kept, 2 * g)
                pe.wait_ge(us_ok, g + 1)
                for i in range(4):
                    k = 4 * g + i
                    pe.transpose(X[0][:, i * P:(i + 1) * P], uext[:, k, PAD + TP - P:PAD + TP], ident[:, :])
                    ins = pe.matmul(X[1][0:NS, i * P:(i + 1) * P], us[:, k, :], ident[:, :], start=True, stop=True,
                                    skip_group_check=True)
                ins.then_inc(np_turned, 1)

            def norm_sum(j):
                pe.wait_ge(ssq_ok, KT * j + KT)
                pe.matmul(X[3][:, 0:T], ones[:, :], acc[:, :], start=True, stop=True).then_inc(r_sum, 1)

            def op_ready(j):
                return lambda k: pe.wait_ge(op_lo_ok, KT * j + k + 1)

            def down_ready(first):
                return lambda k: pe.wait_ge(a_lo_ok, first + (k + 1))

            def ffn(layer, s0, j_op):
                f0 = KT * SLICES * layer
                slab(s0, op_hi, op_lo, op_ready(j_op), lambda c: norm_sum(j_op) if c == 4 else None)
                with pe.Fori(1, MT) as j:
                    slab(s0 + j, op_hi, op_lo)
                with pe.Fori(0, MT) as j:
                    slab(s0 + 4 + j, a_hi, a_lo, down_ready(f0))
                with pe.Fori(1, SLICES - 1) as sl:
                    with pe.Fori(0, MT) as j:
                        slab(s0 + sl * 8 + j, op_hi, op_lo)
                    with pe.Fori(0, MT) as j:
                        slab(s0 + 4 + sl * 8 + j, a_hi, a_lo, down_ready(f0 + sl * KT))
                sl = SLICES - 1
                with pe.Fori(0, MT) as j:
                    slab(s0 + sl * 8 + j, op_hi, op_lo)

            ffn(0, S_FFN0, 0)
            with pe.Fori(0, MT) as j:
                slab(S_QKV - MT + j, a_hi, a_lo, down_ready(KT * (SLICES - 1)))

            pe.wait_ge(gw_lo_ok, 4)
            for k in range(KT):
                pe.wait_ge(op_lo_ok, KT + k + 1)
                for w, x in ((gw_hi, op_hi), (gw_hi, op_lo), (gw_lo, op_hi)):
                    ins = pe.matmul(X[0][0:68, 0:T], w[:, k, :], x[:, k, :], start=k == 0 and w is gw_hi and x is op_hi,
                                    stop=k == KT - 1 and w is gw_lo)
            ins.then_inc(gates_sum, 1)
            slab(S_QKV, op_hi, op_lo, None, lambda c: norm_sum(1) if c == 4 else None)
            with pe.Fori(1, 7) as j:
                slab(S_QKV + j, op_hi, op_lo)

            order = fill_list()

            def bank_free(f):
                n = order.index(f)
                if n:
                    pe.wait_ge(drained, n)
                    for e in reversed(order[:n]):
                        if e in ACT_FILL:
                            pe.wait_ge(drained_a, ACT_FILL[e])
                            break

            def token_gates():
                pe.wait_ge(gates_exp, 1)
                pe.wait_ge(gz_ok, 3)
                eye = ident[GP:GP + HEADS, GP:GP + HEADS]
                for t in range(TT):
                    for n, row in enumerate((grow[:, tok(t)], gates[:, R_WK + t * P:R_WK + t * P + ROWS[t]])):
                        at = 4 * (2 * t + n)
                        for r in range(0, P, ROWS[t]):
                            pe.matmul(X[0][r:r + ROWS[t], at:at + HEADS], row, eye, start=at == 0, stop=True,
                                      skip_group_check=True)
                pe.matmul(X[1][0:1 + NSEQ, 0:HEADS], gates[:, R_DEC:R_DEC + 1 + NSEQ], eye,
                          start=True, stop=True).then_inc(filled, 1)

            def prep(h, i):
                q = head_block(h)
                if i < TT:
                    bank_free(("turn", h, i))
                    pe.wait_ge(evicted, tiles_out(S_QKV + (7 if h else 4), MT - 1))
                    for r in range(0, P, ROWS[i]):
                        for n in range(4):
                            turn(X[0][r:r + ROWS[i], n * P:(n + 1) * P], qkv[:, KT + 4 * h + n, tok(i)])
                        for n in range(2):
                            ins = turn(X[1][r:r + ROWS[i], n * P:(n + 1) * P], qkv[:, q + 2 + n, tok(i)])
                elif i == TT:
                    bank_free(("rows", h, 0))
                    pe.matmul(X[0][:, 0:T], sel[:, h, :], gates[:, R_NEGM:R_E], start=True, stop=True)
                    ins = pe.matmul(X[1][:, 0:BC], sel[:, h, :], gates[:, R_E:R_WK], start=True, stop=True)
                else:
                    bank_free(("score", h, 0))
                    first = True
                    for rows, a, b, at in ((P, 0, TP, 0), (P, P, TP, TP), (NS, TP, T, 384)):
                        for t in range(2):
                            pe.matmul(X[0][0:rows, at:at + b - a], qkv[:, q + 2 + t, a:a + rows], qkv[:, q + t, a:b],
                                      start=first, stop=t == 1, skip_group_check=True)
                            first = False
                    pe.wait_ge(small_in, 16 * 4)
                    for t in range(2):
                        ins = pe.matmul(X[1][:, 9 * t:9 * t + 9], nrow[:, h * DK + t * P:h * DK + (t + 1) * P],
                                        ident[0:9, 0:9], start=t == 0, stop=True, skip_group_check=True)
                ins.then_inc(filled, 1)

            slab(S_QKV + 7, op_hi, op_lo, None, lambda c: token_gates() if c == 0 else prep(0, c - 1) if c <= TT + 2 else None)

            def head_norm_sum(h):
                use = X3_USES[f"ms{h}"]
                pe.wait_ge(hss_ok, h + 1)
                pe.wait_ge(x3_read, use - 1)
                pe.matmul(X[3][:, 0:T], ones[:, :], hss[:, :], start=True, stop=True).then_inc(x3_filled, 1)

            def samples_turned(h):
                pe.wait_ge(hs_kept, h + 1)
                for n in range(4):
                    ins = turn(X[2][:, n * NS:(n + 1) * NS], hs[0:NS, n * P:(n + 1) * P], NS)
                ins.then_inc(x2_turned, 1)

            for h in range(HEADS):
                p = h % 2
                pe.wait_ge(prep_ok, h + 1)
                if h:
                    pe.wait_ge(x3_read, X3_USES[f"den{h}"] - 1)
                pe.matmul(X[3][:, 0:TP], ones[:, :], ST[:, 0:TP], start=True, stop=False, skip_group_check=True)
                pe.matmul(X[3][:, P:TP], ones[:, :], ST[:, TP:384], start=False, stop=False, skip_group_check=True)
                pe.matmul(X[3][:, TP:T], ones[0:NS, :], ST[0:NS, 384:448], start=False, stop=False, skip_group_check=True)
                for t in range(2):
                    ins = pe.matmul(X[3][:, TP:T], ones[:, :], qn[:, t, :], start=False, stop=t == 1, skip_group_check=True)
                ins.then_inc(x3_filled, 1)
                bank_free(("num", h, 0))
                for n in range(4):
                    w = slice(n * P, (n + 1) * P)
                    at = (n % 2) * TP
                    pe.matmul(X[n // 2][:, at:at + TP], kvp[:, 0, w], ST[:, 0:TP], start=n % 2 == 0, stop=False,
                              skip_group_check=True)
                    ins = pe.matmul(X[n // 2][:, at + P:at + TP], kvp[:, 1, w], ST[:, TP:384], start=False, stop=True,
                                    skip_group_check=True)
                ins.then_inc(filled, 1)
                if h:
                    samples_turned(h - 1)
                pe.wait_ge(kw_ok, 2 * h + 2)
                pe.wait_ge(x3_read, X3_USES[f"n{h}"] - 1)
                for t in range(TT):
                    ins = pe.matmul(X[3][0:1 + NSEQ, 0:DK], seqmask[0:ROWS[t], t, :],
                                    kvp[:, t, DV:] if t < 2 else kvs[0:NS, p, DV:], start=t == 0, stop=t == TT - 1)
                ins.then_inc(x3_filled, 1)
                for c in range(CH):
                    s = S_O + h
                    pe.wait_ge(w_lo_ok, chunk_no(s, c) + 1)
                    free = (lambda m: pe.wait_ge(evicted, tiles_out(s - 1, m))) if c == 0 else None
                    chunk(c % RING, op_hi, op_lo, CK * c, c == 0, c == CH - 1, free)
                    if c == 0:
                        bank_free(("updp", h, 0))
                        for t in range(2):
                            for i in range(2):
                                ins = pe.matmul(X[t][:, :], kvp[:, i, DV + t * P:DV + (t + 1) * P], kvp[:, i, 0:DV],
                                                start=i == 0, stop=i == 1)
                        ins.then_inc(filled, 1)
                        if h:
                            pe.wait_ge(att_s, h)
                        pe.matmul(X[2][0:NS, :], ST[0:NS, 384:448], kvs[0:NS, p, 0:DV], start=True, stop=False)
                        pe.wait_ge(qwm_ok, h + 1)
                    if h and c == 2:
                        head_norm_sum(h - 1)
                    if h + 1 < HEADS and 1 <= c <= TT + 2:
                        prep(h + 1, c - 1)
                    pe.wait_ge(c_in[c_slot(c)], 16 * c_loads(h, c))
                    for t in range(2):
                        ins = pe.matmul(X[2][0:NS, :], qwm[:, t, c * NS:(c + 1) * NS], cst[:, c_slot(c), t, :],
                                        start=False, stop=c == CH - 1 and t == 1)
                    if c == CH - 1:
                        ins.then_inc(x2_filled, 1)
                    bank_free(("upd", h, c))
                    pe.wait_ge(v_lo_ok, h + 1)
                    pe.wait_ge(kwb_ok, NSEQ * h + c + 1)
                    for t in range(2):
                        for n, v2 in enumerate((v_hi, v_lo)):
                            ins = pe.matmul(X[t][:, :], kwb[:, c % 2, t * P:(t + 1) * P], v2[:, :], start=n == 0, stop=n == 1)
                    ins.then_inc(filled, 1)
            samples_turned(HEADS - 1)
            slab(S_OUT, a_hi, a_lo, lambda k: pe.wait_ge(att_lo_ok, k + 1),
                 lambda c: head_norm_sum(HEADS - 1) if c == 2 else None)
            with pe.Fori(1, MT) as j:
                slab(S_OUT + j, a_hi, a_lo)
            ffn(1, S_FFN1, 2)
            for j in range(MT):
                slab(S_END - MT + j, a_hi, a_lo, down_ready(KT * (2 * SLICES - 1)))
                pe.wait_ge(y_ok, (j + 1) * MT)
                if j:
                    pe.wait_ge(y_kept_a, 2 * j)
                    pe.wait_ge(y_kept_d, j)
                for t in range(TT):
                    for m in range(MT):
                        ins = turn(X[t][0:ROWS[t], m * P:(m + 1) * P], yT[:, j * MT + m, tok(t)])
                ins.then_inc(y_turned, 1)
            pe.wait_ge(ssq_ok, 4 * KT)
            for t in range(TT):
                ins = pe.matmul(X[3][0:ROWS[t], t:t + 1], acc[:, tok(t)], ones[:, 0:1], start=t == 0, stop=True,
                                skip_group_check=True)
            ins.then_inc(r_sum, 1)


_INS = ["x_prompt", "x_sample", "state_pool", "state_mlstm_C", "state_mlstm_n", "state_mlstm_m", "norm_mix",
        "norm_ffn", "norm_final", "pool_w", "pool_scale", "mlstm_w_in", "mlstm_b_gate", "mlstm_head_norm",
        "mlstm_w_out", "ffn_w_up", "ffn_w_down"]
_OUTS = [("y_prompt", (1, TP, D)), ("y_sample", (NSEQ, TS, D)), ("pool_prompt", (1, 1, PAD, D)),
         ("pool_sample", (1, NSEQ, PAD, D)), ("C_prompt", (1, 1, HEADS, DK, DV)), ("n_prompt", (1, 1, HEADS, DK)),
         ("m_prompt", (1, 1, HEADS)), ("C_sample", (1, NSEQ, HEADS, DK, DV)), ("n_sample", (1, NSEQ, HEADS, DK)),
         ("m_sample", (1, NSEQ, HEADS))]


def kernel(**inputs):
    import concourse.bacc as bacc
    from concourse.bass_utils import run_bass_kernel_spmd

    nc = bacc.Bacc("TRN2", target_bir_lowering=False, num_devices=1)
    arrays, ins, outs = {}, {}, {}
    for name in _INS:
        a = np.ascontiguousarray(inputs[name])
        arrays[f"in_{name}"] = a
        ins[name] = nc.dram_tensor(f"in_{name}", a.shape, F32, kind="ExternalInput").ap()
    for name, shape in _OUTS:
        outs[name] = nc.dram_tensor(f"out_{name}", shape, F32, kind="ExternalOutput").ap()
    build(nc, ins, outs)
    r = run_bass_kernel_spmd(nc, [arrays], core_ids=[0])
    return tuple(r.results[0][f"out_{name}"] for name, _ in _OUTS)
```

```python
from contextlib import ExitStack

import numpy as np

import concourse.bass as bass
from concourse import mybir

F32 = mybir.dt.float32
F32R = mybir.dt.float32r
ACT = mybir.ActivationFunctionType
ALU = mybir.AluOpType

P = 128
D = 2048
KT = D // P
TP, NSEQ, TS = 256, 8, 8
NS = NSEQ * TS
T = TP + NS
TT = 3
ROWS = (P, P, NS)
EPS = 1e-6

RING = 4
CK = 2
NC = 512
MT = NC // P
CH = KT // CK
LEAD = 3

GROUPS = 4
PAD = 15
B0, B1, BS, BP = 0, P + 16, 2 * P + 16, 2 * P + 16 + NS
B_ALL = BP + NS

HEADS, DK, DV = 4, 256, 512
QSCALE = DK ** -0.5
CAP = 15.0
NEG = -1e30
GP = 32
D_FF = 4 * D
SLICES = D_FF // D

V_MIX, V_FFN, V_FIN, V_SCALE, V_HEAD, V_ALL = 0, 32, 64, 80, 96, 112

S_FFN0, S_QKV, S_O, S_OUT, S_FFN1, S_END = 0, 32, 40, 44, 48, 80

R_NEGM, R_E, R_WI, R_DEC, R_WK, R_ALL = 0, T, 2 * T, 2 * T + NS, 2 * T + NS + 16, 3 * T + NS + 16
BC = T + NS + 16


def chunk_no(s, c):
    return s * CH + (2 * GROUPS + c)


def used(s, c):
    return s * (CH + MT - 1) + (5 * GROUPS + (c + 1 if c < CH - 1 else CH + MT - 1))


def tile_done(s, m):
    return s * (CH + MT - 1) + (5 * GROUPS + CH + m)


def pool_used(g, c):
    return 5 * g + (1 if c == 0 else 5)


def pool_tile(g, m):
    return 5 * g + 2 + m


def used_before(s, c):
    if c >= RING:
        return used(s, c - RING)
    if isinstance(s, int) and s == 0:
        return pool_used((RING + c) // 2, c % 2)
    return used(s - 1, c + CH - RING)


def tiles_out(s, m):
    return s * MT + (MT * GROUPS + m + 1)


def fill_list():
    prep = lambda h: [("turn", h, t) for t in range(TT)] + [("rows", h, 0), ("score", h, 0)]
    out = [("cols", 0, 0)] + prep(0)
    for h in range(HEADS):
        out += [("num", h, 0), ("updp", h, 0)]
        pieces = prep(h + 1) if h + 1 < HEADS else []
        for b in range(NSEQ):
            if 1 <= b <= len(pieces):
                out.append(pieces[b - 1])
            out.append(("upd", h, b))
    return out


FILL = {f: n + 1 for n, f in enumerate(fill_list())}
ACT_FILL = {f: n + 1 for n, f in enumerate([f for f in fill_list() if f[0] in ("turn", "rows", "updp")])}
X3_USES = {u: n + 1 for n, u in enumerate(["den0", "n0", "den1", "n1", "ms0", "den2", "n2", "ms1", "den3", "n3", "ms2", "ms3"])}


def item(b):
    return 0 if b == "prompt" else b + 1


def c_slot(b):
    return item(b) % 3


def c_loads(h, b):
    return (3 if c_slot(b) else 2) * h + b // 3 + 1


def c_stores(h, b):
    return 3 * h + item(b) // 3 + 1


WARM = (6, 4, 9)

ACT_HALVES = ((0, 0), (0, 1), (2, 0))
DVE_HALVES = ((1, 0), (1, 1), (2, 1))


def bc(ap, shape):
    return ap.unsqueeze(1).broadcast_to(shape)


def build(nc, A, O):
    with ExitStack() as ctx:
        def sb(name, shape, dt=F32, where=ctx):
            return where.enter_context(nc.sbuf_tensor(name, shape, dt))

        def head_rows(name, shape, where=ctx):
            full = sb(name, [GP + HEADS] + shape, F32, where)
            return full[GP:GP + HEADS, :] if len(shape) == 1 else full[GP:GP + HEADS, :, :]

        def sem(name):
            return ctx.enter_context(nc.semaphore(name))

        hT = sb("hT", [P, KT, T])
        w_raw = sb("w_raw", [P, RING, CK, NC])
        w_hi = sb("w_hi", [P, RING, CK, NC], F32R)
        w_lo = sb("w_lo", [P, RING, CK, NC], F32R)
        ident = sb("ident", [P, P])
        ones = sb("ones", [P, P])
        causal = sb("causal", [P, P])
        causal_s = sb("causal_s", [P, NS])
        seqmask = sb("seqmask", [P, TT, 1 + NSEQ])
        sel = head_rows("sel", [HEADS, P])
        vrow = sb("vrow", [P, P])
        vecs = sb("vecs", [P, V_ALL])
        Rb = sb("Rb", [P, T])
        rv = sb("rv", [P, T])
        acc = sb("acc", [P, T])
        sqt = sb("sqt", [P, T])
        xcol = sb("xcol", [P, 4])
        rcol = sb("rcol", [P, 4])
        bgate = head_rows("bgate", [2])
        m0 = head_rows("m0", [NSEQ])
        mnew = head_rows("mnew", [1 + NSEQ])

        with ExitStack() as r:
            xrow = sb("xrow", [P, TT, D], F32, r)
            gain = sb("gain", [P, D], F32, r)
        with ExitStack() as r:
            yT = sb("yT", [P, KT, T], F32, r)
        op_hi = sb("op_hi", [P, KT, T], F32R)
        op_lo = sb("op_lo", [P, KT, T], F32R)

        with ExitStack() as r:
            qkv = sb("qkv", [P, 2 * KT, T], F32, r)
        a_hi = sb("a_hi", [P, KT, T], F32R)
        a_lo = sb("a_lo", [P, KT, T], F32R)

        with ExitStack() as r:
            band = sb("band", [P, GROUPS, B_ALL], F32, r)
            srow = sb("srow", [P, D], F32, r)
            junk = sb("junk", [P, D], F32, r)
            u = sb("u", [P, TT, D], F32, r)
        with ExitStack() as r:
            with ExitStack() as r2:
                gw_raw = sb("gw_raw", [P, KT, 2 * HEADS], F32, r2)
                gw_hi = sb("gw_hi", [P, KT, 68], F32R, r2)
                gw_lo = sb("gw_lo", [P, KT, 68], F32R, r2)
            with ExitStack() as r2:
                scan_p = [head_rows(f"scan_p{i}", [P + TP], r2) for i in range(2)]
                scan_s = [head_rows(f"scan_s{i}", [NSEQ, 4 + TS], r2) for i in range(2)]
                pad_ = sb("pad_", [P, 1500], F32, r2)
                grow = head_rows("grow", [T], r2)
                nbrow = head_rows("nbrow", [T], r2)
                mrow = head_rows("mrow", [T], r2)
                gz = head_rows("gz", [2, T], r2)
            pad2 = sb("pad2", [P, 4608], F32, r)
            relu = sb("relu", [P, MT, T], F32, r)
            sq = sb("sq", [P, 2, T], F32, r)
            yrow = sb("yrow", [P, TT, D], F32, r)
        with ExitStack() as r:
            kvp = sb("kvp", [P, 2, DV + DK], F32, r)
            kvs = sb("kvs", [P, 2, DV + DK], F32, r)
            v_hi = sb("v_hi", [P, DV], F32R, r)
            v_lo = sb("v_lo", [P, DV], F32R, r)
            kwb = sb("kwb", [P, 2, DK], F32R, r)
            cst = sb("cst", [P, 3, 2, DV], F32, r)
            ST = sb("ST", [P, 448], F32, r)
            EW = sb("EW", [P, 2, BC], F32, r)
            hs = sb("hs", [P, DV], F32, r)
            eb = hs[:, 0:448]
            qw = sb("qw", [P, 2, NS], F32, r)
            qn = sb("qn", [P, 2, NS], F32, r)
            qwm = sb("qwm", [P, 2, NSEQ * (NS + TS)], F32, r)
            nts = sb("nts", [P, 2 * (1 + NSEQ)], F32, r)
            rden_odd = sb("rden_odd", [P, T], F32, r)
            gates_n = sb("gates_n", [GP + HEADS, R_ALL], F32, r)
            nrow = gates_n[0:1 + NSEQ, 0:HEADS * DK]
            gates = gates_n[GP:GP + HEADS, :]
            cols = sb("cols", [P, 6, HEADS], F32, r)
            dect = sb("dect", [1 + NSEQ, HEADS], F32, r)
        rden, r2b, hss = (rv, rden_odd), sqt, acc

        G = ctx.enter_context(nc.psum_tensor("G", [P, MT, 512], F32))
        X = [ctx.enter_context(nc.psum_tensor(f"X{i}", [P, 512], F32)) for i in range(4)]

        x_in = [sem(f"x_in{t}") for t in range(TT)]
        state_in = [sem(f"state_in{i}") for i in range(2)]
        gain_in = [sem(f"gain_in{i}") for i in range(2)]
        vecs_in = sem("vecs_in")
        small_in = sem("small_in")
        w_in = [sem(f"w_in{i}") for i in range(RING)]
        c_in = [sem(f"c_in{i}") for i in range(3)]
        c_out = [sem(f"c_out{i}") for i in range(3)]
        pool_out = sem("pool_out")
        outs = sem("outs")
        y_out = sem("y_out")
        consts = sem("consts")
        w_hi_ok = sem("w_hi_ok")
        w_lo_ok = sem("w_lo_ok")
        gemm = sem("gemm")
        evicted = sem("evicted")
        x_sq = sem("x_sq")
        x_turned = sem("x_turned")
        x_kept_a = sem("x_kept_a")
        x_kept_d = sem("x_kept_d")
        band_drawn = sem("band_drawn")
        band_ok = sem("band_ok")
        r0_inv = sem("r0_inv")
        r0_ok = sem("r0_ok")
        r_sum = sem("r_sum")
        r_inv = sem("r_inv")
        r_ok = sem("r_ok")
        dve = sem("dve_chain")
        pool_c = sem("pool_chain")
        act_c = sem("act_chain")
        vec_turned = sem("vec_turned")
        vecs_ok = sem("vecs_ok")
        u_ok = sem("u_ok")
        d_ok = sem("d_ok")
        d_hi_ok = sem("d_hi_ok")
        d_lo_ok = sem("d_lo_ok")
        op_hi_ok = sem("op_hi_ok")
        op_lo_ok = sem("op_lo_ok")
        sq_ok = sem("sq_ok")
        ssq_ok = sem("ssq_ok")
        a_hi_ok = sem("a_hi_ok")
        a_sq_ok = sem("a_sq_ok")
        a_lo_ok = sem("a_lo_ok")
        gw_hi_ok = sem("gw_hi_ok")
        gw_lo_ok = sem("gw_lo_ok")
        gates_sum = sem("gates_sum")
        gz_ok = sem("gz_ok")
        tanh_ok = sem("tanh_ok")
        g_ok = sem("g_ok")
        m_ok = sem("m_ok")
        rows_ok = sem("rows_ok")
        gates_exp = sem("gates_exp")
        filled = sem("filled")
        drained = sem("drained")
        drained_a = sem("drained_a")
        eb_exp = sem("eb_exp")
        prep_ok = sem("prep_ok")
        x3_filled = sem("x3_filled")
        x3_read = sem("x3_read")
        x2_filled = sem("x2_filled")
        att_s = sem("att_s")
        kw_ok = sem("kw_ok")
        hss_ok = sem("hss_ok")
        ez_ok = sem("ez_ok")
        v_hi_ok = sem("v_hi_ok")
        v_lo_ok = sem("v_lo_ok")
        kwb_hi_ok = sem("kwb_hi_ok")
        kwb_ok = sem("kwb_ok")
        qwm_ok = sem("qwm_ok")
        hs_kept = sem("hs_kept")
        x2_turned = sem("x2_turned")
        r2_inv = sem("r2_inv")
        r2_ok = sem("r2_ok")
        att_ok = sem("att_ok")
        att_hi_ok = sem("att_hi_ok")
        att_lo_ok = sem("att_lo_ok")
        y_ok = sem("y_ok")
        y_turned = sem("y_turned")
        y_kept_a = sem("y_kept_a")
        y_kept_d = sem("y_kept_d")
        sq_end = sem("sq_end")
        y_done_a = sem("y_done_a")
        y_done_d = sem("y_done_d")

        w_up = [A["ffn_w_up"][i].rearrange("(c t p) n -> c p t n", t=CK, p=P) for i in range(2)]
        w_down = [A["ffn_w_down"][i].rearrange("(s c t p) n -> s c p t n", c=CH, t=CK, p=P) for i in range(2)]
        w_qkvo = A["mlstm_w_in"][0].rearrange("(c t p) n -> c p t n", t=CK, p=P)
        w_out = A["mlstm_w_out"][0].rearrange("(c t p) n -> c p t n", t=CK, p=P)
        w_pool = A["pool_w"][0].rearrange("g (c t p) n -> g c p t n", t=CK, p=P)
        w_gate = A["mlstm_w_in"][0].rearrange("(k p) n -> p k n", p=P)[:, :, 2 * HEADS * DK + 2 * D:]
        c_dram = A["state_mlstm_C"][0].rearrange("b h (t p) n -> b h p t n", p=P)
        c_new = O["C_sample"][0].rearrange("b h (t p) n -> b h p t n", p=P)
        c_new_p = O["C_prompt"][0, 0].rearrange("h (t p) n -> h p t n", p=P)

        def vec(n):
            return vecs[:, n:n + 1]

        def tok(t):
            return slice(t * P, t * P + ROWS[t])

        def head_block(h):
            return 4 * h

        def z_block(h):
            return 0 if h < 3 else 12

        def sq_block(h):
            return 4 if h < 3 else 8

        def att(h):
            return qkv[:, KT + 4 * h:KT + 4 * h + 4, :]

        def seqs(row, a=0):
            return row[:, a + TP:a + T].rearrange("h (b t) -> h b t", t=TS)

        def scan(eng, link, op):
            for n in range(8):
                w, a, b = 1 << n, scan_p[n % 2], scan_p[1 - n % 2]
                link(eng.tensor_tensor(b[:, P:], a[:, P:], a[:, P - w:P + TP - w], op))
            for n in range(3):
                w, a, b = 1 << n, scan_s[n % 2], scan_s[1 - n % 2]
                link(eng.tensor_tensor(b[:, :, 4:], a[:, :, 4:], a[:, :, 4 - w:4 + TS - w], op))

        block = ctx.enter_context(nc.Block())

        @block.sync
        def _(sp):
            state = A["state_pool"][0].rearrange("b r d -> (b r) d")
            parts = (slice(0, NC), slice(NC, D))
            for t in range(TT):
                src = A["x_prompt"][0, t * P:(t + 1) * P, :] if t < 2 else A["x_sample"].rearrange("b t d -> (b t) d")
                if t == 2:
                    sp.dma_start(gain[:, parts[0]], A["norm_mix"][0:1, parts[0]].broadcast_to([P, NC])).then_inc(gain_in[0], 16)
                sp.dma_start(xrow[0:ROWS[t], t, :], src).then_inc(x_in[t], 16)
            sp.dma_start(srow[0:NSEQ * PAD, parts[0]], state[:, parts[0]]).then_inc(state_in[0], 16)
            sp.dma_start(gain[:, parts[1]], A["norm_mix"][0:1, parts[1]].broadcast_to([P, D - NC])).then_inc(gain_in[1], 16)
            sp.dma_start(srow[0:NSEQ * PAD, parts[1]], state[:, parts[1]]).then_inc(state_in[1], 16)
            for name, at in (("norm_mix", V_MIX), ("norm_ffn", V_FFN), ("norm_final", V_FIN),
                             ("pool_scale", V_SCALE), ("mlstm_head_norm", V_HEAD)):
                src = A[name]
                src = src.rearrange("(k p) -> k p", p=P) if len(src.shape) == 1 else src.rearrange("l (k p) -> (l k) p", p=P)
                sp.dma_start(vrow[at:at + src.shape[0], :], src).then_inc(vecs_in, 16)

            def load(s, c, src):
                sp.wait_ge(w_lo_ok, chunk_no(s, c) - RING + 1)
                sp.dma_start(w_raw[:, c % RING], src).then_inc(w_in[c % RING], 16)

            def state_load(h, b):
                if b > 1:
                    sp.wait_ge(c_out[c_slot(b)], 16 * (c_stores(h, b) - 1))
                elif h:
                    sp.wait_ge(c_out[c_slot(b)], 16 * c_stores(h - 1, b + 6))
                sp.dma_start(cst[:, c_slot(b)], c_dram[b, h]).then_inc(c_in[c_slot(b)], 16)

            def state_store(h, b):
                if b == "prompt":
                    sp.wait_ge(drained, FILL["updp", h, 0])
                    sp.wait_ge(drained_a, ACT_FILL["updp", h, 0])
                    sp.dma_start(c_new_p[h], cst[:, 0]).then_inc(c_out[0], 16)
                else:
                    sp.wait_ge(drained, FILL["upd", h, b])
                    sp.dma_start(c_new[b, h], cst[:, c_slot(b)]).then_inc(c_out[c_slot(b)], 16)

            for g in range(GROUPS):
                for c in range(2):
                    n = 2 * g + c
                    if n >= RING:
                        sp.wait_ge(w_lo_ok, n - RING + 1)
                    sp.dma_start(w_raw[:, n % RING], w_pool[g, c]).then_inc(w_in[n % RING], 16)
                if g == 2:
                    sp.wait_ge(u_ok, TT * GROUPS)
                    sp.dma_start(O["pool_prompt"][0, 0], u[P - PAD:P, 1, :]).then_inc(pool_out, 16)
                    for b in range(NSEQ):
                        sp.dma_start(O["pool_sample"][0, b, PAD - TS:, :], u[b * TS:(b + 1) * TS, 2, :]).then_inc(pool_out, 16)
                    sp.dma_start(O["pool_sample"][0, :, 0:PAD - TS, :], A["state_pool"][0, :, TS:PAD, :]).then_inc(pool_out, 16)

            def ffn(layer, s0):
                with sp.Fori(0, SLICES) as sl:
                    with sp.Fori(0, MT) as j:
                        for c in range(CH):
                            load(s0 + sl * 8 + j, c, w_up[layer][c][:, :, bass.ds(sl * D + j * NC, NC)])
                    with sp.Fori(0, MT) as j:
                        for c in range(CH):
                            load(s0 + 4 + sl * 8 + j, c, w_down[layer][sl, c][:, :, bass.ds(j * NC, NC)])

            ffn(0, S_FFN0)
            with sp.Fori(0, 8) as j:
                for c in range(CH):
                    load(S_QKV + j, c, w_qkvo[c][:, :, bass.ds(j * NC, NC)])
            sp.wait_ge(op_lo_ok, 2 * KT)
            sp.wait_ge(a_lo_ok, SLICES * KT)
            for b in range(2):
                state_load(0, b)
            for q in range(HEADS + 1):
                for c in range(CH):
                    if q < HEADS:
                        load(S_O + q, c, w_qkvo[c][:, :, (8 + q) * NC:(9 + q) * NC])
                    else:
                        load(S_OUT, c, w_out[c][:, :, 0:NC])
                    if q == 0:
                        continue
                    if c == 0:
                        state_store(q - 1, "prompt")
                        state_load(q - 1, 2)
                    state_store(q - 1, c)
                    if c + 3 < NSEQ:
                        state_load(q - 1, c + 3)
                    elif c > 5 and q < HEADS:
                        state_load(q, c - 6)
            with sp.Fori(1, MT) as j:
                for c in range(CH):
                    load(S_OUT + j, c, w_out[c][:, :, bass.ds(j * NC, NC)])
            ffn(1, S_FFN1)
            for n, halves in enumerate(zip(ACT_HALVES, DVE_HALVES)):
                for done, (t, half) in zip((y_done_a, y_done_d), halves):
                    sp.wait_ge(done, n + 1)
                    y = O["y_prompt"][0, t * P:(t + 1) * P, :] if t < 2 else O["y_sample"].rearrange("b t d -> (b t) d")
                    cut = slice(half * D // 2, (half + 1) * D // 2)
                    sp.dma_start(y[:, cut], yrow[0:ROWS[t], t, cut]).then_inc(y_out, 16)
            for i in range(3):
                sp.wait_ge(c_out[i], 16 * 3 * HEADS)
            sp.wait_ge(pool_out, 16 * (2 + NSEQ))
            sp.wait_ge(outs, 16 * 4)
            sp.wait_ge(y_out, 16 * 2 * TT)

        @block.gpsimd
        def _(pool):
            n_chain = [0]

            def link(ins):
                n_chain[0] += 1
                ins.then_inc(pool_c, 1)
                pool.wait_ge(pool_c, n_chain[0])

            def select(ap, pattern, cm, base=0, op=ALU.is_ge, fill=0.0):
                link(pool.affine_select(out=ap, in_=ap, compare_op=op, fill=fill, base=base, pattern=pattern,
                                        channel_multiplier=cm))

            link(pool.memset(rcol[:, :], 1.0))
            link(pool.memset(ident[:, :], 0.0))
            pool.affine_select(out=ident[:, :], in_=ident[:, :], compare_op=ALU.not_equal, fill=1.0, base=0,
                               pattern=[[-1, P]], channel_multiplier=1).then_inc(consts, 1)
            pool.wait_ge(consts, 1)
            for g in range(GROUPS):
                w = 2 << g
                link(pool.memset(band[:, g, :], 1.0 / w))
                for n in range(w - 1):
                    link(pool.memset(band[:, g, n:n + 1], 1.0 / (n + 1)))
                for at, n in ((B0, P + 16), (B1, P), (BS, NS)):
                    select(band[:, g, at:at + n], [[1, n]], -1)
                    if w < TS or n > NS:
                        select(band[:, g, at:at + n], [[-1, n]], 1, base=w - 1)
                same = band[:, g, BS:BS + NS].rearrange("p (b t) -> p b t", t=TS)
                select(same, [[-TS, NSEQ], [0, TS]], 1)
                past = band[:, g, BP:BP + NS].rearrange("p (b t) -> p b t", t=TS)
                select(past, [[-PAD, NSEQ], [-1, TS]], 1, base=w - 16)
                pool.affine_select(out=past, in_=past, compare_op=ALU.is_ge, fill=0.0, base=PAD - 1,
                                   pattern=[[PAD, NSEQ], [0, TS]], channel_multiplier=-1).then_inc(band_drawn, 1)
            link(pool.memset(ones[:, :], 1.0))
            link(pool.memset(causal[:, :], 0.0))
            select(causal[:, :], [[1, P]], -1, fill=NEG)
            link(pool.memset(causal_s[:, :], 0.0))
            select(causal_s[:, :], [[1, NS]], -1, fill=NEG)
            select(causal_s[:, :].rearrange("p (b t) -> p b t", t=TS), [[-TS, NSEQ], [0, TS]], 1, fill=NEG)
            link(pool.memset(seqmask[:, :, :], 0.0))
            link(pool.memset(seqmask[:, 0:2, 0:1], 1.0))
            link(pool.memset(seqmask[:, 2, 1:], 1.0))
            for at in (0, NS):
                select(seqmask[at:at + NS, 2, 1:], [[-TS, NSEQ]], 1)
                select(seqmask[at:at + NS, 2, 1:], [[TS, NSEQ]], -1, base=TS - 1)
            link(pool.memset(sel[:, :, :], 0.0))
            select(sel[:, :, :], [[-1, HEADS], [0, P]], 1, op=ALU.not_equal, fill=1.0)
            with nc.allow_non_contiguous_dma("a few values"):
                pool.dma_start(bgate[:, :], A["mlstm_b_gate"][0].rearrange("(g h) -> h g", h=HEADS)).then_inc(small_in, 16)
                pool.dma_start(m0[:, :], A["state_mlstm_m"][0].rearrange("b h -> h b")).then_inc(small_in, 16)

            def squares(j, base, tiles=KT):
                if j:
                    pool.wait_ge(r_inv, 2 * j)
                link(pool.memset(acc[:, :], 0.0))
                for k in range(tiles):
                    pool.wait_ge(evicted, base + k + 1)
                    pool.tensor_tensor(sqt[:, :], hT[:, k, :], hT[:, k, :], ALU.mult).then_inc(sq_ok, 1)
                    pool.wait_ge(sq_ok, KT * j + k + 1)
                    pool.tensor_tensor(acc[:, :], acc[:, :], sqt[:, :], ALU.add).then_inc(ssq_ok, 1)
                    pool.wait_ge(ssq_ok, KT * j + k + 1)

            squares(0, 0)
            def ffn(layer, s0):
                f0 = 16 * SLICES * layer
                with pool.Fori(0, SLICES) as sl:
                    with pool.Fori(0, MT) as j:
                        hidden_tiles(f0 + sl * KT + j * MT, s0 + sl * 8 + j, j * MT)

            def hidden_tiles(first, s, k0):
                for m in range(MT):
                    hi = a_hi[:, bass.ds(k0 + m, 1), :]
                    lo = a_lo[:, bass.ds(k0 + m, 1), :]
                    pool.wait_ge(evicted, tiles_out(s, m))
                    pool.tensor_tensor(sq[:, m % 2], relu[:, m], relu[:, m], ALU.mult).then_inc(a_sq_ok, 1)
                    pool.wait_ge(a_sq_ok, first + m + 1)
                    pool.wait_ge(a_hi_ok, first + m + 1)
                    pool.tensor_tensor(lo, sq[:, m % 2:m % 2 + 1], hi.bitcast(F32), ALU.subtract).then_inc(a_lo_ok, 1)

            pool.wait_ge(d_lo_ok, KT)
            pool.wait_ge(pool_out, 16 * (2 + NSEQ))
            with nc.allow_non_contiguous_dma("8 columns"):
                pool.dma_start(gw_raw[:, :, :], w_gate).then_inc(small_in, 16)
            pool.memset(gw_hi[:, :, :].bitcast(F32), 0.0).then_inc(gw_lo_ok, 1)
            pool.memset(gw_lo[:, :, :].bitcast(F32), 0.0).then_inc(gw_lo_ok, 1)

            ffn(0, S_FFN0)
            pool.wait_ge(gw_hi_ok, 2)
            pool.wait_ge(gw_lo_ok, 2)
            for n, at in enumerate((GP, 64)):
                pool.tensor_tensor(gw_lo[:, :, at:at + HEADS], gw_raw[:, :, n * HEADS:(n + 1) * HEADS],
                                   gw_hi[:, :, at:at + HEADS].bitcast(F32), ALU.subtract).then_inc(gw_lo_ok, 1)
            squares(1, MT * GROUPS + MT * (S_QKV - MT))

            pool.wait_ge(gates_sum, 1)
            for i in range(2):
                link(pool.memset(scan_p[i][:, 0:P], 0.0))
                link(pool.memset(scan_s[i][:, :, 0:4], 0.0))
            pool.dma_start(nrow[1:, :], A["state_mlstm_n"][0].rearrange("b h d -> b (h d)")).then_inc(small_in, 16)
            pool.wait_ge(tanh_ok, 4)

            scan(pool, link, ALU.add)
            link(pool.tensor_copy(nbrow[:, 0:TP], scan_p[0][:, P:]))
            link(pool.tensor_copy(seqs(nbrow), scan_s[1][:, :, 4:]))
            link(pool.tensor_scalar(grow[:, :], grow[:, :], CAP, None, ALU.mult))
            link(pool.tensor_tensor(grow[:, :], grow[:, :], nbrow[:, :], ALU.add))
            for i in range(2):
                link(pool.memset(scan_p[i][:, 0:P], NEG))
                link(pool.memset(scan_s[i][:, :, 0:4], NEG))
            link(pool.tensor_copy(scan_p[0][:, P:], grow[:, 0:TP]))
            pool.tensor_copy(scan_s[0][:, :, 4:], seqs(grow)).then_inc(g_ok, 1)
            pool.wait_ge(m_ok, 2)
            m0b = m0[:, :].unsqueeze(2).broadcast_to([HEADS, NSEQ, TS])
            last_s = seqs(mrow)[:, :, TS - 1]
            last_p = mrow[:, TP - 1:TP]
            link(pool.memset(gates[:, R_DEC:R_WK], 0.0))
            link(pool.tensor_scalar(gates[:, R_NEGM:R_E], mrow[:, :], -1.0, None, ALU.mult))
            link(pool.tensor_tensor(gates[:, R_E:R_WI], nbrow[:, :], mrow[:, :], ALU.subtract))
            link(pool.tensor_tensor(gates[:, R_WI:R_DEC].rearrange("h (b t) -> h b t", t=TS), m0b, seqs(mrow), ALU.subtract))
            link(pool.tensor_scalar(gates[:, R_DEC:R_DEC + 1], last_p, -1.0, None, ALU.mult))
            link(pool.tensor_tensor(gates[:, R_DEC + 1:R_DEC + 1 + NSEQ], m0[:, :], last_s, ALU.subtract))
            link(pool.tensor_tensor(gates[:, R_WK:R_WK + TP], grow[:, 0:TP], last_p.broadcast_to([HEADS, TP]), ALU.subtract))
            link(pool.tensor_tensor(seqs(gates, R_WK), seqs(grow),
                                    last_s.unsqueeze(2).broadcast_to([HEADS, NSEQ, TS]), ALU.subtract))
            link(pool.tensor_tensor(mnew[:, 0:1], last_p, nbrow[:, TP - 1:TP], ALU.subtract))
            link(pool.tensor_tensor(mnew[:, 1:], last_s, seqs(nbrow)[:, :, TS - 1], ALU.subtract))
            link(pool.memset(cols[:, :, :], 0.0))
            link(pool.memset(qwm[:, :, :], 0.0))
            pool.memset(nrow[0:1, :], 0.0).then_inc(rows_ok, 1)
            with nc.allow_non_contiguous_dma("36 values"):
                pool.dma_start(O["m_prompt"][0].rearrange("b h -> h b"), mnew[:, 0:1]).then_inc(outs, 16)
                pool.dma_start(O["m_sample"][0].rearrange("b h -> h b"), mnew[:, 1:]).then_inc(outs, 16)

            def weigh_keys(h):
                pool.wait_ge(drained, FILL["turn", h, 2])
                kp, ks = kvp[:, :, DV:], kvs[:, h % 2, DV:]
                pool.tensor_tensor(kp, kp, cols[:, 1:4:2, h].unsqueeze(2).broadcast_to([P, 2, DK]),
                                   ALU.mult).then_inc(kw_ok, 1)
                pool.tensor_scalar(ks, ks, cols[:, 5, h:h + 1], None, ALU.mult).then_inc(kw_ok, 1)

            def head_squares(h):
                pool.wait_ge(att_s, h + 1)
                s4 = qkv[:, sq_block(h):sq_block(h) + 4, :]
                link(pool.tensor_tensor(s4, att(h), att(h), ALU.mult))
                link(pool.tensor_tensor(s4[:, 0:2], s4[:, 0:2], s4[:, 2:4], ALU.add))
                if h:
                    pool.wait_ge(x3_filled, X3_USES[f"ms{h - 1}"])
                pool.tensor_tensor(hss[:, :], s4[:, 0], s4[:, 1], ALU.add).then_inc(hss_ok, 1)

            weigh_keys(0)
            for h in range(HEADS):
                if h:
                    head_squares(h - 1)
                if h + 1 < HEADS:
                    weigh_keys(h + 1)
            head_squares(HEADS - 1)
            pool.wait_ge(x3_read, X3_USES[f"n{HEADS - 1}"])
            pool.dma_start(O["n_prompt"][0].rearrange("b h d -> b (h d)"), nrow[0:1, :]).then_inc(outs, 16)
            pool.dma_start(O["n_sample"][0].rearrange("b h d -> b (h d)"), nrow[1:, :]).then_inc(outs, 16)
            pool.wait_ge(x3_filled, X3_USES["ms3"])
            pool.wait_ge(att_ok, HEADS)
            pool.wait_ge(hss_ok, HEADS)
            squares(2, MT * GROUPS + MT * S_OUT)
            ffn(1, S_FFN1)
            squares(3, MT * GROUPS + MT * (S_END - MT), KT - MT)

        @block.scalar
        def _(act):
            def split(s, c):
                act.wait_ge(w_in[c % RING], (s * (CH // RING) + 2 + c // RING + 1) * 16)
                act.wait_ge(gemm, used_before(s, c))
                act.activation(w_hi[:, c % RING], w_raw[:, c % RING], ACT.Copy).then_inc(w_hi_ok, 1)

            def split_pool(n):
                act.wait_ge(w_in[n % RING], 16 * (n // RING + 1))
                if n >= RING:
                    act.wait_ge(gemm, pool_used((n - RING) // 2, n % 2))
                act.activation(w_hi[:, n % RING], w_raw[:, n % RING], ACT.Copy).then_inc(w_hi_ok, 1)

            def slab(s, after=None, mid=None, last=False):
                for i in range(CH):
                    c = LEAD + i
                    if c < CH:
                        split(s, c)
                    elif not last:
                        split(s + 1, c - CH)
                    if mid and i in mid:
                        mid[i]()
                for m in range(MT):
                    if after:
                        after(m)

            def root(j, dst, src):
                act.wait_ge(r_inv, 2 * j)
                act.activation(dst, src, ACT.Sqrt).then_inc(r_ok, 1)

            for t in range(TT):
                act.wait_ge(x_in[t], 16)
                act.wait_ge(consts, 1)
                if t:
                    act.wait_ge(x_sq, t)
                act.activation(junk[0:ROWS[t], :], xrow[0:ROWS[t], t, :], ACT.Square,
                               accum_out=xcol[0:ROWS[t], t:t + 1]).then_inc(x_sq, 1)
                for q in range(2):
                    if q == 1:
                        act.wait_ge(r0_inv, 2 * t + 2)
                        r = rcol[0:ROWS[t], t:t + 1]
                        act.activation(r, r, ACT.Sqrt).then_inc(r0_ok, 1)
                    act.wait_ge(x_turned, GROUPS * t + q + 1)
                    act.activation(hT[:, MT * q:MT * q + MT, tok(t)],
                                   G[:, q, 0:MT * ROWS[t]].rearrange("p (a r) -> p a r", r=ROWS[t]),
                                   ACT.Copy).then_inc(x_kept_a, 1)
            split_pool(0)
            split_pool(1)

            def op_split(j, k, scale):
                act.activation(op_hi[:, k, :], hT[:, k, :], ACT.Copy, scale=scale).then_inc(op_hi_ok, 1)

            def d_hi(g):
                for i in range(MT):
                    act.wait_ge(d_ok, MT * g + i + 1)
                    act.activation(a_hi[:, MT * g + i, :], X[i][:, 0:T], ACT.Copy).then_inc(d_hi_ok, 1)

            d_hi(0)
            split_pool(2)
            d_hi(1)
            act.wait_ge(u_ok, TT * GROUPS)
            for g in range(GROUPS):
                for n in (2 * g + LEAD, 2 * g + LEAD + 1):
                    split_pool(n) if n < 8 else split(0, n - 8)
                if g + 2 < GROUPS:
                    d_hi(g + 2)
                for k in range(MT * g, MT * g + MT):
                    act.wait_ge(evicted, k + 1)
                    op_split(0, k, vec(V_FFN + k))

            def hidden(s, first, k0):
                def after(m):
                    act.wait_ge(evicted, tiles_out(s, m))
                    act.activation(a_hi[:, bass.ds(k0 + m, 1), :], relu[:, m:m + 1], ACT.Square).then_inc(a_hi_ok, 1)
                return after

            def norm_op(s, j, col):
                def after(m):
                    act.wait_ge(evicted, tiles_out(s, m))
                    op_split(j, (s % 4) * MT + m, vec(col + (s % 4) * MT + m))
                return after

            def ffn(layer, s0, rj):
                f0 = KT * SLICES * layer
                slab(s0, hidden(s0, f0, 0), {6: lambda: root(rj, Rb[:, :], rv[:, :])})
                with act.Fori(1, MT) as j:
                    slab(s0 + j, hidden(s0 + j, f0 + j * MT, j * MT))
                with act.Fori(0, MT) as j:
                    slab(s0 + 4 + j)
                with act.Fori(1, SLICES - 1) as sl:
                    with act.Fori(0, MT) as j:
                        slab(s0 + sl * 8 + j, hidden(s0 + sl * 8 + j, f0 + sl * KT + j * MT, j * MT))
                    with act.Fori(0, MT) as j:
                        slab(s0 + 4 + sl * 8 + j)
                sl = SLICES - 1
                with act.Fori(0, MT) as j:
                    slab(s0 + sl * 8 + j, hidden(s0 + sl * 8 + j, f0 + sl * KT + j * MT, j * MT))

            ffn(0, S_FFN0, 1)
            for j in range(MT):
                s = S_QKV - MT + j
                slab(s, norm_op(s, 1, V_MIX + KT))
                if j == 0:
                    act.wait_ge(small_in, 48)
                    act.wait_ge(gw_lo_ok, 2)
                    for n, at in enumerate((GP, 64)):
                        act.activation(gw_hi[:, :, at:at + HEADS], gw_raw[:, :, n * HEADS:(n + 1) * HEADS],
                                       ACT.Copy).then_inc(gw_hi_ok, 1)
            slab(S_QKV, None, {6: lambda: root(2, Rb[:, :], rv[:, :])})
            act.wait_ge(gz_ok, 3)
            act.activation(grow[:, :], gz[:, 0, :], ACT.Tanh, scale=1.0 / CAP, bias=bgate[:, 0:1]).then_inc(tanh_ok, 1)
            act.activation(gz[:, 1, :], gz[:, 1, :], ACT.Tanh, scale=1.0 / CAP, bias=bgate[:, 1:2]).then_inc(act_c, 1)
            act.wait_ge(act_c, 1)
            act.activation(gz[:, 1, :], gz[:, 1, :], ACT.Exp, scale=-CAP).then_inc(tanh_ok, 1)
            act.wait_ge(tanh_ok, 2)
            act.activation(scan_p[0][:, P:], gz[:, 1, 0:TP], ACT.Ln, bias=1.0).then_inc(tanh_ok, 1)
            act.activation(scan_s[0][:, :, 4:], gz[:, 1, TP:].rearrange("h (b t) -> h b t", t=TS), ACT.Ln,
                           bias=1.0).then_inc(tanh_ok, 1)
            with act.Fori(1, 7) as j:
                slab(S_QKV + j)
            act.wait_ge(rows_ok, 1)
            act.activation(gates[:, R_E:], gates[:, R_E:], ACT.Exp).then_inc(gates_exp, 1)

            def prep(h, i):
                p = h % 2
                if i < TT:
                    act.wait_ge(filled, FILL["turn", h, i])
                    dst = kvp[:, i, 0:DV] if i < 2 else kvs[:, p, 0:DV]
                    act.activation(dst, X[0][:, :], ACT.Copy).then_inc(drained_a, 1)
                elif i == TT:
                    act.wait_ge(filled, FILL["rows", h, 0])
                    act.activation(EW[:, p, :], X[1][:, 0:BC], ACT.Copy).then_inc(drained_a, 1)
                    act.wait_ge(drained, FILL["rows", h, 0])
                    act.activation(eb[:, 0:384], eb[:, 0:384], ACT.Exp).then_inc(eb_exp, 1)
                    act.activation(eb[0:NS, 384:448], eb[0:NS, 384:448], ACT.Exp).then_inc(eb_exp, 1)

            slab(S_QKV + 7, None, {i + 1: (lambda i=i: prep(0, i)) for i in range(TT + 1)})

            def root2(h):
                act.wait_ge(r2_inv, h + 1)
                act.activation(r2b[:, :], r2b[:, :], ACT.Sqrt).then_inc(r2_ok, 1)

            def key_hi(h, b):
                if b > 1:
                    act.wait_ge(filled, FILL["upd", h, b - 2])
                act.activation(kwb[:, b % 2, :], kvs[:, h % 2, DV:], ACT.Copy,
                               scale=seqmask[:, 2, 1 + b:2 + b]).then_inc(kwb_hi_ok, 1)

            def att_hi(k):
                act.wait_ge(att_ok, k // 4 + 1)
                act.activation(a_hi[:, k, :], qkv[:, KT + k, :], ACT.Copy).then_inc(att_hi_ok, 1)

            for h in range(HEADS):
                if h:
                    act.wait_ge(filled, FILL["upd", h - 1, NSEQ - 1])
                act.wait_ge(drained_a, ACT_FILL["turn", h, 2])
                act.activation(v_hi[:, :], kvs[:, h % 2, 0:DV], ACT.Copy).then_inc(v_hi_ok, 1)
                act.wait_ge(kw_ok, 2 * h + 2)
                key_hi(h, 0)
                for c in range(CH):
                    n = LEAD + c
                    split(S_O + h, n) if n < CH else split(S_O + h + 1, n - CH)
                    if c == 0:
                        act.wait_ge(filled, FILL["updp", h, 0])
                        if h:
                            act.wait_ge(c_out[0], 16 * c_stores(h - 1, 5))
                        act.activation(cst[:, 0, 1, :], X[1][:, :], ACT.Copy).then_inc(drained_a, 1)
                    if c + 1 < NSEQ:
                        key_hi(h, c + 1)
                    if h + 1 < HEADS and 1 <= c <= TT + 1:
                        prep(h + 1, c - 1)
                    if h and c == 4:
                        root2(h - 1)
                    if h == HEADS - 1 and c >= 6:
                        act.wait_ge(hss_ok, h)
                        act.wait_ge(att_ok, h)
                        for k in range(4 * (c - 6), 4 * (c - 5)):
                            att_hi(k)
                act.wait_ge(x2_filled, h + 1)
                if h + 1 < HEADS:
                    act.wait_ge(drained, FILL["score", h + 1, 0])
                act.activation(hs[0:NS, :], X[2][0:NS, :], ACT.Copy).then_inc(hs_kept, 1)
                act.wait_ge(evicted, tiles_out(S_O + h, MT - 1))
                z4 = qkv[:, z_block(h):z_block(h) + 4, :]
                act.activation(z4, z4, ACT.Sigmoid).then_inc(ez_ok, 1)

            def third_head_hi():
                act.wait_ge(hss_ok, HEADS)
                for k in range(8, 12):
                    att_hi(k)

            def last_head_hi():
                for k in range(12, KT):
                    att_hi(k)

            slab(S_OUT, norm_op(S_OUT, 2, V_FFN + KT),
                 {2: third_head_hi, 3: lambda: root2(HEADS - 1), 4: last_head_hi})
            for j in range(1, MT):
                s = S_OUT + j
                slab(s, norm_op(s, 2, V_FFN + KT))
            ffn(1, S_FFN1, 3)
            def keep(j):
                act.wait_ge(y_turned, j + 1)
                act.activation(yrow[:, 0, j * NC:(j + 1) * NC], X[0][:, :], ACT.Copy).then_inc(y_kept_a, 1)
                act.activation(yrow[0:NS, 2, j * NC:(j + 1) * NC], X[2][0:NS, :], ACT.Copy).then_inc(y_kept_a, 1)

            def end_square(m):
                act.wait_ge(evicted, tiles_out(S_END - 1, m))
                act.activation(relu[:, m, :], hT[:, KT - MT + m, :], ACT.Square).then_inc(sq_end, 1)

            act.wait_ge(a_lo_ok, 2 * SLICES * KT)
            for j in range(MT):
                slab(S_END - MT + j, end_square if j == MT - 1 else None, {2: lambda: keep(j - 1)} if j else None,
                     last=j == MT - 1)
            keep(MT - 1)
            root(4, rcol[:, 0:TT], rcol[:, 0:TT])
            act.wait_ge(r_ok, 4)
            act.wait_ge(y_kept_a, 2 * MT)
            act.wait_ge(y_kept_d, MT)
            for t, half in ACT_HALVES:
                y = yrow[0:ROWS[t], t, half * D // 2:(half + 1) * D // 2]
                act.activation(y, y, ACT.Copy, scale=rcol[0:ROWS[t], t:t + 1]).then_inc(y_done_a, 1)

        @block.vector
        def _(v):
            n_chain = [0]

            def link(ins):
                n_chain[0] += 1
                ins.then_inc(dve, 1)
                v.wait_ge(dve, n_chain[0])

            def lo_of(slot):
                v.tensor_tensor(w_lo[:, slot], w_raw[:, slot], w_hi[:, slot].bitcast(F32), ALU.subtract).then_inc(w_lo_ok, 1)

            def split(s, c):
                v.wait_ge(w_hi_ok, chunk_no(s, c) + 1)
                lo_of(c % RING)

            def split_pool(n):
                v.wait_ge(w_hi_ok, n + 1)
                lo_of(n % RING)

            def slab(s, evict, mid=None, last=False):
                for i in range(CH):
                    c = LEAD + i
                    if c < CH:
                        split(s, c)
                    elif not last:
                        split(s + 1, c - CH)
                    if mid and i in mid:
                        mid[i]()
                for m in range(MT):
                    v.wait_ge(gemm, tile_done(s, m))
                    evict(m)

            def inverse(j, dst, src, n):
                v.tensor_scalar(dst, src, 1.0 / n, EPS, ALU.mult, ALU.add).then_inc(r_inv, 1)
                v.wait_ge(r_inv, 2 * j - 1)
                v.reciprocal(dst, dst).then_inc(r_inv, 1)

            def tile_inverse(t):
                for q in range(2, GROUPS):
                    v.wait_ge(x_turned, GROUPS * t + q + 1)
                    v.tensor_copy(hT[:, MT * q:MT * q + MT, tok(t)],
                                  G[:, q, 0:MT * ROWS[t]].rearrange("p (a r) -> p a r", r=ROWS[t])).then_inc(x_kept_d, 1)
                v.wait_ge(x_sq, t + 1)
                r = rcol[0:ROWS[t], t:t + 1]
                v.tensor_scalar(r, xcol[0:ROWS[t], t:t + 1], 1.0 / D, EPS, ALU.mult, ALU.add).then_inc(r0_inv, 1)
                v.wait_ge(r0_inv, 2 * t + 1)
                v.reciprocal(r, r).then_inc(r0_inv, 1)

            def less_token(g):
                v.wait_ge(band_drawn, g + 1)
                for at, n in ((B0, P), (B1, P), (BS, NS)):
                    ins = v.tensor_tensor(band[:, g, at:at + n], band[:, g, at:at + n], ident[:, 0:n], ALU.subtract)
                ins.then_inc(band_ok, 1)

            def normalised(g):
                cols_g = slice(g * NC, (g + 1) * NC)
                v.wait_ge(gain_in[1 if g else 0], 16)
                for t in range(TT):
                    rows = slice(0, ROWS[t])
                    if g == 0:
                        tile_inverse(t)
                        v.wait_ge(r0_ok, t + 1)
                    v.scalar_tensor_tensor(out=u[rows, t, cols_g], in0=xrow[rows, t, cols_g], scalar=rcol[rows, t:t + 1],
                                           in1=gain[rows, cols_g], op0=ALU.mult, op1=ALU.mult).then_inc(u_ok, 1)
                if g:
                    less_token(g)

            def d_lo(g):
                for i in range(MT):
                    k = MT * g + i
                    v.wait_ge(d_hi_ok, k + 1)
                    v.tensor_tensor(a_lo[:, k, :], X[i][:, 0:T], a_hi[:, k, :].bitcast(F32), ALU.subtract).then_inc(d_lo_ok, 1)

            def op_split(j, k, col):
                v.wait_ge(op_hi_ok, KT * j + k + 1)
                v.scalar_tensor_tensor(out=op_lo[:, k, :], in0=hT[:, k, :], scalar=vec(col + k),
                                       in1=op_hi[:, k, :].bitcast(F32), op0=ALU.mult, op1=ALU.subtract).then_inc(op_lo_ok, 1)

            v.wait_ge(consts, 1)
            less_token(0)
            normalised(0)
            v.wait_ge(vec_turned, 1)
            v.tensor_copy(vecs[:, :], X[3][:, T:T + V_ALL]).then_inc(vecs_ok, 1)
            normalised(1)
            split_pool(0)
            d_lo(0)
            normalised(2)
            split_pool(1)
            split_pool(2)
            d_lo(1)
            normalised(3)
            for g in range(GROUPS):
                for n in (2 * g + LEAD, 2 * g + LEAD + 1):
                    split_pool(n) if n < 8 else split(0, n - 8)
                for m in range(MT):
                    k = MT * g + m
                    v.wait_ge(gemm, pool_tile(g, m))
                    v.scalar_tensor_tensor(out=hT[:, k, :], in0=G[:, m, 0:T], scalar=vec(V_SCALE + k), in1=hT[:, k, :],
                                           op0=ALU.mult, op1=ALU.add).then_inc(evicted, 1)
                if g + 2 < GROUPS:
                    d_lo(g + 2)
                for k in range(MT * g, MT * g + MT):
                    op_split(0, k, V_FFN)
            v.wait_ge(pool_out, 16 * (2 + NSEQ))

            def hidden(s, first):
                def evict(m):
                    if not (isinstance(first, int) and first == 0):
                        v.wait_ge(a_lo_ok, first + m - 3)
                        v.wait_ge(a_hi_ok, first + m - 3)
                    v.scalar_tensor_tensor(out=relu[:, m], in0=G[:, m, 0:T], scalar=0.0, in1=Rb[:, :], op0=ALU.max,
                                           op1=ALU.mult).then_inc(evicted, 1)
                return evict

            def add(k0):
                def evict(m):
                    h = hT[:, bass.ds(k0 + m, 1), :]
                    v.tensor_tensor(h, G[:, m:m + 1, 0:T], h, ALU.add).then_inc(evicted, 1)
                return evict

            def add_norm(s, j, col):
                k0 = (s % 4) * MT

                def evict(m):
                    h = hT[:, k0 + m, :]
                    v.tensor_tensor(h, G[:, m, 0:T], h, ALU.add).then_inc(evicted, 1)
                    if m:
                        op_split(j, k0 + m - 1, col)
                    if m == MT - 1:
                        op_split(j, k0 + m, col)
                return evict

            def ffn(layer, s0, rj):
                f0 = KT * SLICES * layer

                def norm():
                    v.wait_ge(r_sum, rj)
                    inverse(rj, rv[:, :], X[3][:, 0:T], D)

                def ready():
                    v.wait_ge(r_ok, rj)

                slab(s0, hidden(s0, f0), {5: norm, 7: ready})
                with v.Fori(1, MT) as j:
                    slab(s0 + j, hidden(s0 + j, f0 + j * MT))
                with v.Fori(0, MT) as j:
                    slab(s0 + 4 + j, add(j * MT))
                with v.Fori(1, SLICES - 1) as sl:
                    with v.Fori(0, MT) as j:
                        slab(s0 + sl * 8 + j, hidden(s0 + sl * 8 + j, f0 + sl * KT + j * MT))
                    with v.Fori(0, MT) as j:
                        slab(s0 + 4 + sl * 8 + j, add(j * MT))
                sl = SLICES - 1
                with v.Fori(0, MT) as j:
                    slab(s0 + sl * 8 + j, hidden(s0 + sl * 8 + j, f0 + sl * KT + j * MT))

            ffn(0, S_FFN0, 1)
            for j in range(MT):
                s = S_QKV - MT + j
                slab(s, add_norm(s, 1, V_MIX + KT))

            def proj(pos):
                def evict(m):
                    v.tensor_tensor(qkv[:, bass.ds(pos(m), 1), :], G[:, m:m + 1, 0:T], bc(Rb[:, :], [P, 1, T]),
                                    ALU.mult).then_inc(evicted, 1)
                return evict

            q_pos = lambda j: lambda m: j * 8 + (4 * (m // 2) + m % 2)
            k_pos = lambda j: lambda m: j * 8 + (4 * (m // 2) + 2 + m % 2)

            def norm():
                v.wait_ge(r_sum, 2)
                inverse(2, rv[:, :], X[3][:, 0:T], D)

            def gate_rows():
                v.wait_ge(small_in, 32)
                v.tensor_scalar(bgate[:, :], bgate[:, :], 1.0 / CAP, None, ALU.mult).then_inc(gz_ok, 1)
                v.wait_ge(gates_sum, 1)
                v.wait_ge(r_ok, 2)
                v.tensor_tensor(gz[:, 0, :], X[0][GP:GP + HEADS, 0:T], Rb[GP:GP + HEADS, :], ALU.mult).then_inc(gz_ok, 1)
                v.tensor_tensor(gz[:, 1, :], X[0][64:64 + HEADS, 0:T], Rb[64:64 + HEADS, :], ALU.mult).then_inc(gz_ok, 1)

            slab(S_QKV, proj(q_pos(0)), {5: norm, 7: gate_rows})
            slab(S_QKV + 1, proj(q_pos(1)))
            with v.Fori(0, 2) as j:
                slab(S_QKV + 2 + j, proj(k_pos(j)))
            v.wait_ge(g_ok, 1)
            scan(v, link, ALU.max)
            v.tensor_scalar(mrow[:, 0:TP], scan_p[0][:, P:], 0.0, None, ALU.max).then_inc(m_ok, 1)
            v.tensor_tensor(seqs(mrow), scan_s[1][:, :, 4:], m0[:, :].unsqueeze(2).broadcast_to([HEADS, NSEQ, TS]),
                            ALU.max).then_inc(m_ok, 1)
            with v.Fori(0, 3) as j:
                slab(S_QKV + 4 + j, proj(lambda m: j * MT + (KT + m)))

            def token_gates():
                v.wait_ge(filled, FILL["cols", 0, 0])
                v.tensor_copy(cols[:, :, :], X[0][:, 0:24].rearrange("p (a h) -> p a h", h=HEADS))
                v.tensor_copy(dect[:, :], X[1][0:1 + NSEQ, 0:HEADS]).then_inc(drained, 1)
                v.wait_ge(drained, FILL["cols", 0, 0])

            def prep(h, i):
                p = h % 2
                if i < TT:
                    v.wait_ge(filled, FILL["turn", h, i])
                    dst = kvp[:, i, DV:] if i < 2 else kvs[:, p, DV:]
                    v.tensor_copy(dst, X[1][:, 0:DK]).then_inc(drained, 1)
                elif i == TT:
                    v.wait_ge(filled, FILL["rows", h, 0])
                    if h:
                        v.wait_ge(prep_ok, h)
                    negm = X[0]
                    v.scalar_tensor_tensor(out=eb[:, 0:P], in0=negm[:, 0:P], scalar=cols[:, 0, h:h + 1], in1=causal[:, :],
                                           op0=ALU.add, op1=ALU.add)
                    v.tensor_scalar(eb[:, P:TP], negm[:, P:TP], cols[:, 0, h:h + 1], None, ALU.add)
                    v.scalar_tensor_tensor(out=eb[:, TP:384], in0=negm[:, P:TP], scalar=cols[:, 2, h:h + 1],
                                           in1=causal[:, :], op0=ALU.add, op1=ALU.add)
                    v.scalar_tensor_tensor(out=eb[0:NS, 384:448], in0=negm[0:NS, TP:T], scalar=cols[0:NS, 4, h:h + 1],
                                           in1=causal_s[0:NS, :], op0=ALU.add, op1=ALU.add).then_inc(drained, 1)
                else:
                    v.wait_ge(filled, FILL["score", h, 0])
                    v.wait_ge(eb_exp, 2 * h + 2)
                    v.scalar_tensor_tensor(out=ST[:, 0:384], in0=X[0][:, 0:384], scalar=QSCALE, in1=eb[:, 0:384],
                                           op0=ALU.mult, op1=ALU.mult)
                    v.scalar_tensor_tensor(out=ST[0:NS, 384:448], in0=X[0][0:NS, 384:448], scalar=QSCALE,
                                           in1=eb[0:NS, 384:448], op0=ALU.mult, op1=ALU.mult)
                    v.tensor_copy(nts[:, :], X[1][:, 0:18]).then_inc(drained, 1)
                    v.wait_ge(drained_a, ACT_FILL["rows", h, 0])
                    for t in range(2):
                        ins = v.scalar_tensor_tensor(out=qw[:, t, :], in0=qkv[:, head_block(h) + t, TP:T], scalar=QSCALE,
                                                     in1=EW[:, p, T:T + NS], op0=ALU.mult, op1=ALU.mult)
                    link(ins)
                    v.wait_ge(drained, FILL["score", h, 0])
                    for t in range(2):
                        ins = v.tensor_tensor(qn[:, t, :].rearrange("p (b t) -> p b t", t=TS),
                                              qw[:, t, :].rearrange("p (b t) -> p b t", t=TS),
                                              nts[:, 9 * t + 1:9 * t + 9].unsqueeze(2).broadcast_to([P, NSEQ, TS]), ALU.mult)
                    ins.then_inc(prep_ok, 1)

            slab(S_QKV + 7, proj(lambda m: KT + 12 + m),
                 {0: token_gates, **{i + 1: (lambda i=i: prep(0, i)) for i in range(TT + 2)}})

            def mean_square(h):
                v.wait_ge(x3_filled, X3_USES[f"ms{h}"])
                v.tensor_scalar(r2b[:, :], X[3][:, 0:T], 1.0 / DV, EPS, ALU.mult, ALU.add).then_inc(x3_read, 1)
                v.wait_ge(x3_read, X3_USES[f"ms{h}"])
                v.reciprocal(r2b[:, :], r2b[:, :]).then_inc(r2_inv, 1)

            def gated(h):
                z4 = qkv[:, z_block(h):z_block(h) + 4, :]
                v.wait_ge(ez_ok, h + 1)
                v.wait_ge(r2_ok, h + 1)
                for i in range(4):
                    ins = v.scalar_tensor_tensor(out=att(h)[:, i], in0=att(h)[:, i], scalar=vec(V_HEAD + 4 * h + i),
                                                 in1=r2b[:, :], op0=ALU.mult, op1=ALU.mult)
                link(ins)
                v.tensor_tensor(att(h), att(h), z4, ALU.mult).then_inc(att_ok, 1)

            def a_lo_of(k):
                v.wait_ge(att_hi_ok, k + 1)
                v.tensor_tensor(a_lo[:, k, :], qkv[:, KT + k, :], a_hi[:, k, :].bitcast(F32), ALU.subtract).then_inc(att_lo_ok, 1)

            def samples_out(h):
                v.wait_ge(x2_turned, h + 1)
                v.tensor_tensor(att(h)[:, :, TP:T], X[2][:, 0:4 * NS].rearrange("p (a t) -> p a t", t=NS),
                                bc(rden[h % 2][:, TP:T], [P, 4, NS]), ALU.mult).then_inc(att_s, 1)

            def key_lo(h, b):
                v.wait_ge(kwb_hi_ok, NSEQ * h + b + 1)
                half = slice(NS, 2 * NS)
                v.scalar_tensor_tensor(out=kwb[half, b % 2, :], in0=kvs[half, h % 2, DV:],
                                       scalar=seqmask[half, 2, 1 + b:2 + b], in1=kwb[half, b % 2, :].bitcast(F32),
                                       op0=ALU.mult, op1=ALU.subtract).then_inc(kwb_ok, 1)

            for h in range(HEADS):
                p = h % 2
                rd = rden[p]
                v.wait_ge(x3_filled, X3_USES[f"den{h}"])
                v.wait_ge(drained_a, ACT_FILL["rows", h, 0])
                link(v.scalar_tensor_tensor(out=rd[:, :], in0=X[3][:, 0:T], scalar=-1.0, in1=EW[:, p, 0:T],
                                            op0=ALU.mult, op1=ALU.max))
                v.tensor_tensor(rd[:, :], X[3][:, 0:T], rd[:, :], ALU.max).then_inc(x3_read, 1)
                v.wait_ge(x3_read, X3_USES[f"den{h}"])
                link(v.reciprocal(rd[:, :], rd[:, :]))
                v.wait_ge(filled, FILL["num", h, 0])
                for i in range(2):
                    ins = v.tensor_tensor(att(h)[:, 2 * i:2 * i + 2, 0:TP], X[i][:, :].rearrange("p (a t) -> p a t", t=TP),
                                          bc(rd[:, 0:TP], [P, 2, TP]), ALU.mult)
                ins.then_inc(drained, 1)
                if h:
                    v.wait_ge(x2_filled, h)
                for t in range(2):
                    ins = v.tensor_copy(qwm[:, t, :].rearrange("p (b r) -> p b r", r=NS + TS)[:, :, 0:TS],
                                        qw[:, t, :].rearrange("p (b t) -> p b t", t=TS))
                ins.then_inc(qwm_ok, 1)
                v.wait_ge(v_hi_ok, h + 1)
                v.tensor_tensor(v_lo[:, :], kvs[:, p, 0:DV], v_hi[:, :].bitcast(F32), ALU.subtract).then_inc(v_lo_ok, 1)
                key_lo(h, 0)
                if h:
                    samples_out(h - 1)
                v.wait_ge(x3_filled, X3_USES[f"n{h}"])
                nh = nrow[:, h * DK:(h + 1) * DK]
                v.scalar_tensor_tensor(out=nh, in0=nh, scalar=dect[:, h:h + 1], in1=X[3][0:1 + NSEQ, 0:DK],
                                       op0=ALU.mult, op1=ALU.add).then_inc(x3_read, 1)
                for c in range(CH):
                    n = LEAD + c
                    split(S_O + h, n) if n < CH else split(S_O + h + 1, n - CH)
                    if c == 0:
                        v.wait_ge(filled, FILL["updp", h, 0])
                        if h:
                            v.wait_ge(c_out[0], 16 * c_stores(h - 1, 5))
                        v.tensor_copy(cst[:, 0, 0, :], X[0][:, :]).then_inc(drained, 1)
                    if c + 1 < NSEQ:
                        key_lo(h, c + 1)
                    if h + 1 < HEADS and 1 <= c <= TT + 2:
                        prep(h + 1, c - 1)
                    if h and c == 3:
                        mean_square(h - 1)
                    if h and c == 5:
                        gated(h - 1)
                    if h == HEADS - 1 and c >= 6:
                        for k in range(4 * (c - 6), 4 * (c - 5)):
                            a_lo_of(k)
                    if c == CH - 1:
                        for m in range(MT):
                            v.wait_ge(gemm, tile_done(S_O + h, m))
                            v.tensor_tensor(qkv[:, z_block(h) + m, :], G[:, m, 0:T], Rb[:, :], ALU.mult).then_inc(evicted, 1)
                    v.wait_ge(filled, FILL["upd", h, c])
                    for t in range(2):
                        st = cst[:, c_slot(c), t, :]
                        ins = v.scalar_tensor_tensor(out=st, in0=st, scalar=EW[:, p, T + NS + 1 + c:T + NS + 2 + c],
                                                     in1=X[t][:, :], op0=ALU.mult, op1=ALU.add)
                    ins.then_inc(drained, 1)
            samples_out(HEADS - 1)

            def third_head_lo():
                for k in range(8, 12):
                    a_lo_of(k)
                mean_square(HEADS - 1)

            def last_head_lo():
                for k in range(12, KT):
                    a_lo_of(k)

            for j in range(MT):
                s = S_OUT + j
                slab(s, add_norm(s, 2, V_FFN + KT),
                     {2: third_head_lo, 3: lambda: gated(HEADS - 1), 4: last_head_lo} if j == 0 else None)
            for i in range(3):
                v.wait_ge(c_out[i], 16 * 3 * HEADS)
            v.wait_ge(outs, 16 * 4)
            ffn(1, S_FFN1, 3)
            def keep(j):
                v.wait_ge(y_turned, j + 1)
                v.tensor_copy(yrow[:, 1, j * NC:(j + 1) * NC], X[1][:, :]).then_inc(y_kept_d, 1)

            for j in range(MT):
                def evict(m, j=j):
                    k = j * MT + m
                    h = hT[:, k, :]
                    v.tensor_tensor(h, G[:, m, 0:T], h, ALU.add).then_inc(evicted, 1)
                    v.wait_ge(evicted, tiles_out(S_END - MT + j, m))
                    v.tensor_scalar(yT[:, k, :], h, vec(V_FIN + k), None, ALU.mult).then_inc(y_ok, 1)
                slab(S_END - MT + j, evict, {2: lambda: keep(j - 1)} if j else None, last=j == MT - 1)
            v.wait_ge(r_sum, 4)
            v.tensor_scalar(rcol[:, 0:2], X[3][:, 0:2], 1.0 / D, EPS, ALU.mult, ALU.add)
            v.tensor_scalar(rcol[0:NS, 2:3], X[3][0:NS, 2:3], 1.0 / D, EPS, ALU.mult, ALU.add).then_inc(r_inv, 1)
            v.wait_ge(r_inv, 7)
            v.reciprocal(rcol[:, 0:TT], rcol[:, 0:TT]).then_inc(r_inv, 1)
            keep(MT - 1)
            v.wait_ge(r_ok, 4)
            v.wait_ge(y_kept_a, 2 * MT)
            v.wait_ge(y_kept_d, MT)
            for t, half in DVE_HALVES:
                y = yrow[0:ROWS[t], t, half * D // 2:(half + 1) * D // 2]
                v.tensor_scalar(y, y, rcol[0:ROWS[t], t:t + 1], None, ALU.mult).then_inc(y_done_d, 1)

        @block.tensor
        def _(pe):
            def turn(out, in_, rows=P):
                if in_.shape[-1] == P:
                    return pe.transpose(out, in_, ident[0:rows, 0:rows])
                return pe.matmul(out, in_, ident[0:rows, 0:rows], start=True, stop=True, skip_group_check=True)

            def chunk(slot, hi, lo, k0, first, last, tile=None, ready=None):
                for m in range(MT):
                    if tile:
                        tile(m)
                    for t in range(CK):
                        k = k0 + t
                        if ready and m == 0:
                            ready(k)
                        w = slice(m * P, (m + 1) * P)
                        pe.matmul(G[:, m, 0:T], w_hi[:, slot, t, w], hi[:, k, :], start=first and t == 0, stop=False)
                        pe.matmul(G[:, m, 0:T], w_hi[:, slot, t, w], lo[:, k, :], start=False, stop=False)
                        ins = pe.matmul(G[:, m, 0:T], w_lo[:, slot, t, w], hi[:, k, :], start=False,
                                        stop=last and t == CK - 1)
                    if last:
                        ins.then_inc(gemm, 1)
                if not last:
                    ins.then_inc(gemm, 1)

            def slab(s, hi, lo, ready=None, mid=None):
                for c in range(CH):
                    pe.wait_ge(w_lo_ok, chunk_no(s, c) + 1)
                    free = (lambda m: pe.wait_ge(evicted, s * MT + (MT * (GROUPS - 1) + m + 1))) if c == 0 else None
                    chunk(c % RING, hi, lo, CK * c, c == 0, c == CH - 1, free, ready)
                    if mid:
                        mid(c)

            def keep_warm(n):
                for _ in range(n):
                    pe.matmul(X[0][:, 0:P], ident[:, :], ident[:, :], start=True, stop=True)

            pe.wait_ge(consts, 1)
            keep_warm(9)
            for t in range(TT):
                pe.wait_ge(x_in[t], 16)
                for q in range(GROUPS):
                    if t:
                        kept = x_kept_a if q < 2 else x_kept_d
                        pe.wait_ge(kept, 2 * (t - 1) + q % 2 + 1)
                    for i in range(MT):
                        k = MT * q + i
                        ins = pe.transpose(G[:, q, i * ROWS[t]:(i + 1) * ROWS[t]], xrow[0:ROWS[t], t, k * P:(k + 1) * P],
                                           ident[0:ROWS[t], 0:ROWS[t]])
                    ins.then_inc(x_turned, 1)
                keep_warm(WARM[t])
            pe.wait_ge(vecs_in, 16 * 5)
            pe.transpose(X[3][:, T:T + V_ALL], vrow[0:V_ALL, :], ident[0:V_ALL, 0:V_ALL]).then_inc(vec_turned, 1)

            def differences(g):
                pe.wait_ge(u_ok, TT * (g + 1))
                pe.wait_ge(band_ok, g + 1)
                pe.wait_ge(state_in[1 if g else 0], 16)
                for i in range(MT):
                    f = slice((MT * g + i) * P, (MT * g + i + 1) * P)
                    if g:
                        pe.wait_ge(d_lo_ok, MT * (g - 1) + i + 1)
                    pe.matmul(X[i][:, 0:P + 16], u[:, 0, f], band[:, g, B0:B1], start=True, stop=False, skip_group_check=True)
                    pe.matmul(X[i][:, P:TP], u[:, 1, f], band[:, g, B1:BS], start=False, stop=False, skip_group_check=True)
                    pe.matmul(X[i][:, TP:T], u[0:NS, 2, f], band[0:NS, g, BS:BP], start=False, stop=False, skip_group_check=True)
                    pe.matmul(X[i][:, TP:T], srow[0:NSEQ * PAD, f], band[0:NSEQ * PAD, g, BP:B_ALL], start=False, stop=True,
                              skip_group_check=True).then_inc(d_ok, 1)

            pe.wait_ge(vecs_ok, 1)
            differences(0)
            for g in range(GROUPS):
                if g + 1 < GROUPS:
                    differences(g + 1)
                pe.wait_ge(d_lo_ok, MT * (g + 1))
                for c in range(2):
                    n = 2 * g + c
                    pe.wait_ge(w_lo_ok, n + 1)
                    if n == 0:
                        pe.wait_ge(x_kept_a, 2 * TT)
                        pe.wait_ge(x_kept_d, 2 * TT)
                    free = (lambda m: pe.wait_ge(evicted, MT * (g - 1) + m + 1)) if g and c == 0 else None
                    chunk(n % RING, a_hi, a_lo, 4 * g + CK * c, c == 0, c == 1, free)

            def norm_sum(j):
                pe.wait_ge(ssq_ok, KT * j + KT)
                pe.matmul(X[3][:, 0:T], ones[:, :], acc[:, :], start=True, stop=True).then_inc(r_sum, 1)

            def op_ready(j):
                return lambda k: pe.wait_ge(op_lo_ok, KT * j + k + 1)

            def down_ready(first):
                return lambda k: pe.wait_ge(a_lo_ok, first + (k + 1))

            def ffn(layer, s0, j_op):
                f0 = KT * SLICES * layer
                slab(s0, op_hi, op_lo, op_ready(j_op), lambda c: norm_sum(j_op) if c == 4 else None)
                with pe.Fori(1, MT) as j:
                    slab(s0 + j, op_hi, op_lo)
                with pe.Fori(0, MT) as j:
                    slab(s0 + 4 + j, a_hi, a_lo, down_ready(f0))
                with pe.Fori(1, SLICES - 1) as sl:
                    with pe.Fori(0, MT) as j:
                        slab(s0 + sl * 8 + j, op_hi, op_lo)
                    with pe.Fori(0, MT) as j:
                        slab(s0 + 4 + sl * 8 + j, a_hi, a_lo, down_ready(f0 + sl * KT))
                sl = SLICES - 1
                with pe.Fori(0, MT) as j:
                    slab(s0 + sl * 8 + j, op_hi, op_lo)

            ffn(0, S_FFN0, 0)
            with pe.Fori(0, MT) as j:
                slab(S_QKV - MT + j, a_hi, a_lo, down_ready(KT * (SLICES - 1)))

            pe.wait_ge(gw_lo_ok, 4)
            for k in range(KT):
                pe.wait_ge(op_lo_ok, KT + k + 1)
                for w, x in ((gw_hi, op_hi), (gw_hi, op_lo), (gw_lo, op_hi)):
                    ins = pe.matmul(X[0][0:68, 0:T], w[:, k, :], x[:, k, :], start=k == 0 and w is gw_hi and x is op_hi,
                                    stop=k == KT - 1 and w is gw_lo)
            ins.then_inc(gates_sum, 1)
            slab(S_QKV, op_hi, op_lo, None, lambda c: norm_sum(1) if c == 4 else None)
            with pe.Fori(1, 7) as j:
                slab(S_QKV + j, op_hi, op_lo)

            order = fill_list()

            def bank_free(f):
                n = order.index(f)
                if n:
                    pe.wait_ge(drained, n)
                    for e in reversed(order[:n]):
                        if e in ACT_FILL:
                            pe.wait_ge(drained_a, ACT_FILL[e])
                            break

            def token_gates():
                pe.wait_ge(gates_exp, 1)
                pe.wait_ge(gz_ok, 3)
                eye = ident[GP:GP + HEADS, GP:GP + HEADS]
                for t in range(TT):
                    for n, row in enumerate((grow[:, tok(t)], gates[:, R_WK + t * P:R_WK + t * P + ROWS[t]])):
                        at = 4 * (2 * t + n)
                        for r in range(0, P, ROWS[t]):
                            pe.matmul(X[0][r:r + ROWS[t], at:at + HEADS], row, eye, start=at == 0, stop=True,
                                      skip_group_check=True)
                pe.matmul(X[1][0:1 + NSEQ, 0:HEADS], gates[:, R_DEC:R_DEC + 1 + NSEQ], eye,
                          start=True, stop=True).then_inc(filled, 1)

            def prep(h, i):
                q = head_block(h)
                if i < TT:
                    bank_free(("turn", h, i))
                    pe.wait_ge(evicted, tiles_out(S_QKV + (7 if h else 4), MT - 1))
                    for r in range(0, P, ROWS[i]):
                        for n in range(4):
                            turn(X[0][r:r + ROWS[i], n * P:(n + 1) * P], qkv[:, KT + 4 * h + n, tok(i)])
                        for n in range(2):
                            ins = turn(X[1][r:r + ROWS[i], n * P:(n + 1) * P], qkv[:, q + 2 + n, tok(i)])
                elif i == TT:
                    bank_free(("rows", h, 0))
                    pe.matmul(X[0][:, 0:T], sel[:, h, :], gates[:, R_NEGM:R_E], start=True, stop=True)
                    ins = pe.matmul(X[1][:, 0:BC], sel[:, h, :], gates[:, R_E:R_WK], start=True, stop=True)
                else:
                    bank_free(("score", h, 0))
                    first = True
                    for rows, a, b, at in ((P, 0, TP, 0), (P, P, TP, TP), (NS, TP, T, 384)):
                        for t in range(2):
                            pe.matmul(X[0][0:rows, at:at + b - a], qkv[:, q + 2 + t, a:a + rows], qkv[:, q + t, a:b],
                                      start=first, stop=t == 1, skip_group_check=True)
                            first = False
                    pe.wait_ge(small_in, 16 * 4)
                    for t in range(2):
                        ins = pe.matmul(X[1][:, 9 * t:9 * t + 9], nrow[:, h * DK + t * P:h * DK + (t + 1) * P],
                                        ident[0:9, 0:9], start=t == 0, stop=True, skip_group_check=True)
                ins.then_inc(filled, 1)

            slab(S_QKV + 7, op_hi, op_lo, None, lambda c: token_gates() if c == 0 else prep(0, c - 1) if c <= TT + 2 else None)

            def head_norm_sum(h):
                use = X3_USES[f"ms{h}"]
                pe.wait_ge(hss_ok, h + 1)
                pe.wait_ge(x3_read, use - 1)
                pe.matmul(X[3][:, 0:T], ones[:, :], hss[:, :], start=True, stop=True).then_inc(x3_filled, 1)

            def samples_turned(h):
                pe.wait_ge(hs_kept, h + 1)
                for n in range(4):
                    ins = turn(X[2][:, n * NS:(n + 1) * NS], hs[0:NS, n * P:(n + 1) * P], NS)
                ins.then_inc(x2_turned, 1)

            for h in range(HEADS):
                p = h % 2
                pe.wait_ge(prep_ok, h + 1)
                if h:
                    pe.wait_ge(x3_read, X3_USES[f"den{h}"] - 1)
                pe.matmul(X[3][:, 0:TP], ones[:, :], ST[:, 0:TP], start=True, stop=False, skip_group_check=True)
                pe.matmul(X[3][:, P:TP], ones[:, :], ST[:, TP:384], start=False, stop=False, skip_group_check=True)
                pe.matmul(X[3][:, TP:T], ones[0:NS, :], ST[0:NS, 384:448], start=False, stop=False, skip_group_check=True)
                for t in range(2):
                    ins = pe.matmul(X[3][:, TP:T], ones[:, :], qn[:, t, :], start=False, stop=t == 1, skip_group_check=True)
                ins.then_inc(x3_filled, 1)
                bank_free(("num", h, 0))
                for n in range(4):
                    w = slice(n * P, (n + 1) * P)
                    at = (n % 2) * TP
                    pe.matmul(X[n // 2][:, at:at + TP], kvp[:, 0, w], ST[:, 0:TP], start=n % 2 == 0, stop=False,
                              skip_group_check=True)
                    ins = pe.matmul(X[n // 2][:, at + P:at + TP], kvp[:, 1, w], ST[:, TP:384], start=False, stop=True,
                                    skip_group_check=True)
                ins.then_inc(filled, 1)
                if h:
                    samples_turned(h - 1)
                pe.wait_ge(kw_ok, 2 * h + 2)
                pe.wait_ge(x3_read, X3_USES[f"n{h}"] - 1)
                for t in range(TT):
                    ins = pe.matmul(X[3][0:1 + NSEQ, 0:DK], seqmask[0:ROWS[t], t, :],
                                    kvp[:, t, DV:] if t < 2 else kvs[0:NS, p, DV:], start=t == 0, stop=t == TT - 1)
                ins.then_inc(x3_filled, 1)
                for c in range(CH):
                    s = S_O + h
                    pe.wait_ge(w_lo_ok, chunk_no(s, c) + 1)
                    free = (lambda m: pe.wait_ge(evicted, tiles_out(s - 1, m))) if c == 0 else None
                    chunk(c % RING, op_hi, op_lo, CK * c, c == 0, c == CH - 1, free)
                    if c == 0:
                        bank_free(("updp", h, 0))
                        for t in range(2):
                            for i in range(2):
                                ins = pe.matmul(X[t][:, :], kvp[:, i, DV + t * P:DV + (t + 1) * P], kvp[:, i, 0:DV],
                                                start=i == 0, stop=i == 1)
                        ins.then_inc(filled, 1)
                        if h:
                            pe.wait_ge(att_s, h)
                        pe.matmul(X[2][0:NS, :], ST[0:NS, 384:448], kvs[0:NS, p, 0:DV], start=True, stop=False)
                        pe.wait_ge(qwm_ok, h + 1)
                    if h and c == 2:
                        head_norm_sum(h - 1)
                    if h + 1 < HEADS and 1 <= c <= TT + 2:
                        prep(h + 1, c - 1)
                    pe.wait_ge(c_in[c_slot(c)], 16 * c_loads(h, c))
                    for t in range(2):
                        ins = pe.matmul(X[2][0:NS, :], qwm[:, t, c * NS:(c + 1) * NS], cst[:, c_slot(c), t, :],
                                        start=False, stop=c == CH - 1 and t == 1)
                    if c == CH - 1:
                        ins.then_inc(x2_filled, 1)
                    bank_free(("upd", h, c))
                    pe.wait_ge(v_lo_ok, h + 1)
                    pe.wait_ge(kwb_ok, NSEQ * h + c + 1)
                    for t in range(2):
                        for n, v2 in enumerate((v_hi, v_lo)):
                            ins = pe.matmul(X[t][:, :], kwb[:, c % 2, t * P:(t + 1) * P], v2[:, :], start=n == 0, stop=n == 1)
                    ins.then_inc(filled, 1)
            samples_turned(HEADS - 1)
            slab(S_OUT, a_hi, a_lo, lambda k: pe.wait_ge(att_lo_ok, k + 1),
                 lambda c: head_norm_sum(HEADS - 1) if c == 2 else None)
            with pe.Fori(1, MT) as j:
                slab(S_OUT + j, a_hi, a_lo)
            ffn(1, S_FFN1, 2)
            def y_back(j):
                pe.wait_ge(y_ok, (j + 1) * MT)
                if j:
                    pe.wait_ge(y_kept_a, 2 * j)
                    pe.wait_ge(y_kept_d, j)
                for t in range(TT):
                    for m in range(MT):
                        ins = turn(X[t][0:ROWS[t], m * P:(m + 1) * P], yT[:, j * MT + m, tok(t)])
                ins.then_inc(y_turned, 1)

            def token_sums(x, first, last):
                for t in range(TT):
                    ins = pe.matmul(X[3][0:ROWS[t], t:t + 1], x[:, tok(t)], ones[:, 0:1], start=first and t == 0, stop=last,
                                    skip_group_check=True)
                return ins

            for j in range(MT):
                slab(S_END - MT + j, a_hi, a_lo, down_ready(KT * (2 * SLICES - 1)),
                     (lambda c: y_back(j - 1) if c == 1 else None) if j else None)
            pe.wait_ge(ssq_ok, 4 * KT - MT)
            token_sums(acc, True, False)
            for m in range(MT):
                pe.wait_ge(sq_end, m + 1)
                ins = token_sums(relu[:, m], False, m == MT - 1)
            ins.then_inc(r_sum, 1)
            y_back(MT - 1)


_INS = ["x_prompt", "x_sample", "state_pool", "state_mlstm_C", "state_mlstm_n", "state_mlstm_m", "norm_mix",
        "norm_ffn", "norm_final", "pool_w", "pool_scale", "mlstm_w_in", "mlstm_b_gate", "mlstm_head_norm",
        "mlstm_w_out", "ffn_w_up", "ffn_w_down"]
_OUTS = [("y_prompt", (1, TP, D)), ("y_sample", (NSEQ, TS, D)), ("pool_prompt", (1, 1, PAD, D)),
         ("pool_sample", (1, NSEQ, PAD, D)), ("C_prompt", (1, 1, HEADS, DK, DV)), ("n_prompt", (1, 1, HEADS, DK)),
         ("m_prompt", (1, 1, HEADS)), ("C_sample", (1, NSEQ, HEADS, DK, DV)), ("n_sample", (1, NSEQ, HEADS, DK)),
         ("m_sample", (1, NSEQ, HEADS))]


def kernel(**inputs):
    import concourse.bacc as bacc
    from concourse.bass_utils import run_bass_kernel_spmd

    nc = bacc.Bacc("TRN2", target_bir_lowering=False, num_devices=1)
    arrays, ins, outs = {}, {}, {}
    for name in _INS:
        a = np.ascontiguousarray(inputs[name])
        arrays[f"in_{name}"] = a
        ins[name] = nc.dram_tensor(f"in_{name}", a.shape, F32, kind="ExternalInput").ap()
    for name, shape in _OUTS:
        outs[name] = nc.dram_tensor(f"out_{name}", shape, F32, kind="ExternalOutput").ap()
    build(nc, ins, outs)
    r = run_bass_kernel_spmd(nc, [arrays], core_ids=[0])
    return tuple(r.results[0][f"out_{name}"] for name, _ in _OUTS)
```
